# Optimizing a Trainium2 kernel written in Bass

```python
import jax, jax.numpy as jnp
from jax import lax
import numpy as np

D_MODEL = 1024
BATCH = 1
SEQ = 1024
DEPTH = 1

D_MIX = D_MODEL
ROPE_THETA = 500000.0
Q_BLOCK = 128
NSA_HEADS = 8
NSA_KV_GROUPS = 2
NSA_HPG = NSA_HEADS // NSA_KV_GROUPS
NSA_HEAD_DIM = 64
NSA_ROPE_DIM = NSA_HEAD_DIM // 4
CMP_BLOCK = 32
CMP_STRIDE = 16
CMP_HIDDEN = 4 * NSA_HEAD_DIM
SLC_BLOCK = 64
SLC_TOPK = 16
WINDOW = 512
FORCE_SCORE = 1e9
MLA_HEADS = 8
MLA_NOPE_DIM = 64
MLA_ROPE_DIM = 32
MLA_V_DIM = 64
MLA_Q_RANK = 384
MLA_KV_RANK = 256
D_FF = 2816
ALPHA = (2.0 * DEPTH) ** 0.25
BETA = (8.0 * DEPTH) ** -0.25
N_MOD = 9
EPS = 1e-5

NSA_Q = NSA_HEADS * NSA_HEAD_DIM
NSA_KV = NSA_KV_GROUPS * NSA_HEAD_DIM
NSA_GATE = 3 * NSA_HEADS
IN_SIZES = [NSA_Q] + [NSA_KV] * 6 + [NSA_GATE, MLA_Q_RANK, MLA_KV_RANK, MLA_ROPE_DIM]
D_IN = sum(IN_SIZES)

kernel_name = "hymba_nsa_mla_macaron_deepnorm_adaln"

def layer_norm(x, g, b):
    xf = x.astype(jnp.float32)
    mu = jnp.mean(xf, -1, keepdims=True)
    var = jnp.mean(jnp.square(xf - mu), -1, keepdims=True)
    return ((xf - mu) * lax.rsqrt(var + EPS) * g + b).astype(x.dtype)

def rms_norm(x, g):
    xf = x.astype(jnp.float32)
    return (xf * lax.rsqrt(jnp.mean(xf * xf, -1, keepdims=True) + EPS) * g).astype(x.dtype)

def rope(x, pos, dim):
    half = dim // 2
    inv = ROPE_THETA ** (-jnp.arange(half, dtype=jnp.float32) / half)
    ang = pos.astype(jnp.float32)[:, None] * inv[None, :]
    cos = jnp.cos(ang).astype(x.dtype)
    sin = jnp.sin(ang).astype(x.dtype)
    x1, x2, rest = x[..., :half], x[..., half:dim], x[..., dim:]
    return jnp.concatenate([x1 * cos - x2 * sin, x2 * cos + x1 * sin, rest], axis=-1)

def masked_softmax(s, mask):
    s = jnp.where(mask, s.astype(jnp.float32), -jnp.inf)
    m = jnp.max(s, -1, keepdims=True)
    m = jnp.where(jnp.isfinite(m), m, 0.0)
    e = jnp.where(mask, jnp.exp(s - m), 0.0)
    return e / jnp.maximum(jnp.sum(e, -1, keepdims=True), 1e-30)

def swiglu(u, wg, wu, wd):
    return (jax.nn.silu(u @ wg) * (u @ wu)) @ wd

def compress(kv, pos_emb, w1, w2):
    T = kv.shape[2]
    n_cmp = (T - CMP_BLOCK) // CMP_STRIDE + 1
    idx = np.arange(n_cmp)[:, None] * CMP_STRIDE + np.arange(CMP_BLOCK)[None, :]
    blocks = kv[:, :, idx] + pos_emb
    flat = blocks.reshape(blocks.shape[:3] + (CMP_BLOCK * NSA_HEAD_DIM,))
    return jax.nn.gelu(flat @ w1) @ w2

def gather_blocks(blocks, idx):
    return jax.vmap(jax.vmap(lambda kb, ix: kb[ix]))(blocks, idx)

def nsa_mixer(q, kc, vc, ks, vs, kw, vw, gate_logits, pos,
              cmp_k_pos, cmp_k_w1, cmp_k_w2, cmp_v_pos, cmp_v_w1, cmp_v_w2):
    B, T, _ = q.shape
    nb = T // Q_BLOCK
    scale = NSA_HEAD_DIM ** -0.5
    q = q.reshape(B, T, NSA_KV_GROUPS, NSA_HPG, NSA_HEAD_DIM).transpose(0, 2, 3, 1, 4)
    q = rope(q, pos, NSA_ROPE_DIM)
    gates = jax.nn.sigmoid(gate_logits.reshape(B, T, NSA_KV_GROUPS, NSA_HPG, 3).transpose(0, 2, 3, 1, 4))

    def kv_heads(a):
        return a.reshape(B, T, NSA_KV_GROUPS, NSA_HEAD_DIM).transpose(0, 2, 1, 3)

    kc, vc, ks, vs, kw, vw = [kv_heads(a) for a in (kc, vc, ks, vs, kw, vw)]
    kc, ks, kw = rope(kc, pos, NSA_ROPE_DIM), rope(ks, pos, NSA_ROPE_DIM), rope(kw, pos, NSA_ROPE_DIM)

    k_cmp = compress(kc, cmp_k_pos, cmp_k_w1, cmp_k_w2)
    v_cmp = compress(vc, cmp_v_pos, cmp_v_w1, cmp_v_w2)
    n_cmp = k_cmp.shape[2]
    cmp_start = np.arange(n_cmp) * CMP_STRIDE
    cmp_end = jnp.asarray(cmp_start + CMP_BLOCK - 1)
    n_slc = T // SLC_BLOCK
    n_sel = min(SLC_TOPK, n_slc)
    slc_start = np.arange(n_slc) * SLC_BLOCK
    overlap = jnp.asarray(((cmp_start[:, None] < slc_start[None, :] + SLC_BLOCK) &
                           (cmp_start[:, None] + CMP_BLOCK > slc_start[None, :])).astype(np.float32))
    ks_blk = ks.reshape(B, NSA_KV_GROUPS, n_slc, SLC_BLOCK, NSA_HEAD_DIM)
    vs_blk = vs.reshape(B, NSA_KV_GROUPS, n_slc, SLC_BLOCK, NSA_HEAD_DIM)
    pad = ((0, 0), (0, 0), (WINDOW, 0), (0, 0))
    kw_pad, vw_pad = jnp.pad(kw, pad), jnp.pad(vw, pad)
    jj = jnp.arange(n_slc)

    def block(args):
        i, qb, gb = args
        t = i * Q_BLOCK + jnp.arange(Q_BLOCK)
        s = jnp.einsum('bghqd,bgnd->bghqn', qb, k_cmp) * scale
        p_cmp = masked_softmax(s, cmp_end[None, :] <= t[:, None])
        o_cmp = jnp.einsum('bghqn,bgnd->bghqd', p_cmp.astype(v_cmp.dtype), v_cmp)
        imp = jnp.einsum('bghqn,nj->bgqj', p_cmp, overlap)
        cur = t // SLC_BLOCK
        causal_blk = (jj[None, :] * SLC_BLOCK) <= t[:, None]
        forced = (jj[None, :] == 0) | (jj[None, :] == cur[:, None]) | (jj[None, :] == cur[:, None] - 1)
        imp = jnp.where(forced & causal_blk, FORCE_SCORE, jnp.where(causal_blk, imp, -1.0))
        _, sel = lax.top_k(imp, n_sel)
        k_sel = gather_blocks(ks_blk, sel).reshape(B, NSA_KV_GROUPS, Q_BLOCK, n_sel * SLC_BLOCK, NSA_HEAD_DIM)
        v_sel = gather_blocks(vs_blk, sel).reshape(B, NSA_KV_GROUPS, Q_BLOCK, n_sel * SLC_BLOCK, NSA_HEAD_DIM)
        sel_pos = (sel[..., None] * SLC_BLOCK + jnp.arange(SLC_BLOCK)).reshape(B, NSA_KV_GROUPS, Q_BLOCK, n_sel * SLC_BLOCK)
        m_sel = (sel_pos <= t[None, None, :, None])[:, :, None]
        s = jnp.einsum('bghqd,bgqkd->bghqk', qb, k_sel) * scale
        p_sel = masked_softmax(s, m_sel)
        o_sel = jnp.einsum('bghqk,bgqkd->bghqd', p_sel.astype(v_sel.dtype), v_sel)
        kwb = lax.dynamic_slice_in_dim(kw_pad, i * Q_BLOCK, WINDOW + Q_BLOCK, axis=2)
        vwb = lax.dynamic_slice_in_dim(vw_pad, i * Q_BLOCK, WINDOW + Q_BLOCK, axis=2)
        s_pos = i * Q_BLOCK - WINDOW + jnp.arange(WINDOW + Q_BLOCK)
        diff = t[:, None] - s_pos[None, :]
        m_win = (s_pos[None, :] >= 0) & (diff >= 0) & (diff < WINDOW)
        s = jnp.einsum('bghqd,bgkd->bghqk', qb, kwb) * scale
        p_win = masked_softmax(s, m_win)
        o_win = jnp.einsum('bghqk,bgkd->bghqd', p_win.astype(vwb.dtype), vwb)
        gb = gb.astype(qb.dtype)
        return gb[..., 0:1] * o_cmp + gb[..., 1:2] * o_sel + gb[..., 2:3] * o_win

    qbs = jnp.moveaxis(q.reshape(B, NSA_KV_GROUPS, NSA_HPG, nb, Q_BLOCK, NSA_HEAD_DIM), 3, 0)
    gbs = jnp.moveaxis(gates.reshape(B, NSA_KV_GROUPS, NSA_HPG, nb, Q_BLOCK, 3), 3, 0)
    out = lax.map(block, (jnp.arange(nb), qbs, gbs))
    out = jnp.moveaxis(out, 0, 3).reshape(B, NSA_KV_GROUPS, NSA_HPG, T, NSA_HEAD_DIM)
    return out.transpose(0, 3, 1, 2, 4).reshape(B, T, NSA_HEADS * NSA_HEAD_DIM)

def mla_mixer(cq, ckv, k_rope, pos, q_norm_g, kv_norm_g, w_uq, w_ukv):
    B, T, _ = cq.shape
    nb = T // Q_BLOCK
    scale = (MLA_NOPE_DIM + MLA_ROPE_DIM) ** -0.5
    q = (rms_norm(cq, q_norm_g) @ w_uq).reshape(B, T, MLA_HEADS, MLA_NOPE_DIM + MLA_ROPE_DIM).transpose(0, 2, 1, 3)
    q_nope, q_rope = q[..., :MLA_NOPE_DIM], rope(q[..., MLA_NOPE_DIM:], pos, MLA_ROPE_DIM)
    kv = (rms_norm(ckv, kv_norm_g) @ w_ukv).reshape(B, T, MLA_HEADS, MLA_NOPE_DIM + MLA_V_DIM).transpose(0, 2, 1, 3)
    k_nope, v = kv[..., :MLA_NOPE_DIM], kv[..., MLA_NOPE_DIM:]
    k_rope = rope(k_rope, pos, MLA_ROPE_DIM)
    key_pos = jnp.arange(T)

    def block(args):
        i, qn, qr = args
        t = i * Q_BLOCK + jnp.arange(Q_BLOCK)
        s = (jnp.einsum('bhqd,bhkd->bhqk', qn, k_nope) + jnp.einsum('bhqd,bkd->bhqk', qr, k_rope)) * scale
        p = masked_softmax(s, key_pos[None, :] <= t[:, None])
        return jnp.einsum('bhqk,bhkd->bhqd', p.astype(v.dtype), v)

    qn_b = jnp.moveaxis(q_nope.reshape(B, MLA_HEADS, nb, Q_BLOCK, MLA_NOPE_DIM), 2, 0)
    qr_b = jnp.moveaxis(q_rope.reshape(B, MLA_HEADS, nb, Q_BLOCK, MLA_ROPE_DIM), 2, 0)
    out = lax.map(block, (jnp.arange(nb), qn_b, qr_b))
    out = jnp.moveaxis(out, 0, 2).reshape(B, MLA_HEADS, T, MLA_V_DIM)
    return out.transpose(0, 2, 1, 3).reshape(B, T, MLA_HEADS * MLA_V_DIM)

def setup_inputs(seed: int = 0) -> dict:
    key = jax.random.key(seed)
    ks = jax.random.split(key, 24)
    n = lambda k, shape, s: jax.random.normal(k, shape, jnp.float32) * s
    L = DEPTH
    return {
        "x": n(ks[0], (BATCH, SEQ, D_MODEL), 1.0),
        "c": n(ks[1], (BATCH, D_MODEL), 1.0),
        "w_ada": n(ks[2], (L, D_MODEL, N_MOD * D_MODEL), 0.25 * D_MODEL ** -0.5),
        "b_ada": n(ks[3], (L, N_MOD * D_MODEL), 0.01),
        "ln_g": 1.0 + n(ks[4], (L, 3, D_MODEL), 0.02),
        "ln_b": n(ks[5], (L, 3, D_MODEL), 0.02),
        "ffn1_wg": n(ks[6], (L, D_MODEL, D_FF), D_MODEL ** -0.5),
        "ffn1_wu": n(ks[7], (L, D_MODEL, D_FF), D_MODEL ** -0.5),
        "ffn1_wd": n(ks[8], (L, D_FF, D_MODEL), BETA * D_FF ** -0.5),
        "w_in": n(ks[9], (L, D_MODEL, D_IN), D_MODEL ** -0.5),
        "cmp_k_pos": n(ks[10], (L, CMP_BLOCK, NSA_HEAD_DIM), 0.02),
        "cmp_k_w1": n(ks[11], (L, CMP_BLOCK * NSA_HEAD_DIM, CMP_HIDDEN), (CMP_BLOCK * NSA_HEAD_DIM) ** -0.5),
        "cmp_k_w2": n(ks[12], (L, CMP_HIDDEN, NSA_HEAD_DIM), CMP_HIDDEN ** -0.5),
        "cmp_v_pos": n(ks[13], (L, CMP_BLOCK, NSA_HEAD_DIM), 0.02),
        "cmp_v_w1": n(ks[14], (L, CMP_BLOCK * NSA_HEAD_DIM, CMP_HIDDEN), (CMP_BLOCK * NSA_HEAD_DIM) ** -0.5),
        "cmp_v_w2": n(ks[15], (L, CMP_HIDDEN, NSA_HEAD_DIM), CMP_HIDDEN ** -0.5),
        "mla_q_norm": 1.0 + n(ks[16], (L, MLA_Q_RANK), 0.02),
        "mla_kv_norm": 1.0 + n(ks[17], (L, MLA_KV_RANK), 0.02),
        "mla_w_uq": n(ks[18], (L, MLA_Q_RANK, MLA_HEADS * (MLA_NOPE_DIM + MLA_ROPE_DIM)), MLA_Q_RANK ** -0.5),
        "mla_w_ukv": n(ks[19], (L, MLA_KV_RANK, MLA_HEADS * (MLA_NOPE_DIM + MLA_V_DIM)), MLA_KV_RANK ** -0.5),
        "w_out": n(ks[20], (L, D_MIX, D_MODEL), BETA * D_MIX ** -0.5),
        "ffn2_wg": n(ks[21], (L, D_MODEL, D_FF), D_MODEL ** -0.5),
        "ffn2_wu": n(ks[22], (L, D_MODEL, D_FF), D_MODEL ** -0.5),
        "ffn2_wd": n(ks[23], (L, D_FF, D_MODEL), BETA * D_FF ** -0.5),
    }

def reference(x, c, w_ada, b_ada, ln_g, ln_b, ffn1_wg, ffn1_wu, ffn1_wd, w_in,
              cmp_k_pos, cmp_k_w1, cmp_k_w2, cmp_v_pos, cmp_v_w1, cmp_v_w2,
              mla_q_norm, mla_kv_norm, mla_w_uq, mla_w_ukv, w_out,
              ffn2_wg, ffn2_wu, ffn2_wd):
    T = x.shape[1]
    pos = jnp.arange(T)
    split_at = [int(v) for v in np.cumsum(IN_SIZES)[:-1]]
    for l in range(DEPTH):
        mod = jax.nn.silu(c) @ w_ada[l] + b_ada[l]
        sh1, sc1, g1, sh2, sc2, g2, sh3, sc3, g3 = jnp.split(mod[:, None, :], N_MOD, axis=-1)
        u = x * (1.0 + sc1) + sh1
        x = layer_norm(ALPHA * x + 0.5 * (1.0 + g1) * swiglu(u, ffn1_wg[l], ffn1_wu[l], ffn1_wd[l]), ln_g[l, 0], ln_b[l, 0])
        u = x * (1.0 + sc2) + sh2
        h = u @ w_in[l]
        q_a, kc, vc, ksl, vsl, kwn, vwn, gate_logits, cq, ckv, k_rope = jnp.split(h, split_at, axis=-1)
        o_nsa = nsa_mixer(q_a, kc, vc, ksl, vsl, kwn, vwn, gate_logits, pos,
                          cmp_k_pos[l], cmp_k_w1[l], cmp_k_w2[l], cmp_v_pos[l], cmp_v_w1[l], cmp_v_w2[l])
        o_mla = mla_mixer(cq, ckv, k_rope, pos, mla_q_norm[l], mla_kv_norm[l], mla_w_uq[l], mla_w_ukv[l])
        y = jnp.concatenate([o_nsa, o_mla], axis=-1) @ w_out[l]
        x = layer_norm(ALPHA * x + (1.0 + g2) * y, ln_g[l, 1], ln_b[l, 1])
        u = x * (1.0 + sc3) + sh3
        x = layer_norm(ALPHA * x + 0.5 * (1.0 + g3) * swiglu(u, ffn2_wg[l], ffn2_wu[l], ffn2_wd[l]), ln_g[l, 2], ln_b[l, 2])
    return x


_drawn_inputs = setup_inputs


def setup_inputs(seed=0):
    import zlib

    import numpy as np

    out = dict(_drawn_inputs(seed))
    spreads = {}
    factors = {'b_ada': 7.767,
     'cmp_k_pos': 50.813,
     'cmp_k_w1': 3.713,
     'cmp_k_w2': 3.694,
     'cmp_v_pos': 64.0,
     'mla_q_norm': 8.0,
     'mla_kv_norm': 8.0}
    for name, (base, spread) in spreads.items():
        noise = np.random.default_rng([zlib.crc32(name.encode()), seed]).standard_normal(out[name].shape)
        drawn = base * np.exp(spread * noise) if base else spread * noise
        out[name] = __import__('jax').numpy.asarray(drawn.astype(out[name].dtype))
    for name, factor in factors.items():
        out[name] = (out[name] * factor).astype(out[name].dtype)
    return out
```

```python
from contextlib import ExitStack

import concourse.bass as bass
from concourse import mybir

F32 = mybir.dt.float32
F32R = mybir.dt.float32r
ALU = mybir.AluOpType
ACT = mybir.ActivationFunctionType
AX = mybir.AxisListType.X

P = 128
HALF = 512
T = 1024
D = 1024
TT = T // P
DC = D // P
D_FF = 2816
FC = D_FF // P
N_MOD = 9
ALPHA = 2.0 ** 0.25
EPS = 1e-5

HD = 64
HEADS = 8
GROUPS = 2
HPG = HEADS // GROUPS
COL_Q = 0
COL_KC, COL_VC, COL_KS, COL_VS, COL_KW, COL_VW = (HEADS * HD + n * GROUPS * HD for n in range(6))
COL_GATE = COL_VW + GROUPS * HD
N_GATE = 3 * HEADS
Q_RANK = 384
KV_RANK = 256
COL_CQ = COL_GATE + N_GATE
COL_CKV = COL_CQ + Q_RANK
COL_KR = COL_CKV + KV_RANK
ROPE_N = 16
ROPE_M = 32
D_IN = COL_KR + ROPE_M
MD = HD + ROPE_M
COL_QM = HEADS * HD
NSA_SCALE = HD ** -0.5
MLA_SCALE = MD ** -0.5
ROPE_THETA = 500000.0

N_CMP = 63
CMP_PAD = 64
CMP_STRIDE = 16
CMP_BLOCK = 32
CMP_PAIRS = CMP_BLOCK // 2
CMP_HIDDEN = 4 * HD
WINDOW_BLOCKS = 4
MASKED = -1e30
NO_KEY = -1e20


class Scope:

    finished = []

    def __init__(self, nc, stage, side="left"):
        self.nc, self.stage, self.side, self.stack, self.sems = nc, stage, side, ExitStack(), []

    def __enter__(self):
        self.stack.__enter__()
        return self

    def __exit__(self, *a):
        Scope.finished += self.sems
        return self.stack.__exit__(*a)

    def sb(self, name, shape, dt=F32):
        return self.stack.enter_context(self.nc.sbuf_tensor(f"{self.stage}_{name}", shape, dt, side=self.side))

    def ps(self, name, shape):
        return self.stack.enter_context(self.nc.psum_tensor(f"{self.stage}_{name}", shape, F32))

    def sem(self, name):
        self.sems.append(self.nc.alloc_semaphore(f"{self.stage}_{name}"))
        return self.sems[-1]

    def block(self):
        return self.stack.enter_context(self.nc.Block())


def constants(nc, ident, ones):
    with Scope(nc, "const") as s:
        filled = s.sem("filled")
        block = s.block()

        @block.gpsimd
        def _(pool):
            pool.memset(ones[:, :], 1.0)
            pool.memset(ident[:, :], 0.0).then_inc(filled, 1)
            pool.wait_ge(filled, 1)
            pool.affine_select(out=ident[:, :], in_=ident[:, :], compare_op=ALU.not_equal, fill=1.0,
                               base=0, pattern=[[-1, P]], channel_multiplier=1)


def modulation(nc, c, w_ada, b_ada, x, ones, x_sb, shift, scale, gate_dram):
    with Scope(nc, "mod") as s:
        gate = s.sb("gate", [P, 3, D])
        gate_made, gate_out = s.sem("gate_made"), s.sem("gate_out")
        c_col = s.sb("c_col", [P, DC])
        silu_c = s.sb("silu_c", [P, DC])
        w = s.sb("w", [P, DC, D])
        part = s.sb("part", [P, N_MOD, D])
        cols = s.ps("cols", [P, 6, DC])
        rows = s.ps("rows", [P, 6, HALF])
        x_in, c_in, b_in, w_in = s.sem("x_in"), s.sem("c_in"), s.sem("b_in"), [s.sem(f"w_in{k}") for k in range(DC)]
        zeroed, silu_done, w_used = s.sem("zeroed"), s.sem("silu_done"), s.sem("w_used")
        summed, moved = s.sem("summed"), s.sem("moved")
        block = s.block()
        w_src = w_ada[0].rearrange("(p k) n -> p k n", k=DC)

        @block.sync
        def _(sp):
            sp.dma_start(c_col[:, :], c.rearrange("b (p k) -> (b p) k", k=DC)).then_inc(c_in, 16)
            sp.wait_ge(zeroed, 1)
            sp.dma_start(part[0:1, :, :], b_ada.rearrange("l (v n) -> l v n", n=D)).then_inc(b_in, 16)

            def load(v):
                for k in range(DC):
                    if not isinstance(v, int):
                        sp.wait_ge(w_used, (v - 1) * DC + k + 1)
                    sp.dma_start(w[:, k, :], w_src[:, k, bass.ts(v, D)]).then_inc(w_in[k], 16)

            load(0)
            with sp.Fori(1, N_MOD) as v:
                load(v)
            sp.dma_start(x_sb[:, :, :], x[0].rearrange("(i p) d -> p i d", p=P)).then_inc(x_in, 16)
            sp.wait_ge(x_in, 16)
            sp.wait_ge(gate_made, 3)
            sp.dma_start(gate_dram.unsqueeze(0), gate[0:1, :, :]).then_inc(gate_out, 16)
            sp.wait_ge(gate_out, 16)

        @block.gpsimd
        def _(pool):
            pool.memset(part[:, :, :], 0.0).then_inc(zeroed, 1)

        @block.scalar
        def _(act):
            act.wait_ge(c_in, 16)
            act.activation(silu_c[:, :], c_col[:, :], ACT.Silu).then_inc(silu_done, 1)
            act.wait_ge(summed, 1)
            for n in range(3):
                act.activation(shift[:, n, :], cols[:, 2 * n, :], ACT.Identity)
                act.activation(scale[:, n, :], cols[:, 2 * n + 1, :], ACT.Identity, bias=ones[:, 0:1])
            half_one = (0.5, 1.0, 0.5)
            for n in range(3):
                f = half_one[n]
                act.activation(gate[0:1, n, :], rows[0:1, 2 * n:2 * n + 2, :].rearrange("p a b -> p (a b)"),
                               ACT.Copy, scale=f, bias=f).then_inc(gate_made, 1)

        @block.vector
        def _(dve):
            dve.wait_ge(silu_done, 1)
            dve.wait_ge(b_in, 16)

            def weigh(v):
                for k in range(DC):
                    dve.wait_ge(w_in[k], v * 16 + 16)
                    if not isinstance(v, int) or k:
                        dve.wait_ge(w_used, v * DC + k)
                    acc = part[:, bass.ts(v, 1), :].rearrange("p a n -> p (a n)")
                    dve.scalar_tensor_tensor(out=acc, in0=w[:, k, :], scalar=silu_c[:, k:k + 1], in1=acc,
                                             op0=ALU.mult, op1=ALU.add).then_inc(w_used, 1)

            weigh(0)
            with dve.Fori(1, N_MOD) as v:
                weigh(v)

        @block.tensor
        def _(pe):
            pe.wait_ge(w_used, N_MOD * DC)
            for n in range(3):
                for q in range(2):
                    for cc in range(DC):
                        pe.matmul(cols[:, 2 * n + q, cc:cc + 1], part[:, 3 * n + q, cc * P:(cc + 1) * P],
                                  ones[:, 0:1], start=True, stop=True)
                for h in range(2):
                    last = pe.matmul(rows[0:1, 2 * n + h, :], ones[:, 0:1], part[:, 3 * n + 2, h * HALF:(h + 1) * HALF],
                                     start=True, stop=True)
            last.then_inc(summed, 1)


def modulated_transpose(nc, stage, x_sb, shift, scale, ident, u_hi, u_lo, spill=None):
    with Scope(nc, stage) as s:
        u = s.sb("u", [P, 2, HALF])
        tp = s.ps("tp", [P, 4, HALF])
        turned, placed, hi_done, lo_done = s.sem("turned"), s.sem("placed"), s.sem("hi_done"), s.sem("lo_done")
        block = s.block()
        units = [(c, h) for c in range(DC) for h in range(2)]
        grown = s.sem("grown")

        @block.sync
        def _(sp):
            if spill is not None:
                for i in range(TT):
                    sp.wait_ge(grown, i + 1)
                    sp.dma_start(spill[0][i * P:(i + 1) * P, :], x_sb[:, i, :]).then_inc(spill[1], 16)

        @block.tensor
        def _(pe):
            for n, (c, h) in enumerate(units):
                if n >= 4:
                    pe.wait_ge(placed, n - 3)
                for i in range(4):
                    t = pe.transpose(tp[:, n % 4, i * P:(i + 1) * P], x_sb[:, 4 * h + i, c * P:(c + 1) * P], ident[:, :])
                t.then_inc(turned, 1)

        @block.scalar
        def _(act):
            for n, (c, h) in enumerate(units):
                act.wait_ge(turned, n + 1)
                if n >= 2:
                    act.wait_ge(lo_done, n - 1)
                if scale is None:
                    made = act.activation(u[:, n % 2, :], tp[:, n % 4, :], ACT.Copy)
                else:
                    made = act.activation(u[:, n % 2, :], tp[:, n % 4, :], ACT.Identity, scale=scale[:, c:c + 1],
                                          bias=shift[:, c:c + 1])
                made.then_inc(placed, 1)
            if scale is not None:
                for i in range(TT):
                    act.mul(x_sb[:, i, :], x_sb[:, i, :], ALPHA).then_inc(grown, 1)

        @block.vector
        def _(dve):
            for n, (c, h) in enumerate(units):
                dve.wait_ge(placed, n + 1)
                hi = u_hi[:, c, h * HALF:(h + 1) * HALF]
                dve.tensor_copy(hi, u[:, n % 2, :]).then_inc(hi_done, 1)
                dve.wait_ge(hi_done, n + 1)
                dve.tensor_tensor(u_lo[:, c, h * HALF:(h + 1) * HALF], u[:, n % 2, :], hi.bitcast(F32),
                                  ALU.subtract).then_inc(lo_done, 1)


def swiglu(nc, stage, wg, wu, wd, gate_dram, x_sb, u_hi, u_lo):
    with Scope(nc, stage) as s:
        raw = {k: s.sb(f"w{k}_raw", [P, DC, P]) for k in "gud"}
        hi = {k: s.sb(f"w{k}_hi", [P, DC, P], F32R) for k in "gud"}
        lo = {k: s.sb(f"w{k}_lo", [P, DC, P], F32R) for k in "gud"}
        wd_gated = s.sb("wd_gated", [P, D])
        gate = s.sb("gate", [P, D])
        gate_in = s.sem("gate_in")
        silu_g = s.sb("silu_g", [P, T])
        h_f32 = s.sb("h_f32", [P, T])
        h_hi = s.sb("h_hi", [P, 2, T], F32R)
        h_lo = s.sb("h_lo", [P, 2, T], F32R)
        g_ps = s.ps("g_ps", [P, T])
        u_ps = s.ps("u_ps", [P, T])
        y_ps = s.ps("y_ps", [P, 2, D])
        landed = {k: s.sem(f"w{k}_landed") for k in "gud"}
        hi_ready = {k: s.sem(f"w{k}_hi_ready") for k in "gud"}
        split = {k: s.sem(f"w{k}_split") for k in "gud"}
        g_done, u_done, y_done = s.sem("g_done"), s.sem("u_done"), s.sem("y_done")
        silu_done, h_made, h_hi_ready, h_split = s.sem("silu_done"), s.sem("h_made"), s.sem("h_hi_ready"), s.sem("h_split")
        gated, y_added = s.sem("gated"), s.sem("y_added")
        block = s.block()
        flat = lambda a: a.rearrange("p c n -> p (c n)")
        src = {k: a[0].rearrange("(c p) n -> p c n", p=P) for k, a in (("g", wg), ("u", wu))}
        src["d"] = wd[0].rearrange("(f p) n -> f p n", p=P)

        def steps(eng, one, tail=None):
            one(0, 0)
            one(1, 1)
            with eng.Fori(2, FC - 2, 2) as f:
                one(f, 0)
                one(f + 1, 1)
            one(FC - 2, 0)
            one(FC - 1, 1)

        def after_first(f):
            return not isinstance(f, int) or f > 0

        def not_last(f):
            return not isinstance(f, int) or f < FC - 1

        @block.sync
        def _(sp):
            def load(f, parity):
                for k in "gud":
                    if after_first(f):
                        sp.wait_ge(gated if k == "d" else split[k], f)
                    if k == "d":
                        at = src["d"][bass.ts(f, 1)].rearrange("a p n -> p (a n)")
                        sp.dma_start(flat(raw["d"]), at).then_inc(landed["d"], 16)
                    else:
                        sp.dma_start(raw[k][:, :, :], src[k][:, :, bass.ts(f, P)]).then_inc(landed[k], 16)

            sp.dma_start(gate[:, :], gate_dram.to_broadcast([P, D])).then_inc(gate_in, 16)
            steps(sp, load)

        @block.scalar
        def _(act):
            def hi_of(k, f, source, done):
                if after_first(f):
                    act.wait_ge(done, f * (TT if k == "d" else 1))
                act.activation(flat(hi[k]), source, ACT.Copy).then_inc(hi_ready[k], 1)

            def hidden(f, parity):
                act.wait_ge(gated, f + 1)
                hi_of("d", f, wd_gated[:, :], y_done)
                act.wait_ge(h_made, f + 1)
                act.activation(h_hi[:, parity, :], h_f32[:, :], ACT.Copy).then_inc(h_hi_ready, 1)

            def step(f, parity):
                act.wait_ge(landed["u"], f * 16 + 16)
                hi_of("u", f, flat(raw["u"]), u_done)
                if after_first(f):
                    hidden(f - 1, 1 - parity)
                act.wait_ge(g_done, f + 1)
                if after_first(f):
                    act.wait_ge(h_made, f)
                act.activation(silu_g[:, :], g_ps[:, :], ACT.Silu).then_inc(silu_done, 1)
                if not_last(f):
                    act.wait_ge(landed["g"], f * 16 + 32)
                    hi_of("g", f + 1, flat(raw["g"]), g_done)

            act.wait_ge(landed["g"], 16)
            hi_of("g", 0, flat(raw["g"]), g_done)
            steps(act, step)
            hidden(FC - 1, (FC - 1) % 2)

        @block.vector
        def _(dve):
            def lo_of(k, f, source):
                dve.wait_ge(hi_ready[k], f + 1)
                dve.tensor_tensor(flat(lo[k]), source, flat(hi[k]).bitcast(F32), ALU.subtract).then_inc(split[k], 1)

            def hidden(f, parity):
                dve.wait_ge(landed["d"], f * 16 + 16)
                if after_first(f):
                    dve.wait_ge(split["d"], f)
                dve.tensor_tensor(wd_gated[:, :], flat(raw["d"]), gate[:, :], ALU.mult).then_inc(gated, 1)
                dve.wait_ge(u_done, f + 1)
                dve.wait_ge(silu_done, f + 1)
                if after_first(f):
                    dve.wait_ge(h_split, f)
                dve.tensor_tensor(h_f32[:, :], silu_g[:, :], u_ps[:, :], ALU.mult).then_inc(h_made, 1)
                lo_of("d", f, wd_gated[:, :])
                dve.wait_ge(h_hi_ready, f + 1)
                dve.tensor_tensor(h_lo[:, parity, :], h_f32[:, :], h_hi[:, parity, :].bitcast(F32),
                                  ALU.subtract).then_inc(h_split, 1)

            def add_down(f):
                for i in range(TT):
                    dve.wait_ge(y_done, f * TT + i + 1)
                    dve.tensor_tensor(x_sb[:, i, :], x_sb[:, i, :], y_ps[:, i % 2, :], ALU.add).then_inc(y_added, 1)

            def step(f, parity):
                lo_of("u", f, flat(raw["u"]))
                if after_first(f):
                    hidden(f - 1, 1 - parity)
                if not_last(f):
                    lo_of("g", f + 1, flat(raw["g"]))
                if after_first(f):
                    add_down(f - 1)

            dve.wait_ge(gate_in, 16)
            lo_of("g", 0, flat(raw["g"]))
            steps(dve, step)
            hidden(FC - 1, (FC - 1) % 2)
            add_down(FC - 1)

        @block.tensor
        def _(pe):
            def project(k, out, f, done):
                pe.wait_ge(split[k], f + 1)
                for c in range(DC):
                    for n, (w, u) in enumerate(((hi[k], u_hi), (hi[k], u_lo), (lo[k], u_hi))):
                        for h in range(2):
                            last = pe.matmul(out[:, h * HALF:(h + 1) * HALF], w[:, c, :], u[:, c, h * HALF:(h + 1) * HALF],
                                             start=(c == 0 and n == 0), stop=(c == DC - 1 and n == 2))
                last.then_inc(done, 1)

            def down(f, parity):
                pe.wait_ge(split["d"], f + 1)
                pe.wait_ge(h_split, f + 1)
                for i in range(TT):
                    if not (isinstance(f, int) and f == 0 and i < 2):
                        pe.wait_ge(y_added, f * TT + i - 1)
                    for n, (h, w) in enumerate(((h_hi, hi["d"]), (h_hi, lo["d"]), (h_lo, hi["d"]))):
                        for e in range(2):
                            last = pe.matmul(y_ps[:, i % 2, e * HALF:(e + 1) * HALF], h[:, parity, i * P:(i + 1) * P],
                                             flat(w)[:, e * HALF:(e + 1) * HALF], start=(n == 0), stop=(n == 2))
                    last.then_inc(y_done, 1)

            def step(f, parity):
                if after_first(f):
                    pe.wait_ge(silu_done, f)
                project("g", g_ps, f, g_done)
                if after_first(f):
                    pe.wait_ge(h_made, f)
                project("u", u_ps, f, u_done)
                if after_first(f):
                    down(f - 1, 1 - parity)

            steps(pe, step)
            down(FC - 1, (FC - 1) % 2)


def layer_norm(nc, stage, x_sb, g_dram, b_dram, out_dram=None):
    with Scope(nc, stage) as s:
        g_row = s.sb("g_row", [P, D])
        b_row = s.sb("b_row", [P, D])
        stats = s.sb("stats", [P, TT, 2, 6])
        mv = s.sb("mv", [P, TT, 2])
        std = s.sb("std", [P, TT])
        eps = s.sb("eps", [P, 1])
        rstd = s.sb("rstd", [P, TT])
        rows_in, eps_set, measured, rooted = s.sem("rows_in"), s.sem("eps_set"), s.sem("measured"), s.sem("rooted")
        step, scaled, shifted, stored = s.sem("step"), s.sem("scaled"), s.sem("shifted"), s.sem("stored")
        normed = s.sem("normed")
        block = s.block()

        @block.sync
        def _(sp):
            sp.dma_start(g_row[:, :], g_dram.to_broadcast([P, D])).then_inc(rows_in, 16)
            sp.dma_start(b_row[:, :], b_dram.to_broadcast([P, D])).then_inc(rows_in, 16)
            if out_dram is not None:
                for i in range(TT):
                    sp.wait_ge(shifted, i + 1)
                    sp.dma_start(out_dram[0, i * P:(i + 1) * P, :], x_sb[:, i, :]).then_inc(stored, 16)
                sp.wait_ge(stored, 16 * TT)

        @block.vector
        def _(dve):
            dve.memset(eps[:, :], EPS).then_inc(eps_set, 1)
            for i in range(TT):
                for h in range(2):
                    dve.bn_stats(stats[:, i, h, :], x_sb[:, i, h * HALF:(h + 1) * HALF]).then_inc(step, 1)
            for i in range(TT):
                dve.wait_ge(step, 2 * (i + 1))
                dve.bn_aggr(mv[:, i, :], stats[:, i, :, :].rearrange("p h s -> p (h s)")).then_inc(measured, 1)
            dve.wait_ge(rooted, 1)
            dve.reciprocal(rstd[:, :], std[:, :]).then_inc(step, 1)
            dve.wait_ge(step, 2 * TT + 1)
            for i in range(TT):
                dve.tensor_scalar(x_sb[:, i, :], x_sb[:, i, :], mv[:, i, 0:1], rstd[:, i:i + 1], ALU.subtract,
                                  ALU.mult).then_inc(normed, 1)
                if i == 0:
                    dve.wait_ge(rows_in, 32)
                dve.wait_ge(normed, i + 1)
                dve.tensor_tensor(x_sb[:, i, :], x_sb[:, i, :], g_row[:, :], ALU.mult).then_inc(scaled, 1)
                dve.wait_ge(scaled, i + 1)
                dve.tensor_tensor(x_sb[:, i, :], x_sb[:, i, :], b_row[:, :], ALU.add).then_inc(shifted, 1)

        @block.scalar
        def _(act):
            act.wait_ge(measured, TT)
            act.wait_ge(eps_set, 1)
            act.activation(std[:, :], mv[:, :, 1], ACT.Sqrt, bias=eps[:, 0:1]).then_inc(rooted, 1)


def project(nc, stage, w_dram, width, blocks, u_hi, u_lo, out, gate_dram=None):
    slots = 4
    with Scope(nc, stage) as s:
        raw = s.sb("w_raw", [P, slots, width])
        hi = s.sb("w_hi", [P, slots, width], F32R)
        lo = s.sb("w_lo", [P, slots, width], F32R)
        if gate_dram is not None:
            gate = s.sb("gate", [P, blocks * width])
        acc = s.ps("acc", [P, TT, HALF])
        landed = [s.sem(f"w_landed{k}") for k in range(slots)]
        gate_in, gated, hi_ready, split = s.sem("gate_in"), s.sem("gated"), s.sem("hi_ready"), s.sem("split")
        used, row_done, taken = s.sem("used"), s.sem("row_done"), s.sem("taken")
        block = s.block()
        src = w_dram.rearrange("(c p) n -> p c n", p=P)

        def wait_slot_used(eng, n, c):
            if c >= slots:
                eng.wait_ge(used, n * (DC - 1) + c - slots + 1)
            elif c == slots - 1:
                eng.wait_ge(row_done, n * TT)
            else:
                eng.wait_ge(used, (n - 1) * (DC - 1) + c + slots + 1)

        def steps(eng, one):
            one(0)
            with eng.Fori(1, blocks - 1) as n:
                one(n)
            one(blocks - 1)

        if blocks == 2:
            def steps(eng, one):
                one(0)
                one(1)

        later = lambda n, c: not isinstance(n, int) or n > 0 or c >= slots

        def per_block(split_chunk, take):
            def one(n):
                for c in range(slots, DC):
                    split_chunk(n, c)
                more = not isinstance(n, int) or n < blocks - 1
                if more:
                    for c in range(slots - 1):
                        split_chunk(n + 1, c)
                take(n)
                if more:
                    split_chunk(n + 1, slots - 1)
            return one

        @block.sync
        def _(sp):
            if gate_dram is not None:
                sp.dma_start(gate[:, :], gate_dram.to_broadcast([P, blocks * width])).then_inc(gate_in, 16)

            def load(n):
                for c in range(DC):
                    if later(n, c):
                        sp.wait_ge(split, n * DC + c - slots + 1)
                    at = src[:, c, bass.ds(n * width, width)]
                    sp.dma_start(raw[:, c % slots, :], at).then_inc(landed[c % slots], 16)

            steps(sp, load)

        @block.scalar
        def _(act):
            def make_hi(n, c):
                k = c % slots
                if gate_dram is None:
                    act.wait_ge(landed[k], (n * 2 + c // slots) * 16 + 16)
                else:
                    act.wait_ge(gated, n * DC + c + 1)
                if later(n, c):
                    wait_slot_used(act, n, c)
                act.activation(hi[:, k, :], raw[:, k, :], ACT.Copy).then_inc(hi_ready, 1)

            def take(n):
                if gate_dram is None:
                    for i in range(TT):
                        act.wait_ge(row_done, n * TT + i + 1)
                        act.activation(out[:, i, bass.ds(n * width, width)], acc[:, i, 0:width],
                                       ACT.Copy).then_inc(taken, 1)

            for c in range(slots):
                make_hi(0, c)
            steps(act, per_block(make_hi, take))

        @block.vector
        def _(dve):
            def make_lo(n, c):
                k = c % slots
                if gate_dram is not None:
                    dve.wait_ge(landed[k], (n * 2 + c // slots) * 16 + 16)
                    dve.tensor_tensor(raw[:, k, :], raw[:, k, :], gate[:, bass.ds(n * width, width)],
                                      ALU.mult).then_inc(gated, 1)
                dve.wait_ge(hi_ready, n * DC + c + 1)
                dve.tensor_tensor(lo[:, k, :], raw[:, k, :], hi[:, k, :].bitcast(F32), ALU.subtract).then_inc(split, 1)

            def take(n):
                if gate_dram is not None:
                    for i in range(TT):
                        dve.wait_ge(row_done, n * TT + i + 1)
                        at = out[:, i, bass.ds(n * width, width)]
                        dve.tensor_tensor(at, at, acc[:, i, 0:width], ALU.add).then_inc(taken, 1)

            if gate_dram is not None:
                dve.wait_ge(gate_in, 16)
            for c in range(slots):
                make_lo(0, c)
            steps(dve, per_block(make_lo, take))

        @block.tensor
        def _(pe):
            def one(n):
                for c in range(DC):
                    pe.wait_ge(split, n * DC + c + 1)
                    for i in range(TT):
                        if c == 0 and later(n, 0):
                            pe.wait_ge(taken, (n - 1) * TT + i + 1)
                        for m, (u, w) in enumerate(((u_hi, hi), (u_hi, lo), (u_lo, hi))):
                            last = pe.matmul(acc[:, i, 0:width], u[:, c, i * P:(i + 1) * P], w[:, c % slots, :],
                                             start=(c == 0 and m == 0), stop=(c == DC - 1 and m == 2))
                        if c == DC - 1:
                            last.then_inc(row_done, 1)
                    if c < DC - 1:
                        last.then_inc(used, 1)

            steps(pe, one)


def rope_rows(dve, at, heads, half, cos, sin, tmp, ticks):
    sem, n = ticks
    x1, x2 = at[:, :, 0:half], at[:, :, half:2 * half]
    wide = lambda table: table.unsqueeze(1).to_broadcast([P, heads, half])
    a, b, c, d = (tmp[:, k, 0:heads * half].rearrange("p (h j) -> p h j", j=half) for k in range(4))
    if n:
        dve.wait_ge(sem, n)
    dve.tensor_tensor(a, x1, wide(cos), ALU.mult).then_inc(sem, 1)
    dve.tensor_tensor(b, x2, wide(sin), ALU.mult).then_inc(sem, 1)
    dve.tensor_tensor(c, x2, wide(cos), ALU.mult).then_inc(sem, 1)
    dve.tensor_tensor(d, x1, wide(sin), ALU.mult).then_inc(sem, 1)
    dve.wait_ge(sem, n + 4)
    dve.tensor_tensor(x1, a, b, ALU.subtract).then_inc(sem, 1)
    dve.tensor_tensor(x2, c, d, ALU.add).then_inc(sem, 1)
    return sem, n + 6


def rope_sparse(nc, stage, h, table):
    with Scope(nc, stage) as s:
        tmp = s.sb("tmp", [P, 4, (HEADS + GROUPS) * ROPE_N // 2])
        ticks = s.sem("ticks")
        block = s.block()

        @block.vector
        def _(dve):
            count = (ticks, 0)
            half = ROPE_N // 2
            for i in range(TT):
                cos, sin = table[:, i, 0:half], table[:, i, half:2 * half]
                for col, heads in ((COL_Q, HEADS + GROUPS), (COL_KS, GROUPS), (COL_KW, GROUPS)):
                    at = h[:, i, col:col + heads * HD].rearrange("p (h d) -> p h d", d=HD)
                    count = rope_rows(dve, at, heads, half, cos, sin, tmp, count)
                half_m = ROPE_M // 2
                cos, sin = table[:, i, ROPE_N:ROPE_N + half_m], table[:, i, ROPE_N + half_m:ROPE_N + ROPE_M]
                at = h[:, i, COL_KR:COL_KR + ROPE_M].rearrange("p (h d) -> p h d", h=1)
                count = rope_rows(dve, at, 1, half_m, cos, sin, tmp, count)


def sparse_keys(nc, stage, h, ident, k_hi, k_lo, v, x2):
    with Scope(nc, stage) as s:
        tp = s.ps("tp", [P, 4, HALF])
        turned, hi_done, lo_done, moved = s.sem("turned"), s.sem("hi_done"), s.sem("lo_done"), s.sem("moved")
        v_hi_done = s.sem("v_hi_done")
        block = s.block()
        keys = [(br, half) for br in range(2) for half in range(2)]
        tokens = [(kv, half) for kv in range(2) for half in range(2)]
        col_k, col_v, col_c = (COL_KS, COL_KW), (COL_VS, COL_VW), (COL_KC, COL_VC)

        @block.tensor
        def _(pe):
            for n, (kind, half) in enumerate(keys + tokens):
                col = col_k[kind] if n < len(keys) else col_c[kind]
                if n >= 4:
                    pe.wait_ge(lo_done, 4 * (n - 3))
                for i in range(4):
                    t = pe.transpose(tp[:, n % 4, i * P:(i + 1) * P], h[:, 4 * half + i, col:col + P], ident[:, :])
                t.then_inc(turned, 1)

        @block.scalar
        def _(act):
            for n, (br, half) in enumerate(keys):
                act.wait_ge(turned, n + 1)
                for g in range(GROUPS):
                    for place in range(2):
                        act.activation(k_hi[place * HD:(place + 1) * HD, br, g, half * HALF:(half + 1) * HALF],
                                       tp[g * HD:(g + 1) * HD, n % 4, :], ACT.Copy).then_inc(hi_done, 1)
            for br in range(2):
                for g in range(GROUPS):
                    rows = h[:, :, col_v[br] + g * HD:col_v[br] + (g + 1) * HD]
                    act.activation(v[:, br, g, :, 0:HD], rows, ACT.Copy).then_inc(v_hi_done, 1)
            for n, (kv, half) in enumerate(tokens):
                act.wait_ge(turned, len(keys) + n + 1)
                for g in range(GROUPS):
                    for odd in range(2):
                        act.activation(x2[odd * HD:(odd + 1) * HD, kv, g, half * 256:(half + 1) * 256],
                                       tp[g * HD:(g + 1) * HD, n % 4, odd::2], ACT.Copy).then_inc(moved, 1)

        @block.vector
        def _(dve):
            for n, (br, half) in enumerate(keys):
                for g in range(GROUPS):
                    dve.wait_ge(hi_done, 4 * n + 2 * g + 2)
                    for place in range(2):
                        cols = slice(half * HALF, (half + 1) * HALF)
                        same = k_hi[g * HD:(g + 1) * HD, br, g, cols]
                        dve.tensor_tensor(k_lo[place * HD:(place + 1) * HD, br, g, cols], tp[g * HD:(g + 1) * HD, n % 4, :],
                                          same.bitcast(F32), ALU.subtract).then_inc(lo_done, 1)
            for n, (br, g) in enumerate((br, g) for br in range(2) for g in range(GROUPS)):
                dve.wait_ge(v_hi_done, n + 1)
                rows = h[:, :, col_v[br] + g * HD:col_v[br] + (g + 1) * HD]
                dve.tensor_tensor(v[:, br, g, :, HD:2 * HD], rows, v[:, br, g, :, 0:HD].bitcast(F32), ALU.subtract)


def compress(nc, stage, x2, pos, w1, w2, k_hi, k_lo, v):
    with Scope(nc, stage) as s:
        blocks = s.sb("blocks", [P, 2, CMP_PAIRS, GROUPS, CMP_PAD])
        w1_sb = s.sb("w1", [P, 2, CMP_PAIRS, CMP_HIDDEN])
        w2_sb = s.sb("w2", [P, 2, 2, P])
        pos_sb = s.sb("pos", [P, 2, CMP_PAIRS])
        hidden = s.sb("hidden", [P, 2, 2, GROUPS * CMP_PAD])
        hid_ps = s.ps("hid_ps", [P, 2, 2, HALF])
        out_ps = s.ps("out_ps", [P, 3, HALF])
        w_in, w2_in, pos_in, padded = s.sem("w_in"), s.sem("w2_in"), s.sem("pos_in"), s.sem("padded")
        placed, hid_done, gelu_done, out_done = s.sem("placed"), s.sem("hid_done"), s.sem("gelu_done"), s.sem("out_done")
        hi_done = s.sem("hi_done")
        block = s.block()

        @block.sync
        def _(sp):
            with nc.allow_non_contiguous_dma(reason="two small tables of positions with their dimension on partitions"):
                for kv in range(2):
                    sp.dma_start(pos_sb[:, kv, :], pos[kv][0].rearrange("(a j) d -> (j d) a", j=2)).then_inc(pos_in, 16)
            for kv in range(2):
                sp.dma_start(w1_sb[:, kv, :, :], w1[kv][0].rearrange("(a p) n -> p a n", p=P)).then_inc(w_in, 16)
                for twice in range(2):
                    sp.dma_start(w2_sb[:, kv, :, twice * HD:(twice + 1) * HD],
                                 w2[kv][0].rearrange("(m p) d -> p m d", p=P)).then_inc(w2_in, 16)

        @block.gpsimd
        def _(pool):
            pool.memset(blocks[:, :, :, :, N_CMP:CMP_PAD], 0.0).then_inc(padded, 1)

        @block.vector
        def _(dve):
            dve.wait_ge(pos_in, 32)
            for kv in range(2):
                for a in range(CMP_PAIRS):
                    tokens = x2[:, kv, :, a:a + 8 * (N_CMP - 1) + 1:8]
                    dve.tensor_scalar(blocks[:, kv, a, :, 0:N_CMP], tokens, pos_sb[:, kv, a:a + 1], None,
                                      ALU.add).then_inc(placed, 1)
            dve.wait_ge(hi_done, 1)
            keys = out_ps[:, 0, 0:GROUPS * CMP_PAD].rearrange("p (g n) -> p g n", g=GROUPS)
            dve.tensor_tensor(k_lo[:, :, :], keys, k_hi[:, :, :].bitcast(F32), ALU.subtract)
            for g in range(GROUPS):
                dve.wait_ge(hi_done, 2 + g)
                dve.tensor_tensor(v[0:CMP_PAD, g, HD:2 * HD], out_ps[0:CMP_PAD, 1 + g, 0:HD],
                                  v[0:CMP_PAD, g, 0:HD].bitcast(F32), ALU.subtract)

        @block.tensor
        def _(pe):
            pe.wait_ge(padded, 1)
            for kv in range(2):
                pe.wait_ge(w_in, 32)
                for m in range(2):
                    for a in range(CMP_PAIRS):
                        pe.wait_ge(placed, kv * CMP_PAIRS + a + 1)
                        last = pe.matmul(hid_ps[:, kv, m, 0:GROUPS * CMP_PAD], w1_sb[:, kv, a, m * P:(m + 1) * P],
                                         blocks[:, kv, a, :, :].rearrange("p g n -> p (g n)"),
                                         start=(a == 0), stop=(a == CMP_PAIRS - 1))
                    last.then_inc(hid_done, 1)
            pe.wait_ge(w2_in, 64)
            pe.wait_ge(gelu_done, 2)
            for m in range(2):
                last = pe.matmul(out_ps[:, 0, 0:GROUPS * CMP_PAD], w2_sb[:, 0, m, :], hidden[:, 0, m, :],
                                 start=(m == 0), stop=(m == 1))
            last.then_inc(out_done, 1)
            pe.wait_ge(gelu_done, 4)
            for g in range(GROUPS):
                for m in range(2):
                    last = pe.matmul(out_ps[0:CMP_PAD, 1 + g, 0:HD], hidden[:, 1, m, g * CMP_PAD:(g + 1) * CMP_PAD],
                                     w2_sb[:, 1, m, 0:HD], start=(m == 0), stop=(m == 1))
                last.then_inc(out_done, 1)

        @block.scalar
        def _(act):
            for n in range(4):
                kv, m = divmod(n, 2)
                act.wait_ge(hid_done, n + 1)
                act.activation(hidden[:, kv, m, :], hid_ps[:, kv, m, 0:GROUPS * CMP_PAD],
                               ACT.Gelu_apprx_tanh).then_inc(gelu_done, 1)
            act.wait_ge(out_done, 1)
            keys = out_ps[:, 0, 0:GROUPS * CMP_PAD].rearrange("p (g n) -> p g n", g=GROUPS)
            act.activation(k_hi[:, :, :], keys, ACT.Copy).then_inc(hi_done, 1)
            for g in range(GROUPS):
                act.wait_ge(out_done, 2 + g)
                act.activation(v[0:CMP_PAD, g, 0:HD], out_ps[0:CMP_PAD, 1 + g, 0:HD], ACT.Copy).then_inc(hi_done, 1)


def masks(nc, stage, ident, ident_r, causal, window, compressed):
    with Scope(nc, stage) as s:
        width = 2 * P + TT * CMP_PAD
        m = s.sb("m", [P, width])
        zeroed, cut, copied = s.sem("zeroed"), s.sem("cut"), s.sem("copied")
        block = s.block()

        @block.gpsimd
        def _(pool):
            pool.memset(m[:, :], 0.0).then_inc(zeroed, 1)
            pool.wait_ge(zeroed, 1)
            pool.affine_select(out=m[:, 0:P], in_=m[:, 0:P], compare_op=ALU.is_ge, fill=MASKED, base=0,
                               pattern=[[-1, P]], channel_multiplier=1).then_inc(cut, 1)
            pool.affine_select(out=m[:, P:2 * P], in_=m[:, P:2 * P], compare_op=ALU.is_gt, fill=MASKED, base=0,
                               pattern=[[1, P]], channel_multiplier=-1).then_inc(cut, 1)
            last = m[:, 2 * P:width].rearrange("p (i n) -> p i n", n=CMP_PAD)
            pool.affine_select(out=last, in_=last, compare_op=ALU.is_ge, fill=MASKED, base=1 - CMP_BLOCK,
                               pattern=[[P, TT], [-CMP_STRIDE, CMP_PAD]], channel_multiplier=1).then_inc(cut, 1)

        @block.vector
        def _(dve):
            dve.tensor_copy(ident_r[:, :], ident[:, :])
            dve.wait_ge(cut, 3)
            dve.tensor_copy(causal[:, :], m[:, 0:P])
            dve.tensor_copy(window[:, :], m[:, P:2 * P])
            dve.tensor_copy(compressed[:, :, :], m[:, 2 * P:width].rearrange("p (i n) -> p i n", n=CMP_PAD))


def latents(nc, stage, h, ident, q_norm, kv_norm, q_hi, q_lo, kv_hi, kv_lo):
    with Scope(nc, stage) as s:
        g_col = s.sb("g_col", [P, 5])
        square = s.sb("square", [P, Q_RANK])
        sums = s.sb("sums", [P, 2, TT])
        eps = s.sb("eps", [P, 1])
        root = s.sb("root", [P, 2, TT])
        rstd = s.sb("rstd", [P, 2, TT])
        u = s.sb("u", [P, 2, HALF])
        tp = s.ps("tp", [P, 4, HALF])
        g_in, eps_set, summed, rooted, inverted = (s.sem(x) for x in ("g_in", "eps_set", "summed", "rooted", "inverted"))
        scaled, turned, placed, hi_done, lo_done = (s.sem(x) for x in ("scaled", "turned", "placed", "hi_done", "lo_done"))
        block = s.block()
        sides = ((COL_CQ, Q_RANK), (COL_CKV, KV_RANK))
        units = [(n, c, half) for n in range(2) for c in range(sides[n][1] // P) for half in range(2)]

        @block.sync
        def _(sp):
            with nc.allow_non_contiguous_dma(reason="two norms' gains, one column each chunk"):
                sp.dma_start(g_col[:, 0:3], q_norm[0].rearrange("(c p) -> p c", p=P)).then_inc(g_in, 16)
                sp.dma_start(g_col[:, 3:5], kv_norm[0].rearrange("(c p) -> p c", p=P)).then_inc(g_in, 16)

        @block.scalar
        def _(act):
            count = 0
            for n, (col, rank) in enumerate(sides):
                for i in range(TT):
                    if count:
                        act.wait_ge(summed, count)
                    act.activation(square[:, 0:rank], h[:, i, col:col + rank], ACT.Square,
                                   accum_out=sums[:, n, i:i + 1]).then_inc(summed, 1)
                    count += 1
            act.wait_ge(summed, count)
            act.wait_ge(eps_set, 1)
            for n, (col, rank) in enumerate(sides):
                act.activation(root[:, n, :], sums[:, n, :], ACT.Sqrt, scale=1.0 / rank, bias=eps[:, 0:1]).then_inc(rooted, 1)
            act.wait_ge(g_in, 32)
            for m, (n, c, half) in enumerate(units):
                act.wait_ge(turned, m + 1)
                if m >= 2:
                    act.wait_ge(lo_done, m - 1)
                act.activation(u[:, m % 2, :], tp[:, m % 4, :], ACT.Copy, scale=g_col[:, 3 * n + c:3 * n + c + 1]).then_inc(placed, 1)

        @block.vector
        def _(dve):
            dve.memset(eps[:, :], EPS).then_inc(eps_set, 1)
            dve.wait_ge(rooted, 2)
            dve.reciprocal(rstd[:, :, :], root[:, :, :]).then_inc(inverted, 1)
            dve.wait_ge(inverted, 1)
            for n, (col, rank) in enumerate(sides):
                for i in range(TT):
                    at = h[:, i, col:col + rank]
                    dve.tensor_scalar(at, at, rstd[:, n, i:i + 1], None, ALU.mult).then_inc(scaled, 1)
            for m, (n, c, half) in enumerate(units):
                cols = slice(half * HALF, (half + 1) * HALF)
                hi, lo = ((q_hi, q_lo), (kv_hi, kv_lo))[n]
                dve.wait_ge(placed, m + 1)
                dve.tensor_copy(hi[:, c, cols], u[:, m % 2, :]).then_inc(hi_done, 1)
                dve.wait_ge(hi_done, m + 1)
                dve.tensor_tensor(lo[:, c, cols], u[:, m % 2, :], hi[:, c, cols].bitcast(F32), ALU.subtract).then_inc(lo_done, 1)

        @block.tensor
        def _(pe):
            pe.wait_ge(scaled, 2 * TT)
            for m, (n, c, half) in enumerate(units):
                if m >= 4:
                    pe.wait_ge(placed, m - 3)
                col = sides[n][0] + c * P
                for i in range(4):
                    t = pe.transpose(tp[:, m % 4, i * P:(i + 1) * P], h[:, 4 * half + i, col:col + P], ident[:, :])
                t.then_inc(turned, 1)


def latent_up(nc, stage, h, w_uq, w_ukv, q_hi, q_lo, kv_hi, kv_lo, ukv_hi, ukv_lo, v):
    with Scope(nc, stage) as s:
        half_q = HEADS * MD // 2
        uq_raw = s.sb("uq_raw", [P, 3, HEADS * MD])
        uq_hi = s.sb("uq_hi", [P, 3, HEADS * MD], F32R)
        uq_lo = s.sb("uq_lo", [P, 3, HEADS * MD], F32R)
        ukv_raw = s.sb("ukv_raw", [P, 2, HEADS * P])
        q_ps = s.ps("q_ps", [P, 4, HALF])
        v_ps = s.ps("v_ps", [P, 4, HALF])
        landed, hi_ready, split = s.sem("landed"), s.sem("hi_ready"), s.sem("split")
        v_done, v_hi_done, v_lo_done, q_done, q_taken = (s.sem(x) for x in ("v_done", "v_hi_done", "v_lo_done", "q_done", "q_taken"))
        block = s.block()
        parts = [(ukv_raw, ukv_hi, ukv_lo, 2), (uq_raw, uq_hi, uq_lo, 3)]

        @block.sync
        def _(sp):
            sp.dma_start(ukv_raw[:, :, :], w_ukv[0].rearrange("(c p) n -> p c n", p=P)).then_inc(landed, 16)
            sp.wait_ge(landed, 16)
            sp.dma_start(uq_raw[:, :, :], w_uq[0].rearrange("(c p) n -> p c n", p=P)).then_inc(landed, 16)

        @block.scalar
        def _(act):
            for m, (raw, hi, lo, chunks) in enumerate(parts):
                act.wait_ge(landed, 16 * (m + 1))
                for c in range(chunks):
                    act.activation(hi[:, c, :], raw[:, c, :], ACT.Copy).then_inc(hi_ready, 1)
            for i in range(TT):
                act.wait_ge(v_done, i + 1)
                act.activation(v[:, :, i, 0:HD], v_ps[:, i % 4, :].rearrange("p (h d) -> p h d", d=HD), ACT.Copy).then_inc(v_hi_done, 1)
            for n in range(2 * TT):
                i, e = divmod(n, 2)
                act.wait_ge(q_done, n + 1)
                at = h[:, i, COL_QM + e * half_q:COL_QM + (e + 1) * half_q]
                act.activation(at, q_ps[:, n % 4, 0:half_q], ACT.Copy, scale=MLA_SCALE).then_inc(q_taken, 1)

        @block.vector
        def _(dve):
            n = 0
            for raw, hi, lo, chunks in parts:
                for c in range(chunks):
                    n += 1
                    dve.wait_ge(hi_ready, n)
                    dve.tensor_tensor(lo[:, c, :], raw[:, c, :], hi[:, c, :].bitcast(F32), ALU.subtract).then_inc(split, 1)
            for i in range(TT):
                dve.wait_ge(v_hi_done, i + 1)
                dve.tensor_tensor(v[:, :, i, HD:2 * HD], v_ps[:, i % 4, :].rearrange("p (h d) -> p h d", d=HD),
                                  v[:, :, i, 0:HD].bitcast(F32), ALU.subtract).then_inc(v_lo_done, 1)

        @block.tensor
        def _(pe):
            pe.wait_ge(split, 2)
            for i in range(TT):
                if i >= 4:
                    pe.wait_ge(v_lo_done, i - 3)
                rows = slice(i * P, (i + 1) * P)
                for c in range(2):
                    for m, (a, w) in enumerate(((kv_hi, ukv_hi), (kv_hi, ukv_lo), (kv_lo, ukv_hi))):
                        values = w[:, c, :].rearrange("p (h d) -> p h d", d=P)[:, :, HD:2 * HD]
                        last = pe.matmul(v_ps[:, i % 4, :], a[:, c, rows], values, start=(c == 0 and m == 0), stop=(c == 1 and m == 2))
                last.then_inc(v_done, 1)
            pe.wait_ge(split, 5)
            for n in range(2 * TT):
                i, e = divmod(n, 2)
                if n >= 4:
                    pe.wait_ge(q_taken, n - 3)
                for c in range(3):
                    for m, (a, w) in enumerate(((q_hi, uq_hi), (q_hi, uq_lo), (q_lo, uq_hi))):
                        last = pe.matmul(q_ps[:, n % 4, 0:half_q], a[:, c, i * P:(i + 1) * P],
                                         w[:, c, e * half_q:(e + 1) * half_q], start=(c == 0 and m == 0), stop=(c == 2 and m == 2))
                last.then_inc(q_done, 1)


def rope_latent(nc, stage, h, table):
    with Scope(nc, stage) as s:
        half = ROPE_M // 2
        tmp = s.sb("tmp", [P, 4, HEADS * half])
        ticks = s.sem("ticks")
        block = s.block()

        @block.vector
        def _(dve):
            count = (ticks, 0)
            for i in range(TT):
                cos, sin = table[:, i, ROPE_N:ROPE_N + half], table[:, i, ROPE_N + half:ROPE_N + 2 * half]
                at = h[:, i, COL_QM:COL_QM + HEADS * MD].rearrange("p (h d) -> p h d", d=MD)[:, :, HD:MD]
                count = rope_rows(dve, at, HEADS, half, cos, sin, tmp, count)


class Unit:

    def __init__(self, blocks, keys, first_row, key_of, widths, mask_of, value_of, out, adds, gate, before):
        self.blocks = blocks
        self.keys = keys
        self.first_row = first_row
        self.key_of = key_of
        self.widths = widths
        self.mask_of = mask_of
        self.value_of = value_of
        self.out = out
        self.adds = adds
        self.gate = gate
        self.before = before


def attend(nc, stage, units, staging, ident, ident_r):
    steps = []

    def ahead(n):
        return [("stage", n, x) for x in units[n].before] + [("score", n, r) for r in range(4)]

    steps += ahead(0)
    for n, u in enumerate(units):
        later = ahead(n + 1) if n + 1 < len(units) else []
        for k in range(len(u.blocks)):
            steps.append(("turn", n, k))
            if k == 0 and n:
                steps.append(("finish", n - 1, 0))
            share = -(-len(later) // (len(u.blocks) - k))
            steps += later[:share]
            later = later[share:]
            if k:
                steps.append(("apply", n, k - 1))
        steps.append(("apply", n, len(u.blocks) - 1))
    steps.append(("finish", len(units) - 1, 0))

    turn_no = {x: m for m, x in enumerate(x for x in steps if x[0] == "turn")}
    side_no = {x: m for m, x in enumerate(x for x in steps if x[0] in ("stage", "finish"))}
    stage_no = {x: m for m, x in enumerate(x for x in steps if x[0] == "stage")}

    with Scope(nc, stage) as s:
        exps = s.sb("exps", [P, 2, 4, T])
        sums = s.sb("sums", [P, 2, 4])
        neg_max = s.sb("neg_max", [P, 2, 4])
        turned_hi = s.sb("turned_hi", [P, 2, HALF], F32R)
        turned_lo = s.sb("turned_lo", [P, 2, HALF], F32R)
        out_sb = s.sb("out_sb", [P, 4, P])
        floor = s.sb("floor", [P, 4])
        factor = s.sb("factor", [P, 4])
        factor_g = s.sb("factor_g", [P, 4])
        joined = s.sb("joined", [P, 4, HD])
        weighted = s.sb("weighted", [P, 4, HD])
        scores = s.ps("scores", [P, 2, T])
        turn_ps = s.ps("turn_ps", [P, 2, HALF])
        out_ps = s.ps("out_ps", [P, HALF])
        side_ps = s.ps("side_ps", [P, HALF])
        scored, maxed, exped, guarded = s.sem("scored"), s.sem("maxed"), s.sem("exped"), s.sem("guarded")
        turn_done, turn_hi, turn_split = s.sem("turn_done"), s.sem("turn_hi"), s.sem("turn_split")
        applied, out_moved = s.sem("applied"), s.sem("out_moved")
        side_done, side_hi, side_free = s.sem("side_done"), s.sem("side_hi"), s.sem("side_free")
        tail, fin = s.sem("tail"), s.sem("fin")
        block = s.block()

        @block.tensor
        def _(pe):
            for step in steps:
                kind, n, k = step
                u = units[n]
                if kind in ("stage", "finish"):
                    m = side_no[step]
                    if m:
                        pe.wait_ge(side_free, m)
                if kind == "stage":
                    staging.pe(pe, k, side_ps).then_inc(side_done, 1)
                elif kind == "score":
                    row = 4 * n + k
                    pe.wait_ge(side_free, staging.needed(step, steps, side_no))
                    if row >= 2:
                        pe.wait_ge(exped, row - 1)
                    w = u.widths[k]
                    for c0 in range(0, w, HALF):
                        c1 = min(c0 + HALF, w)
                        products = u.key_of(k, c0, c1 - c0)
                        for m, (q, key) in enumerate(products):
                            last = pe.matmul(scores[:, row % 2, c0:c1], q, key, start=(m == 0), stop=(m == len(products) - 1))
                            if m == 0:
                                for at, mask in u.mask_of(k):
                                    if c0 <= at < c1:
                                        pe.matmul(scores[:, row % 2, at:at + u.keys], ident_r[:, :], mask, start=False, stop=False)
                    last.then_inc(scored, 1)
                elif kind == "turn":
                    j = turn_no[step]
                    first = u.first_row(u.blocks[k])
                    pe.wait_ge(exped, 4 * n + 4)
                    if j >= 2:
                        pe.wait_ge(turn_split, j - 1)
                    for r in range(first, 4):
                        last = pe.transpose(turn_ps[0:u.keys, j % 2, r * P:(r + 1) * P],
                                            exps[:, n % 2, r, k * u.keys:(k + 1) * u.keys], ident[:, :])
                    last.then_inc(turn_done, 1)
                elif kind == "apply":
                    j = turn_no[("turn", n, k)]
                    cols = slice(u.first_row(u.blocks[k]) * P, HALF)
                    pe.wait_ge(turn_split, j + 1)
                    if k == 0 and n:
                        pe.wait_ge(out_moved, n)
                    for m, part in enumerate((turned_hi, turned_lo)):
                        last = pe.matmul(out_ps[:, cols], u.value_of(u.blocks[k]), part[0:u.keys, j % 2, cols],
                                         start=(k == 0 and m == 0), stop=(k == len(u.blocks) - 1 and m == 1))
                    last.then_inc(applied, 1)
                else:
                    pe.wait_ge(out_moved, n + 1)
                    for r in range(4):
                        last = pe.transpose(side_ps[:, r * P:(r + 1) * P], out_sb[:, r, :], ident[:, :])
                    last.then_inc(side_done, 1)

        @block.scalar
        def _(act):
            for step in steps:
                kind, n, k = step
                u = units[n]
                if kind == "stage":
                    act.wait_ge(side_done, side_no[step] + 1)
                    staging.act(act, k, side_ps).then_inc(side_hi, 1)
                elif kind == "score":
                    row = 4 * n + k
                    act.wait_ge(maxed, row + 1)
                    act.activation(exps[:, n % 2, k, 0:u.widths[k]], scores[:, row % 2, 0:u.widths[k]], ACT.Exp,
                                   bias=neg_max[:, n % 2, k:k + 1], accum_out=sums[:, n % 2, k:k + 1]).then_inc(exped, 1)
                elif kind == "turn":
                    j = turn_no[step]
                    cols = slice(u.first_row(u.blocks[k]) * P, HALF)
                    act.wait_ge(turn_done, j + 1)
                    if j >= 2:
                        act.wait_ge(applied, j - 1)
                    act.activation(turned_hi[0:u.keys, j % 2, cols], turn_ps[0:u.keys, j % 2, cols], ACT.Copy).then_inc(turn_hi, 1)
                elif kind == "apply" and k == len(u.blocks) - 1:
                    act.wait_ge(applied, turn_no[("turn", n, k)] + 1)
                    act.activation(out_sb[:, :, :].rearrange("p r c -> p (r c)"), out_ps[:, :], ACT.Copy).then_inc(out_moved, 1)

        @block.vector
        def _(dve):
            guards = 0
            for step in steps:
                kind, n, k = step
                u = units[n]
                if kind == "stage":
                    dve.wait_ge(side_hi, stage_no[step] + 1)
                    staging.dve(dve, k, side_ps).then_inc(side_free, 1)
                elif kind == "score":
                    row = 4 * n + k
                    dve.wait_ge(scored, row + 1)
                    at = neg_max[:, n % 2, k:k + 1]
                    top = dve.reduce_max(at, scores[:, row % 2, 0:u.widths[k]], AX, negate=True)
                    if u.keys == CMP_PAD:
                        top.then_inc(guarded, 1)
                        guards += 1
                        dve.wait_ge(guarded, guards)
                        top = dve.tensor_scalar(at, at, -NO_KEY, None, ALU.min)
                    top.then_inc(maxed, 1)
                elif kind == "turn":
                    j = turn_no[step]
                    cols = slice(u.first_row(u.blocks[k]) * P, HALF)
                    dve.wait_ge(turn_hi, j + 1)
                    dve.tensor_tensor(turned_lo[0:u.keys, j % 2, cols], turn_ps[0:u.keys, j % 2, cols],
                                      turned_hi[0:u.keys, j % 2, cols].bitcast(F32), ALU.subtract).then_inc(turn_split, 1)
                elif kind == "finish":
                    if n:
                        dve.wait_ge(fin, n)
                    dve.tensor_scalar(floor[:, :], sums[:, n % 2, :], 1e-30, None, ALU.max).then_inc(tail, 1)
                    dve.wait_ge(tail, 3 * n + 1)
                    dve.reciprocal(factor[:, :], floor[:, :]).then_inc(tail, 1)
                    dve.wait_ge(side_done, side_no[step] + 1)
                    parts = side_ps[:, :].rearrange("p (r a d) -> p r d a", a=2, d=HD)
                    dve.tensor_reduce(joined[:, :, :], parts, AX, ALU.add).then_inc(side_free, 1)
                    dve.wait_ge(tail, 3 * n + 2)
                    by = factor
                    if u.gate is not None:
                        dve.tensor_tensor(factor_g[:, :], factor[:, :], u.gate, ALU.mult).then_inc(tail, 1)
                        dve.wait_ge(tail, 3 * n + 3)
                        by = factor_g
                    else:
                        dve.sem_inc(tail, 1)
                    dve.wait_ge(side_free, side_no[step] + 1)
                    wide = by[:, :].unsqueeze(2).to_broadcast([P, 4, HD])
                    if u.adds:
                        dve.tensor_tensor(weighted[:, :, :], joined[:, :, :], wide, ALU.mult).then_inc(guarded, 1)
                        guards += 1
                        dve.wait_ge(guarded, guards)
                        dve.tensor_tensor(u.out, u.out, weighted[:, :, :], ALU.add).then_inc(fin, 1)
                    else:
                        dve.tensor_tensor(u.out, joined[:, :, :], wide, ALU.mult).then_inc(fin, 1)


def sparse_attention(nc, stage, h, k_hi, k_lo, v, kc_hi, kc_lo, vc, gates, ident, ident_r, causal, window, compressed):
    with Scope(nc, stage) as s:
        q = s.sb("q", [P, 2, HPG, P], F32R)

        class Staging:

            def places(self, t, side):
                for odd in range(2):
                    own, other = slice(odd * HD, (odd + 1) * HD), slice((1 - odd) * HD, (2 - odd) * HD)
                    rows = side[own, 0:2 * P].rearrange("p (a n) -> p a n", a=2)
                    yield rows, q[own, t % 2, odd::2, :], q[other, t % 2, odd::2, :]

            def pe(self, pe, t, side):
                g, i = divmod(t, TT)
                for pair in range(2):
                    col = COL_Q + (g * HPG + 2 * pair) * HD
                    last = pe.transpose(side[:, pair * P:(pair + 1) * P], h[:, i, col:col + P], ident[:, :])
                return last

            def act(self, act, t, side):
                for rows, hi, lo in self.places(t, side):
                    last = act.activation(hi, rows, ACT.Copy, scale=NSA_SCALE)
                return last

            def dve(self, dve, t, side):
                for rows, hi, lo in self.places(t, side):
                    last = dve.scalar_tensor_tensor(out=lo, in0=rows, scalar=NSA_SCALE, in1=hi.bitcast(F32),
                                                    op0=ALU.mult, op1=ALU.subtract)
                return last

            def needed(self, step, steps, side_no):
                tiles = [x for x in steps if x[0] == "stage" and x[1] <= step[1]]
                return side_no[tiles[-1]] + 1

        def unit(g, i, branch):
            col = COL_Q + g * HPG * HD
            out = h[:, i, col:col + HPG * HD].rearrange("p (r d) -> p r d", d=HD)
            gate = gates[:, i, g * HPG * 3 + (1, 2, 0)[branch]:(g + 1) * HPG * 3:3]
            at = (g * TT + i) % 2
            if branch == 2:
                blocks, keys, base = [0], CMP_PAD, 0
                kh, kl = kc_hi[:, g, :], kc_lo[:, g, :]
                mask = [(0, compressed[:, i, :])]
                value = lambda j: vc[0:CMP_PAD, g, :]
            else:
                blocks = list(range(max(0, i - WINDOW_BLOCKS) if branch == 1 else 0, i + 1))
                keys, base = P, blocks[0] * P
                kh, kl = k_hi[:, branch, g, :], k_lo[:, branch, g, :]
                mask = [((len(blocks) - 1) * P, causal[:, :])]
                if branch == 1 and i >= WINDOW_BLOCKS:
                    mask.append((0, window[:, :]))
                value = lambda j: v[:, branch, g, j, :]

            def key_of(r, c0, w):
                return [(q[:, at, r, :], k[:, base + c0:base + c0 + w]) for k in (kh, kl)]

            return Unit(blocks, keys, lambda j: 0, key_of, [len(blocks) * keys] * 4, lambda r: mask, value, out,
                        branch > 0, gate, [g * TT + i] if branch == 0 else [])

        units = [unit(g, i, b) for g in range(GROUPS) for i in range(TT) for b in range(3)]
        attend(nc, stage + "a", units, Staging(), ident, ident_r)


def latent_attention(nc, stage, h, kv_hi, kv_lo, ukv_hi, ukv_lo, v, ident, ident_r, causal):
    with Scope(nc, stage) as s:
        k_hi = s.sb("k_hi", [P, 2, T], F32R)
        k_lo = s.sb("k_lo", [P, 2, T], F32R)
        q_hi = s.sb("q_hi", [P, 2, HALF], F32R)
        q_lo = s.sb("q_lo", [P, 2, HALF], F32R)

        class Staging:

            def pe(self, pe, what, side):
                if what[0] == "k":
                    _, head, half = what
                    for c in range(2):
                        for m, (w, a) in enumerate(((ukv_hi, kv_hi), (ukv_hi, kv_lo), (ukv_lo, kv_hi))):
                            last = pe.matmul(side[:, :], w[:, c, head * P:(head + 1) * P], a[:, c, half * HALF:(half + 1) * HALF],
                                             start=(c == 0 and m == 0), stop=(c == 1 and m == 2))
                    return last
                for r in range(4):
                    if what[0] == "q":
                        _, head, half = what
                        rows = h[:, 4 * half + r, COL_QM + head * MD:COL_QM + (head + 1) * MD]
                    else:
                        rows = h[:, 4 * what[1] + r, COL_KR - HD:COL_KR + ROPE_M]
                    last = pe.transpose(side[0:MD, r * P:(r + 1) * P], rows, ident[:, :])
                return last

            def places(self, what, side):
                if what[0] == "q":
                    _, head, half = what
                    return [(side[0:MD, :], q_hi[0:MD, half, :], q_lo[0:MD, half, :])]
                cols = slice(what[-1] * HALF, (what[-1] + 1) * HALF)
                if what[0] == "k":
                    b = what[1] % 2
                    return [(side[0:HD, :], k_hi[0:HD, b, cols], k_lo[0:HD, b, cols])]
                return [(side[HD:MD, :], k_hi[HD:MD, b, cols], k_lo[HD:MD, b, cols]) for b in range(2)]

            def act(self, act, what, side):
                for rows, hi, lo in self.places(what, side):
                    last = act.activation(hi, rows, ACT.Copy)
                return last

            def dve(self, dve, what, side):
                for rows, hi, lo in self.places(what, side):
                    last = dve.tensor_tensor(lo, rows, hi.bitcast(F32), ALU.subtract)
                return last

            def needed(self, step, steps, side_no):
                own = [x for x in steps if x[0] == "stage" and x[1] <= step[1]]
                return side_no[own[-1]] + 1

        def unit(head, half):
            blocks = list(range(4 * half + 4))
            b = head % 2
            col = COL_QM + head * HD
            out = h[:, 4 * half:4 * half + 4, col:col + HD]

            def key_of(r, c0, w):
                rows = slice(r * P, (r + 1) * P)
                hi, lo = q_hi[0:MD, half, rows], q_lo[0:MD, half, rows]
                return [(hi, k_hi[0:MD, b, c0:c0 + w]), (hi, k_lo[0:MD, b, c0:c0 + w]), (lo, k_hi[0:MD, b, c0:c0 + w])]

            before = [("k", head, half), ("q", head, half)]
            if head == 0:
                before = [("r", half)] + before
            widths = [(4 * half + r + 1) * P for r in range(4)]
            return Unit(blocks, P, lambda j: max(0, j - 4 * half), key_of, widths,
                        lambda r: [((4 * half + r) * P, causal[:, :])], lambda j: v[:, head, j, :], out, False, None, before)

        units = [unit(head, half) for head in range(HEADS) for half in range(2)]
        attend(nc, stage + "a", units, Staging(), ident, ident_r)


def load_rows(nc, stage, pairs):
    with Scope(nc, stage) as s:
        landed = s.sem("landed")
        block = s.block()

        @block.sync
        def _(sp):
            for place, rows in pairs:
                sp.dma_start(place, rows.rearrange("(i p) d -> p i d", p=P)).then_inc(landed, 16)
            sp.wait_ge(landed, 16 * len(pairs))


def sigmoid_gates(nc, stage, h, gates):
    with Scope(nc, stage) as s:
        block = s.block()

        @block.scalar
        def _(act):
            act.activation(gates[:, :, :], h[:, :, COL_GATE:COL_GATE + N_GATE], ACT.Sigmoid)


def spilled(nc, stage, sem, count):
    with Scope(nc, stage) as s:
        block = s.block()

        @block.sync
        def _(sp):
            sp.wait_ge(sem, count)


def clear_semaphores(nc):
    nc.clear_and_free_semaphores(Scope.finished)
    nc.all_engine_barrier()
    Scope.finished = []


def layer(nc, x, c, w_ada, b_ada, ln_g, ln_b, ffn1_wg, ffn1_wu, ffn1_wd, w_in, cmp_k_pos, cmp_k_w1, cmp_k_w2,
          cmp_v_pos, cmp_v_w1, cmp_v_w2, mla_q_norm, mla_kv_norm, mla_w_uq, mla_w_ukv, w_out, ffn2_wg, ffn2_wu,
          ffn2_wd, rope_table, out):
    Scope.finished = []
    gate_dram = nc.dram_tensor("gate_rows", [3, D], F32, kind="Internal").ap()
    x_dram = nc.dram_tensor("x_rows", [T, D], F32, kind="Internal").ap()
    norm_rows = lambda n: (ln_g[0, n:n + 1, :], ln_b[0, n:n + 1, :])
    with Scope(nc, "all") as a:
        ident = a.sb("ident", [P, P])
        ones = a.sb("ones", [P, P])
        ident_r = a.sb("ident_r", [P, P], F32R)
        causal = a.sb("causal", [P, P], F32R)
        window = a.sb("window", [P, P], F32R)
        compressed = a.sb("compressed", [P, TT, CMP_PAD], F32R)
        table = a.sb("table", [P, TT, ROPE_N + ROPE_M])
        gates = a.sb("gates", [P, TT, N_GATE])
        shift = a.sb("shift", [P, 3, DC])
        scale = a.sb("scale", [P, 3, DC])
        x_out = a.sem("x_out")
        constants(nc, ident, ones)
        masks(nc, "masks", ident, ident_r, causal, window, compressed)
        load_rows(nc, "tables", [(table[:, :, :], rope_table)])

        with ExitStack() as h_alive:
            with Scope(nc, "mix_in", side="right") as r:
                x_sb = r.sb("x", [P, TT, D])
                modulation(nc, c, w_ada, b_ada, x, ones, x_sb, shift, scale, gate_dram)
                u_hi = r.sb("u_hi", [P, DC, T], F32R)
                u_lo = r.sb("u_lo", [P, DC, T], F32R)
                modulated_transpose(nc, "turn1", x_sb, shift[:, 0, :], scale[:, 0, :], ident, u_hi, u_lo)
                swiglu(nc, "ffn1", ffn1_wg, ffn1_wu, ffn1_wd, gate_dram[0:1, :], x_sb, u_hi, u_lo)
                layer_norm(nc, "norm1", x_sb, *norm_rows(0))
                modulated_transpose(nc, "turn2", x_sb, shift[:, 1, :], scale[:, 1, :], ident, u_hi, u_lo, (x_dram, x_out))
                h = h_alive.enter_context(Scope(nc, "h")).sb("h", [P, TT, D_IN])
                project(nc, "in", w_in[0], D_IN // 4, 4, u_hi, u_lo, h)
                spilled(nc, "x_kept", x_out, 16 * TT)

            clear_semaphores(nc)
            rope_sparse(nc, "rope1", h, table)
            sigmoid_gates(nc, "gates", h, gates)
            with Scope(nc, "sparse") as b:
                k_hi = b.sb("k_hi", [P, 2, GROUPS, T], F32R)
                k_lo = b.sb("k_lo", [P, 2, GROUPS, T], F32R)
                v = b.sb("v", [P, 2, GROUPS, TT, P], F32R)
                kc_hi = b.sb("kc_hi", [P, GROUPS, CMP_PAD], F32R)
                kc_lo = b.sb("kc_lo", [P, GROUPS, CMP_PAD], F32R)
                vc = b.sb("vc", [P, GROUPS, P], F32R)
                with Scope(nc, "compress") as t:
                    x2 = t.sb("x2", [P, 2, GROUPS, HALF])
                    sparse_keys(nc, "keys", h, ident, k_hi, k_lo, v, x2)
                    compress(nc, "cmp", x2, (cmp_k_pos, cmp_v_pos), (cmp_k_w1, cmp_v_w1), (cmp_k_w2, cmp_v_w2),
                             kc_hi, kc_lo, vc)
                sparse_attention(nc, "nsa", h, k_hi, k_lo, v, kc_hi, kc_lo, vc, gates, ident, ident_r, causal, window,
                                 compressed)
            with Scope(nc, "latent") as b:
                kv_hi = b.sb("kv_hi", [P, 2, T], F32R)
                kv_lo = b.sb("kv_lo", [P, 2, T], F32R)
                ukv_hi = b.sb("ukv_hi", [P, 2, HEADS * P], F32R)
                ukv_lo = b.sb("ukv_lo", [P, 2, HEADS * P], F32R)
                v = b.sb("v", [P, HEADS, TT, P], F32R)
                with Scope(nc, "queries") as t:
                    q_hi = t.sb("q_hi", [P, 3, T], F32R)
                    q_lo = t.sb("q_lo", [P, 3, T], F32R)
                    latents(nc, "rms", h, ident, mla_q_norm, mla_kv_norm, q_hi, q_lo, kv_hi, kv_lo)
                    latent_up(nc, "up", h, mla_w_uq, mla_w_ukv, q_hi, q_lo, kv_hi, kv_lo, ukv_hi, ukv_lo, v)
                rope_latent(nc, "rope2", h, table)
                latent_attention(nc, "mla", h, kv_hi, kv_lo, ukv_hi, ukv_lo, v, ident, ident_r, causal)

            clear_semaphores(nc)
            r = Scope(nc, "mix_out", side="right")
            r.__enter__()
            x_sb = r.sb("x", [P, TT, D])
            u_hi = r.sb("u_hi", [P, DC, T], F32R)
            u_lo = r.sb("u_lo", [P, DC, T], F32R)
            load_rows(nc, "x_back", [(x_sb[:, :, :], x_dram)])
            modulated_transpose(nc, "turn3", h, None, None, ident, u_hi, u_lo)
        project(nc, "out", w_out[0], HALF, 2, u_hi, u_lo, x_sb, gate_dram[1:2, :])
        layer_norm(nc, "norm2", x_sb, *norm_rows(1))
        modulated_transpose(nc, "turn4", x_sb, shift[:, 2, :], scale[:, 2, :], ident, u_hi, u_lo)
        swiglu(nc, "ffn2", ffn2_wg, ffn2_wu, ffn2_wd, gate_dram[2:3, :], x_sb, u_hi, u_lo)
        layer_norm(nc, "norm3", x_sb, *norm_rows(2), out)
        r.__exit__(None, None, None)


INPUTS = ("x", "c", "w_ada", "b_ada", "ln_g", "ln_b", "ffn1_wg", "ffn1_wu", "ffn1_wd", "w_in", "cmp_k_pos", "cmp_k_w1",
          "cmp_k_w2", "cmp_v_pos", "cmp_v_w1", "cmp_v_w2", "mla_q_norm", "mla_kv_norm", "mla_w_uq", "mla_w_ukv",
          "w_out", "ffn2_wg", "ffn2_wu", "ffn2_wd")


def rope_rows_table():
    import numpy as np

    parts = []
    for width in (ROPE_N, ROPE_M):
        half = width // 2
        inverse = np.float32(ROPE_THETA) ** (-np.arange(half, dtype=np.float32) / np.float32(half))
        angle = np.arange(T, dtype=np.float32)[:, None] * inverse[None, :]
        parts += [np.cos(angle), np.sin(angle)]
    return np.concatenate(parts, axis=1).astype(np.float32)


def kernel(**inputs):
    import numpy as np
    import concourse.bacc as bacc
    from concourse.bass_utils import run_bass_kernel_spmd

    nc = bacc.Bacc("TRN2", target_bir_lowering=False, num_devices=1)
    arrays = {f"in_{name}": np.ascontiguousarray(inputs[name]) for name in INPUTS}
    arrays["in_rope_table"] = rope_rows_table()
    args = [nc.dram_tensor(name, a.shape, mybir.dt.from_np(a.dtype), kind="ExternalInput").ap() for name, a in arrays.items()]
    out = nc.dram_tensor("out_x", (1, T, D), F32, kind="ExternalOutput").ap()
    layer(nc, *args, out)
    result = run_bass_kernel_spmd(nc, [arrays], core_ids=[0])
    return result.results[0]["out_x"]
```

```python
from contextlib import ExitStack

import concourse.bass as bass
from concourse import mybir

F32 = mybir.dt.float32
F32R = mybir.dt.float32r
ALU = mybir.AluOpType
ACT = mybir.ActivationFunctionType
AX = mybir.AxisListType.X

P = 128
HALF = 512
T = 1024
D = 1024
TT = T // P
DC = D // P
D_FF = 2816
FC = D_FF // P
N_MOD = 9
ALPHA = 2.0 ** 0.25
EPS = 1e-5

HD = 64
HEADS = 8
GROUPS = 2
HPG = HEADS // GROUPS
COL_Q = 0
COL_KC, COL_VC, COL_KS, COL_VS, COL_KW, COL_VW = (HEADS * HD + n * GROUPS * HD for n in range(6))
COL_GATE = COL_VW + GROUPS * HD
N_GATE = 3 * HEADS
Q_RANK = 384
KV_RANK = 256
COL_CQ = COL_GATE + N_GATE
COL_CKV = COL_CQ + Q_RANK
COL_KR = COL_CKV + KV_RANK
ROPE_N = 16
ROPE_M = 32
D_IN = COL_KR + ROPE_M
MD = HD + ROPE_M
COL_QM = HEADS * HD
NSA_SCALE = HD ** -0.5
MLA_SCALE = MD ** -0.5
ROPE_THETA = 500000.0

N_CMP = 63
CMP_PAD = 64
CMP_STRIDE = 16
CMP_BLOCK = 32
CMP_PAIRS = CMP_BLOCK // 2
CMP_HIDDEN = 4 * HD
WINDOW_BLOCKS = 4
MASKED = -1e30
NO_KEY = -1e20


class Scope:

    finished = []

    def __init__(self, nc, stage, side="left"):
        self.nc, self.stage, self.side, self.stack, self.sems = nc, stage, side, ExitStack(), []

    def __enter__(self):
        self.stack.__enter__()
        return self

    def __exit__(self, *a):
        Scope.finished += self.sems
        return self.stack.__exit__(*a)

    def sb(self, name, shape, dt=F32):
        return self.stack.enter_context(self.nc.sbuf_tensor(f"{self.stage}_{name}", shape, dt, side=self.side))

    def ps(self, name, shape):
        return self.stack.enter_context(self.nc.psum_tensor(f"{self.stage}_{name}", shape, F32))

    def sem(self, name):
        self.sems.append(self.nc.alloc_semaphore(f"{self.stage}_{name}"))
        return self.sems[-1]

    def block(self):
        return self.stack.enter_context(self.nc.Block())


def constants(nc, ident, ones):
    with Scope(nc, "const") as s:
        filled = s.sem("filled")
        block = s.block()

        @block.gpsimd
        def _(pool):
            pool.memset(ones[:, :], 1.0)
            pool.memset(ident[:, :], 0.0).then_inc(filled, 1)
            pool.wait_ge(filled, 1)
            pool.affine_select(out=ident[:, :], in_=ident[:, :], compare_op=ALU.not_equal, fill=1.0,
                               base=0, pattern=[[-1, P]], channel_multiplier=1)


def modulation(nc, c, w_ada, b_ada, x, ones, x_sb, shift, scale, gate_dram):
    with Scope(nc, "mod") as s:
        gate = s.sb("gate", [P, 3, D])
        gate_made, gate_out = s.sem("gate_made"), s.sem("gate_out")
        c_col = s.sb("c_col", [P, DC])
        silu_c = s.sb("silu_c", [P, DC])
        w = s.sb("w", [P, DC, D])
        part = s.sb("part", [P, N_MOD, D])
        cols = s.ps("cols", [P, 6, DC])
        rows = s.ps("rows", [P, 6, HALF])
        x_in, c_in, b_in, w_in = s.sem("x_in"), s.sem("c_in"), s.sem("b_in"), [s.sem(f"w_in{k}") for k in range(DC)]
        zeroed, silu_done, w_used = s.sem("zeroed"), s.sem("silu_done"), s.sem("w_used")
        summed, moved = s.sem("summed"), s.sem("moved")
        block = s.block()
        w_src = w_ada[0].rearrange("(p k) n -> p k n", k=DC)

        @block.sync
        def _(sp):
            sp.dma_start(c_col[:, :], c.rearrange("b (p k) -> (b p) k", k=DC)).then_inc(c_in, 16)
            sp.wait_ge(zeroed, 1)
            sp.dma_start(part[0:1, :, :], b_ada.rearrange("l (v n) -> l v n", n=D)).then_inc(b_in, 16)

            def load(v):
                for k in range(DC):
                    if not isinstance(v, int):
                        sp.wait_ge(w_used, (v - 1) * DC + k + 1)
                    sp.dma_start(w[:, k, :], w_src[:, k, bass.ts(v, D)]).then_inc(w_in[k], 16)

            load(0)
            with sp.Fori(1, N_MOD) as v:
                load(v)
            sp.dma_start(x_sb[:, :, :], x[0].rearrange("(i p) d -> p i d", p=P)).then_inc(x_in, 16)
            sp.wait_ge(x_in, 16)
            sp.wait_ge(gate_made, 3)
            sp.dma_start(gate_dram.unsqueeze(0), gate[0:1, :, :]).then_inc(gate_out, 16)
            sp.wait_ge(gate_out, 16)

        @block.gpsimd
        def _(pool):
            pool.memset(part[:, :, :], 0.0).then_inc(zeroed, 1)

        @block.scalar
        def _(act):
            act.wait_ge(c_in, 16)
            act.activation(silu_c[:, :], c_col[:, :], ACT.Silu).then_inc(silu_done, 1)
            act.wait_ge(summed, 1)
            for n in range(3):
                act.activation(shift[:, n, :], cols[:, 2 * n, :], ACT.Identity)
                act.activation(scale[:, n, :], cols[:, 2 * n + 1, :], ACT.Identity, bias=ones[:, 0:1])
            half_one = (0.5, 1.0, 0.5)
            for n in range(3):
                f = half_one[n]
                act.activation(gate[0:1, n, :], rows[0:1, 2 * n:2 * n + 2, :].rearrange("p a b -> p (a b)"),
                               ACT.Copy, scale=f, bias=f).then_inc(gate_made, 1)

        @block.vector
        def _(dve):
            dve.wait_ge(silu_done, 1)
            dve.wait_ge(b_in, 16)

            def weigh(v):
                for k in range(DC):
                    dve.wait_ge(w_in[k], v * 16 + 16)
                    if not isinstance(v, int) or k:
                        dve.wait_ge(w_used, v * DC + k)
                    acc = part[:, bass.ts(v, 1), :].rearrange("p a n -> p (a n)")
                    dve.scalar_tensor_tensor(out=acc, in0=w[:, k, :], scalar=silu_c[:, k:k + 1], in1=acc,
                                             op0=ALU.mult, op1=ALU.add).then_inc(w_used, 1)

            weigh(0)
            with dve.Fori(1, N_MOD) as v:
                weigh(v)

        @block.tensor
        def _(pe):
            pe.wait_ge(w_used, N_MOD * DC)
            for n in range(3):
                for q in range(2):
                    for cc in range(DC):
                        pe.matmul(cols[:, 2 * n + q, cc:cc + 1], part[:, 3 * n + q, cc * P:(cc + 1) * P],
                                  ones[:, 0:1], start=True, stop=True)
                for h in range(2):
                    last = pe.matmul(rows[0:1, 2 * n + h, :], ones[:, 0:1], part[:, 3 * n + 2, h * HALF:(h + 1) * HALF],
                                     start=True, stop=True)
            last.then_inc(summed, 1)


def modulated_transpose(nc, stage, x_sb, shift, scale, ident, u_hi, u_lo, spill=None, reload=None):
    with Scope(nc, stage) as s:
        u = s.sb("u", [P, 2, HALF])
        tp = s.ps("tp", [P, 4, HALF])
        turned, placed, hi_done, lo_done = s.sem("turned"), s.sem("placed"), s.sem("hi_done"), s.sem("lo_done")
        block = s.block()
        units = [(c, h) for c in range(DC) for h in range(2)]
        grown = s.sem("grown")

        @block.sync
        def _(sp):
            if reload is not None:
                for i in range(TT):
                    sp.dma_start(reload[0][:, i, :], reload[1][i * P:(i + 1) * P, :]).then_inc(reload[2], 16)
            if spill is not None:
                for i in range(TT):
                    sp.wait_ge(grown, i + 1)
                    sp.dma_start(spill[0][i * P:(i + 1) * P, :], x_sb[:, i, :]).then_inc(spill[1], 16)

        @block.tensor
        def _(pe):
            for n, (c, h) in enumerate(units):
                if n >= 4:
                    pe.wait_ge(placed, n - 3)
                for i in range(4):
                    t = pe.transpose(tp[:, n % 4, i * P:(i + 1) * P], x_sb[:, 4 * h + i, c * P:(c + 1) * P], ident[:, :])
                t.then_inc(turned, 1)

        @block.scalar
        def _(act):
            for n, (c, h) in enumerate(units):
                act.wait_ge(turned, n + 1)
                if n >= 2:
                    act.wait_ge(lo_done, n - 1)
                if scale is None:
                    made = act.activation(u[:, n % 2, :], tp[:, n % 4, :], ACT.Copy)
                else:
                    made = act.activation(u[:, n % 2, :], tp[:, n % 4, :], ACT.Identity, scale=scale[:, c:c + 1],
                                          bias=shift[:, c:c + 1])
                made.then_inc(placed, 1)
            if scale is not None:
                for i in range(TT):
                    act.mul(x_sb[:, i, :], x_sb[:, i, :], ALPHA).then_inc(grown, 1)

        @block.vector
        def _(dve):
            for n, (c, h) in enumerate(units):
                dve.wait_ge(placed, n + 1)
                hi = u_hi[:, c, h * HALF:(h + 1) * HALF]
                dve.tensor_copy(hi, u[:, n % 2, :]).then_inc(hi_done, 1)
                dve.wait_ge(hi_done, n + 1)
                dve.tensor_tensor(u_lo[:, c, h * HALF:(h + 1) * HALF], u[:, n % 2, :], hi.bitcast(F32),
                                  ALU.subtract).then_inc(lo_done, 1)


def swiglu(nc, stage, wg, wu, wd, gate_dram, x_sb, u_hi, u_lo):
    with Scope(nc, stage) as s:
        raw = {k: s.sb(f"w{k}_raw", [P, DC, P]) for k in "gud"}
        hi = {k: s.sb(f"w{k}_hi", [P, DC, P], F32R) for k in "gud"}
        lo = {k: s.sb(f"w{k}_lo", [P, DC, P], F32R) for k in "gud"}
        wd_gated = s.sb("wd_gated", [P, D])
        gate = s.sb("gate", [P, D])
        gate_in = s.sem("gate_in")
        silu_g = s.sb("silu_g", [P, T])
        h_f32 = s.sb("h_f32", [P, T])
        h_hi = s.sb("h_hi", [P, 2, T], F32R)
        h_lo = s.sb("h_lo", [P, 2, T], F32R)
        g_ps = s.ps("g_ps", [P, T])
        u_ps = s.ps("u_ps", [P, T])
        y_ps = s.ps("y_ps", [P, 2, D])
        landed = {k: s.sem(f"w{k}_landed") for k in "gud"}
        hi_ready = {k: s.sem(f"w{k}_hi_ready") for k in "gud"}
        split = {k: s.sem(f"w{k}_split") for k in "gud"}
        g_done, u_done, y_done = s.sem("g_done"), s.sem("u_done"), s.sem("y_done")
        silu_done, h_made, h_hi_ready, h_split = s.sem("silu_done"), s.sem("h_made"), s.sem("h_hi_ready"), s.sem("h_split")
        gated, y_added = s.sem("gated"), s.sem("y_added")
        block = s.block()
        flat = lambda a: a.rearrange("p c n -> p (c n)")
        src = {k: a[0].rearrange("(c p) n -> p c n", p=P) for k, a in (("g", wg), ("u", wu))}
        src["d"] = wd[0].rearrange("(f p) n -> f p n", p=P)

        def steps(eng, one, tail=None):
            one(0, 0)
            one(1, 1)
            with eng.Fori(2, FC - 2, 2) as f:
                one(f, 0)
                one(f + 1, 1)
            one(FC - 2, 0)
            one(FC - 1, 1)

        def after_first(f):
            return not isinstance(f, int) or f > 0

        def not_last(f):
            return not isinstance(f, int) or f < FC - 1

        @block.sync
        def _(sp):
            def load(f, parity):
                for k in "gud":
                    if after_first(f):
                        sp.wait_ge(gated if k == "d" else split[k], f)
                    if k == "d":
                        at = src["d"][bass.ts(f, 1)].rearrange("a p n -> p (a n)")
                        sp.dma_start(flat(raw["d"]), at).then_inc(landed["d"], 16)
                    else:
                        sp.dma_start(raw[k][:, :, :], src[k][:, :, bass.ts(f, P)]).then_inc(landed[k], 16)

            sp.dma_start(gate[:, :], gate_dram.to_broadcast([P, D])).then_inc(gate_in, 16)
            steps(sp, load)

        @block.scalar
        def _(act):
            def hi_of(k, f, source, done):
                if after_first(f):
                    act.wait_ge(done, f * (TT if k == "d" else 1))
                act.activation(flat(hi[k]), source, ACT.Copy).then_inc(hi_ready[k], 1)

            def hidden(f, parity):
                act.wait_ge(gated, f + 1)
                hi_of("d", f, wd_gated[:, :], y_done)
                act.wait_ge(h_made, f + 1)
                act.activation(h_hi[:, parity, :], h_f32[:, :], ACT.Copy).then_inc(h_hi_ready, 1)

            def step(f, parity):
                act.wait_ge(landed["u"], f * 16 + 16)
                hi_of("u", f, flat(raw["u"]), u_done)
                if after_first(f):
                    hidden(f - 1, 1 - parity)
                act.wait_ge(g_done, f + 1)
                if after_first(f):
                    act.wait_ge(h_made, f)
                act.activation(silu_g[:, :], g_ps[:, :], ACT.Silu).then_inc(silu_done, 1)
                if not_last(f):
                    act.wait_ge(landed["g"], f * 16 + 32)
                    hi_of("g", f + 1, flat(raw["g"]), g_done)

            act.wait_ge(landed["g"], 16)
            hi_of("g", 0, flat(raw["g"]), g_done)
            steps(act, step)
            hidden(FC - 1, (FC - 1) % 2)

        @block.vector
        def _(dve):
            def lo_of(k, f, source):
                dve.wait_ge(hi_ready[k], f + 1)
                dve.tensor_tensor(flat(lo[k]), source, flat(hi[k]).bitcast(F32), ALU.subtract).then_inc(split[k], 1)

            def hidden(f, parity):
                dve.wait_ge(landed["d"], f * 16 + 16)
                if after_first(f):
                    dve.wait_ge(split["d"], f)
                dve.tensor_tensor(wd_gated[:, :], flat(raw["d"]), gate[:, :], ALU.mult).then_inc(gated, 1)
                dve.wait_ge(u_done, f + 1)
                dve.wait_ge(silu_done, f + 1)
                if after_first(f):
                    dve.wait_ge(h_split, f)
                dve.tensor_tensor(h_f32[:, :], silu_g[:, :], u_ps[:, :], ALU.mult).then_inc(h_made, 1)
                lo_of("d", f, wd_gated[:, :])
                dve.wait_ge(h_hi_ready, f + 1)
                dve.tensor_tensor(h_lo[:, parity, :], h_f32[:, :], h_hi[:, parity, :].bitcast(F32),
                                  ALU.subtract).then_inc(h_split, 1)

            def add_down(f):
                for i in range(TT):
                    dve.wait_ge(y_done, f * TT + i + 1)
                    dve.tensor_tensor(x_sb[:, i, :], x_sb[:, i, :], y_ps[:, i % 2, :], ALU.add).then_inc(y_added, 1)

            def step(f, parity):
                lo_of("u", f, flat(raw["u"]))
                if after_first(f):
                    hidden(f - 1, 1 - parity)
                if not_last(f):
                    lo_of("g", f + 1, flat(raw["g"]))
                if after_first(f):
                    add_down(f - 1)

            dve.wait_ge(gate_in, 16)
            lo_of("g", 0, flat(raw["g"]))
            steps(dve, step)
            hidden(FC - 1, (FC - 1) % 2)
            add_down(FC - 1)

        @block.tensor
        def _(pe):
            def project(k, out, f, done):
                pe.wait_ge(split[k], f + 1)
                for c in range(DC):
                    for n, (w, u) in enumerate(((hi[k], u_hi), (hi[k], u_lo), (lo[k], u_hi))):
                        for h in range(2):
                            last = pe.matmul(out[:, h * HALF:(h + 1) * HALF], w[:, c, :], u[:, c, h * HALF:(h + 1) * HALF],
                                             start=(c == 0 and n == 0), stop=(c == DC - 1 and n == 2))
                last.then_inc(done, 1)

            def down(f, parity):
                pe.wait_ge(split["d"], f + 1)
                pe.wait_ge(h_split, f + 1)
                for i in range(TT):
                    if not (isinstance(f, int) and f == 0 and i < 2):
                        pe.wait_ge(y_added, f * TT + i - 1)
                    for n, (h, w) in enumerate(((h_hi, hi["d"]), (h_hi, lo["d"]), (h_lo, hi["d"]))):
                        for e in range(2):
                            last = pe.matmul(y_ps[:, i % 2, e * HALF:(e + 1) * HALF], h[:, parity, i * P:(i + 1) * P],
                                             flat(w)[:, e * HALF:(e + 1) * HALF], start=(n == 0), stop=(n == 2))
                    last.then_inc(y_done, 1)

            def step(f, parity):
                if after_first(f):
                    pe.wait_ge(silu_done, f)
                project("g", g_ps, f, g_done)
                if after_first(f):
                    pe.wait_ge(h_made, f)
                project("u", u_ps, f, u_done)
                if after_first(f):
                    down(f - 1, 1 - parity)

            steps(pe, step)
            down(FC - 1, (FC - 1) % 2)


def layer_norm(nc, stage, x_sb, g_dram, b_dram, out_dram=None):
    with Scope(nc, stage) as s:
        g_row = s.sb("g_row", [P, D])
        b_row = s.sb("b_row", [P, D])
        stats = s.sb("stats", [P, TT, 2, 6])
        mv = s.sb("mv", [P, TT, 2])
        std = s.sb("std", [P, TT])
        eps = s.sb("eps", [P, 1])
        rstd = s.sb("rstd", [P, TT])
        rows_in, eps_set, measured, rooted = s.sem("rows_in"), s.sem("eps_set"), s.sem("measured"), s.sem("rooted")
        step, scaled, shifted, stored = s.sem("step"), s.sem("scaled"), s.sem("shifted"), s.sem("stored")
        normed = s.sem("normed")
        block = s.block()

        @block.sync
        def _(sp):
            sp.dma_start(g_row[:, :], g_dram.to_broadcast([P, D])).then_inc(rows_in, 16)
            sp.dma_start(b_row[:, :], b_dram.to_broadcast([P, D])).then_inc(rows_in, 16)
            if out_dram is not None:
                for i in range(TT):
                    sp.wait_ge(shifted, i + 1)
                    sp.dma_start(out_dram[0, i * P:(i + 1) * P, :], x_sb[:, i, :]).then_inc(stored, 16)
                sp.wait_ge(stored, 16 * TT)

        @block.vector
        def _(dve):
            dve.memset(eps[:, :], EPS).then_inc(eps_set, 1)
            for i in range(TT):
                for h in range(2):
                    dve.bn_stats(stats[:, i, h, :], x_sb[:, i, h * HALF:(h + 1) * HALF]).then_inc(step, 1)
            for i in range(TT):
                dve.wait_ge(step, 2 * (i + 1))
                dve.bn_aggr(mv[:, i, :], stats[:, i, :, :].rearrange("p h s -> p (h s)")).then_inc(measured, 1)
            dve.wait_ge(rooted, 1)
            dve.reciprocal(rstd[:, :], std[:, :]).then_inc(step, 1)
            dve.wait_ge(step, 2 * TT + 1)
            for i in range(TT):
                dve.tensor_scalar(x_sb[:, i, :], x_sb[:, i, :], mv[:, i, 0:1], rstd[:, i:i + 1], ALU.subtract,
                                  ALU.mult).then_inc(normed, 1)
                if i == 0:
                    dve.wait_ge(rows_in, 32)
                dve.wait_ge(normed, i + 1)
                dve.tensor_tensor(x_sb[:, i, :], x_sb[:, i, :], g_row[:, :], ALU.mult).then_inc(scaled, 1)
                dve.wait_ge(scaled, i + 1)
                dve.tensor_tensor(x_sb[:, i, :], x_sb[:, i, :], b_row[:, :], ALU.add).then_inc(shifted, 1)

        @block.scalar
        def _(act):
            act.wait_ge(measured, TT)
            act.wait_ge(eps_set, 1)
            act.activation(std[:, :], mv[:, :, 1], ACT.Sqrt, bias=eps[:, 0:1]).then_inc(rooted, 1)


def project(nc, stage, w_dram, width, blocks, u_hi, u_lo, out, gate_dram=None, out_in=None):
    slots = 4
    with Scope(nc, stage) as s:
        raw = s.sb("w_raw", [P, slots, width])
        hi = s.sb("w_hi", [P, slots, width], F32R)
        lo = s.sb("w_lo", [P, slots, width], F32R)
        if gate_dram is not None:
            gate = s.sb("gate", [P, blocks * width])
        acc = s.ps("acc", [P, TT, HALF])
        landed = [s.sem(f"w_landed{k}") for k in range(slots)]
        gate_in, gated, hi_ready, split = s.sem("gate_in"), s.sem("gated"), s.sem("hi_ready"), s.sem("split")
        used, row_done, taken = s.sem("used"), s.sem("row_done"), s.sem("taken")
        block = s.block()
        src = w_dram.rearrange("(c p) n -> p c n", p=P)

        def wait_slot_used(eng, n, c):
            if c >= slots:
                eng.wait_ge(used, n * (DC - 1) + c - slots + 1)
            elif c == slots - 1:
                eng.wait_ge(row_done, n * TT)
            else:
                eng.wait_ge(used, (n - 1) * (DC - 1) + c + slots + 1)

        def steps(eng, one):
            one(0)
            with eng.Fori(1, blocks - 1) as n:
                one(n)
            one(blocks - 1)

        if blocks == 2:
            def steps(eng, one):
                one(0)
                one(1)

        later = lambda n, c: not isinstance(n, int) or n > 0 or c >= slots

        def per_block(split_chunk, take):
            def one(n):
                for c in range(slots, DC):
                    split_chunk(n, c)
                more = not isinstance(n, int) or n < blocks - 1
                if more:
                    for c in range(slots - 1):
                        split_chunk(n + 1, c)
                take(n)
                if more:
                    split_chunk(n + 1, slots - 1)
            return one

        @block.sync
        def _(sp):
            if gate_dram is not None:
                sp.dma_start(gate[:, :], gate_dram.to_broadcast([P, blocks * width])).then_inc(gate_in, 16)

            def load(n):
                for c in range(DC):
                    if later(n, c):
                        sp.wait_ge(split, n * DC + c - slots + 1)
                    at = src[:, c, bass.ds(n * width, width)]
                    sp.dma_start(raw[:, c % slots, :], at).then_inc(landed[c % slots], 16)

            steps(sp, load)

        @block.scalar
        def _(act):
            def make_hi(n, c):
                k = c % slots
                if gate_dram is None:
                    act.wait_ge(landed[k], (n * 2 + c // slots) * 16 + 16)
                else:
                    act.wait_ge(gated, n * DC + c + 1)
                if later(n, c):
                    wait_slot_used(act, n, c)
                act.activation(hi[:, k, :], raw[:, k, :], ACT.Copy).then_inc(hi_ready, 1)

            def take(n):
                if gate_dram is None:
                    for i in range(TT):
                        act.wait_ge(row_done, n * TT + i + 1)
                        act.activation(out[:, i, bass.ds(n * width, width)], acc[:, i, 0:width],
                                       ACT.Copy).then_inc(taken, 1)

            for c in range(slots):
                make_hi(0, c)
            steps(act, per_block(make_hi, take))

        @block.vector
        def _(dve):
            def make_lo(n, c):
                k = c % slots
                if gate_dram is not None:
                    dve.wait_ge(landed[k], (n * 2 + c // slots) * 16 + 16)
                    dve.tensor_tensor(raw[:, k, :], raw[:, k, :], gate[:, bass.ds(n * width, width)],
                                      ALU.mult).then_inc(gated, 1)
                dve.wait_ge(hi_ready, n * DC + c + 1)
                dve.tensor_tensor(lo[:, k, :], raw[:, k, :], hi[:, k, :].bitcast(F32), ALU.subtract).then_inc(split, 1)

            def take(n):
                if gate_dram is not None:
                    if n == 0:
                        dve.wait_ge(*out_in)
                    for i in range(TT):
                        dve.wait_ge(row_done, n * TT + i + 1)
                        at = out[:, i, bass.ds(n * width, width)]
                        dve.tensor_tensor(at, at, acc[:, i, 0:width], ALU.add).then_inc(taken, 1)

            if gate_dram is not None:
                dve.wait_ge(gate_in, 16)
            for c in range(slots):
                make_lo(0, c)
            steps(dve, per_block(make_lo, take))

        @block.tensor
        def _(pe):
            def one(n):
                for c in range(DC):
                    pe.wait_ge(split, n * DC + c + 1)
                    for i in range(TT):
                        if c == 0 and later(n, 0):
                            pe.wait_ge(taken, (n - 1) * TT + i + 1)
                        for m, (u, w) in enumerate(((u_hi, hi), (u_hi, lo), (u_lo, hi))):
                            last = pe.matmul(acc[:, i, 0:width], u[:, c, i * P:(i + 1) * P], w[:, c % slots, :],
                                             start=(c == 0 and m == 0), stop=(c == DC - 1 and m == 2))
                        if c == DC - 1:
                            last.then_inc(row_done, 1)
                    if c < DC - 1:
                        last.then_inc(used, 1)

            steps(pe, one)


def rope_rows(dve, at, heads, half, cos, sin, tmp, ticks):
    sem, n = ticks
    x1, x2 = at[:, :, 0:half], at[:, :, half:2 * half]
    wide = lambda table: table.unsqueeze(1).to_broadcast([P, heads, half])
    a, b, c, d = (tmp[:, k, 0:heads * half].rearrange("p (h j) -> p h j", j=half) for k in range(4))
    if n:
        dve.wait_ge(sem, n)
    dve.tensor_tensor(a, x1, wide(cos), ALU.mult).then_inc(sem, 1)
    dve.tensor_tensor(b, x2, wide(sin), ALU.mult).then_inc(sem, 1)
    dve.tensor_tensor(c, x2, wide(cos), ALU.mult).then_inc(sem, 1)
    dve.tensor_tensor(d, x1, wide(sin), ALU.mult).then_inc(sem, 1)
    dve.wait_ge(sem, n + 4)
    dve.tensor_tensor(x1, a, b, ALU.subtract).then_inc(sem, 1)
    dve.tensor_tensor(x2, c, d, ALU.add).then_inc(sem, 1)
    return sem, n + 6


def rope_sparse(nc, stage, h, table):
    with Scope(nc, stage) as s:
        tmp = s.sb("tmp", [P, 4, (HEADS + GROUPS) * ROPE_N // 2])
        ticks = s.sem("ticks")
        block = s.block()

        @block.vector
        def _(dve):
            count = (ticks, 0)
            half = ROPE_N // 2
            for i in range(TT):
                cos, sin = table[:, i, 0:half], table[:, i, half:2 * half]
                for col, heads in ((COL_Q, HEADS + GROUPS), (COL_KS, GROUPS), (COL_KW, GROUPS)):
                    at = h[:, i, col:col + heads * HD].rearrange("p (h d) -> p h d", d=HD)
                    count = rope_rows(dve, at, heads, half, cos, sin, tmp, count)
                half_m = ROPE_M // 2
                cos, sin = table[:, i, ROPE_N:ROPE_N + half_m], table[:, i, ROPE_N + half_m:ROPE_N + ROPE_M]
                at = h[:, i, COL_KR:COL_KR + ROPE_M].rearrange("p (h d) -> p h d", h=1)
                count = rope_rows(dve, at, 1, half_m, cos, sin, tmp, count)


def sparse_keys(nc, stage, h, ident, k_hi, k_lo, v, x2):
    with Scope(nc, stage) as s:
        tp = s.ps("tp", [P, 4, HALF])
        turned, hi_done, lo_done, moved = s.sem("turned"), s.sem("hi_done"), s.sem("lo_done"), s.sem("moved")
        v_hi_done = s.sem("v_hi_done")
        block = s.block()
        keys = [(br, half) for br in range(2) for half in range(2)]
        tokens = [(kv, half) for kv in range(2) for half in range(2)]
        col_k, col_v, col_c = (COL_KS, COL_KW), (COL_VS, COL_VW), (COL_KC, COL_VC)

        @block.tensor
        def _(pe):
            for n, (kind, half) in enumerate(keys + tokens):
                col = col_k[kind] if n < len(keys) else col_c[kind]
                if n >= 4:
                    pe.wait_ge(lo_done, 4 * (n - 3))
                for i in range(4):
                    t = pe.transpose(tp[:, n % 4, i * P:(i + 1) * P], h[:, 4 * half + i, col:col + P], ident[:, :])
                t.then_inc(turned, 1)

        @block.scalar
        def _(act):
            for n, (br, half) in enumerate(keys):
                act.wait_ge(turned, n + 1)
                for g in range(GROUPS):
                    for place in range(2):
                        act.activation(k_hi[place * HD:(place + 1) * HD, br, g, half * HALF:(half + 1) * HALF],
                                       tp[g * HD:(g + 1) * HD, n % 4, :], ACT.Copy).then_inc(hi_done, 1)
            for br in range(2):
                for g in range(GROUPS):
                    rows = h[:, :, col_v[br] + g * HD:col_v[br] + (g + 1) * HD]
                    act.activation(v[:, br, g, :, 0:HD], rows, ACT.Copy).then_inc(v_hi_done, 1)
            for n, (kv, half) in enumerate(tokens):
                act.wait_ge(turned, len(keys) + n + 1)
                for g in range(GROUPS):
                    for odd in range(2):
                        act.activation(x2[odd * HD:(odd + 1) * HD, kv, g, half * 256:(half + 1) * 256],
                                       tp[g * HD:(g + 1) * HD, n % 4, odd::2], ACT.Copy).then_inc(moved, 1)

        @block.vector
        def _(dve):
            for n, (br, half) in enumerate(keys):
                for g in range(GROUPS):
                    dve.wait_ge(hi_done, 4 * n + 2 * g + 2)
                    for place in range(2):
                        cols = slice(half * HALF, (half + 1) * HALF)
                        same = k_hi[g * HD:(g + 1) * HD, br, g, cols]
                        dve.tensor_tensor(k_lo[place * HD:(place + 1) * HD, br, g, cols], tp[g * HD:(g + 1) * HD, n % 4, :],
                                          same.bitcast(F32), ALU.subtract).then_inc(lo_done, 1)
            for n, (br, g) in enumerate((br, g) for br in range(2) for g in range(GROUPS)):
                dve.wait_ge(v_hi_done, n + 1)
                rows = h[:, :, col_v[br] + g * HD:col_v[br] + (g + 1) * HD]
                dve.tensor_tensor(v[:, br, g, :, HD:2 * HD], rows, v[:, br, g, :, 0:HD].bitcast(F32), ALU.subtract)


def compress(nc, stage, x2, pos, w1, w2, k_hi, k_lo, v):
    with Scope(nc, stage) as s:
        blocks = s.sb("blocks", [P, 2, CMP_PAIRS, GROUPS, CMP_PAD])
        w1_sb = s.sb("w1", [P, 2, CMP_PAIRS, CMP_HIDDEN])
        w2_sb = s.sb("w2", [P, 2, 2, P])
        pos_sb = s.sb("pos", [P, 2, CMP_PAIRS])
        hidden = s.sb("hidden", [P, 2, 2, GROUPS * CMP_PAD])
        hid_ps = s.ps("hid_ps", [P, 2, 2, HALF])
        out_ps = s.ps("out_ps", [P, 3, HALF])
        w_in, w2_in, pos_in, padded = s.sem("w_in"), s.sem("w2_in"), s.sem("pos_in"), s.sem("padded")
        placed, hid_done, gelu_done, out_done = s.sem("placed"), s.sem("hid_done"), s.sem("gelu_done"), s.sem("out_done")
        hi_done = s.sem("hi_done")
        block = s.block()

        @block.sync
        def _(sp):
            with nc.allow_non_contiguous_dma(reason="two small tables of positions with their dimension on partitions"):
                for kv in range(2):
                    sp.dma_start(pos_sb[:, kv, :], pos[kv][0].rearrange("(a j) d -> (j d) a", j=2)).then_inc(pos_in, 16)
            for kv in range(2):
                sp.dma_start(w1_sb[:, kv, :, :], w1[kv][0].rearrange("(a p) n -> p a n", p=P)).then_inc(w_in, 16)
                for twice in range(2):
                    sp.dma_start(w2_sb[:, kv, :, twice * HD:(twice + 1) * HD],
                                 w2[kv][0].rearrange("(m p) d -> p m d", p=P)).then_inc(w2_in, 16)

        @block.gpsimd
        def _(pool):
            pool.memset(blocks[:, :, :, :, N_CMP:CMP_PAD], 0.0).then_inc(padded, 1)

        @block.vector
        def _(dve):
            dve.wait_ge(pos_in, 32)
            for kv in range(2):
                for a in range(CMP_PAIRS):
                    tokens = x2[:, kv, :, a:a + 8 * (N_CMP - 1) + 1:8]
                    dve.tensor_scalar(blocks[:, kv, a, :, 0:N_CMP], tokens, pos_sb[:, kv, a:a + 1], None,
                                      ALU.add).then_inc(placed, 1)
            dve.wait_ge(hi_done, 1)
            keys = out_ps[:, 0, 0:GROUPS * CMP_PAD].rearrange("p (g n) -> p g n", g=GROUPS)
            dve.tensor_tensor(k_lo[:, :, :], keys, k_hi[:, :, :].bitcast(F32), ALU.subtract)
            for g in range(GROUPS):
                dve.wait_ge(hi_done, 2 + g)
                dve.tensor_tensor(v[0:CMP_PAD, g, HD:2 * HD], out_ps[0:CMP_PAD, 1 + g, 0:HD],
                                  v[0:CMP_PAD, g, 0:HD].bitcast(F32), ALU.subtract)

        @block.tensor
        def _(pe):
            pe.wait_ge(padded, 1)
            for kv in range(2):
                pe.wait_ge(w_in, 32)
                for m in range(2):
                    for a in range(CMP_PAIRS):
                        pe.wait_ge(placed, kv * CMP_PAIRS + a + 1)
                        last = pe.matmul(hid_ps[:, kv, m, 0:GROUPS * CMP_PAD], w1_sb[:, kv, a, m * P:(m + 1) * P],
                                         blocks[:, kv, a, :, :].rearrange("p g n -> p (g n)"),
                                         start=(a == 0), stop=(a == CMP_PAIRS - 1))
                    last.then_inc(hid_done, 1)
            pe.wait_ge(w2_in, 64)
            pe.wait_ge(gelu_done, 2)
            for m in range(2):
                last = pe.matmul(out_ps[:, 0, 0:GROUPS * CMP_PAD], w2_sb[:, 0, m, :], hidden[:, 0, m, :],
                                 start=(m == 0), stop=(m == 1))
            last.then_inc(out_done, 1)
            pe.wait_ge(gelu_done, 4)
            for g in range(GROUPS):
                for m in range(2):
                    last = pe.matmul(out_ps[0:CMP_PAD, 1 + g, 0:HD], hidden[:, 1, m, g * CMP_PAD:(g + 1) * CMP_PAD],
                                     w2_sb[:, 1, m, 0:HD], start=(m == 0), stop=(m == 1))
                last.then_inc(out_done, 1)

        @block.scalar
        def _(act):
            for n in range(4):
                kv, m = divmod(n, 2)
                act.wait_ge(hid_done, n + 1)
                act.activation(hidden[:, kv, m, :], hid_ps[:, kv, m, 0:GROUPS * CMP_PAD],
                               ACT.Gelu_apprx_tanh).then_inc(gelu_done, 1)
            act.wait_ge(out_done, 1)
            keys = out_ps[:, 0, 0:GROUPS * CMP_PAD].rearrange("p (g n) -> p g n", g=GROUPS)
            act.activation(k_hi[:, :, :], keys, ACT.Copy).then_inc(hi_done, 1)
            for g in range(GROUPS):
                act.wait_ge(out_done, 2 + g)
                act.activation(v[0:CMP_PAD, g, 0:HD], out_ps[0:CMP_PAD, 1 + g, 0:HD], ACT.Copy).then_inc(hi_done, 1)


def masks(nc, stage, ident, ident_r, causal, window, compressed):
    with Scope(nc, stage) as s:
        width = 2 * P + TT * CMP_PAD
        m = s.sb("m", [P, width])
        zeroed, cut, copied = s.sem("zeroed"), s.sem("cut"), s.sem("copied")
        block = s.block()

        @block.gpsimd
        def _(pool):
            pool.memset(m[:, :], 0.0).then_inc(zeroed, 1)
            pool.wait_ge(zeroed, 1)
            pool.affine_select(out=m[:, 0:P], in_=m[:, 0:P], compare_op=ALU.is_ge, fill=MASKED, base=0,
                               pattern=[[-1, P]], channel_multiplier=1).then_inc(cut, 1)
            pool.affine_select(out=m[:, P:2 * P], in_=m[:, P:2 * P], compare_op=ALU.is_gt, fill=MASKED, base=0,
                               pattern=[[1, P]], channel_multiplier=-1).then_inc(cut, 1)
            last = m[:, 2 * P:width].rearrange("p (i n) -> p i n", n=CMP_PAD)
            pool.affine_select(out=last, in_=last, compare_op=ALU.is_ge, fill=MASKED, base=1 - CMP_BLOCK,
                               pattern=[[P, TT], [-CMP_STRIDE, CMP_PAD]], channel_multiplier=1).then_inc(cut, 1)

        @block.vector
        def _(dve):
            dve.tensor_copy(ident_r[:, :], ident[:, :])
            dve.wait_ge(cut, 3)
            dve.tensor_copy(causal[:, :], m[:, 0:P])
            dve.tensor_copy(window[:, :], m[:, P:2 * P])
            dve.tensor_copy(compressed[:, :, :], m[:, 2 * P:width].rearrange("p (i n) -> p i n", n=CMP_PAD))


def latents(nc, stage, h, ident, q_norm, kv_norm, q_hi, q_lo, kv_hi, kv_lo):
    with Scope(nc, stage) as s:
        g_col = s.sb("g_col", [P, 5])
        square = s.sb("square", [P, Q_RANK])
        sums = s.sb("sums", [P, 2, TT])
        eps = s.sb("eps", [P, 1])
        root = s.sb("root", [P, 2, TT])
        rstd = s.sb("rstd", [P, 2, TT])
        u = s.sb("u", [P, 2, HALF])
        tp = s.ps("tp", [P, 4, HALF])
        g_in, eps_set, summed, rooted, inverted = (s.sem(x) for x in ("g_in", "eps_set", "summed", "rooted", "inverted"))
        scaled, turned, placed, hi_done, lo_done = (s.sem(x) for x in ("scaled", "turned", "placed", "hi_done", "lo_done"))
        block = s.block()
        sides = ((COL_CQ, Q_RANK), (COL_CKV, KV_RANK))
        units = [(n, c, half) for n in range(2) for c in range(sides[n][1] // P) for half in range(2)]

        @block.sync
        def _(sp):
            with nc.allow_non_contiguous_dma(reason="two norms' gains, one column each chunk"):
                sp.dma_start(g_col[:, 0:3], q_norm[0].rearrange("(c p) -> p c", p=P)).then_inc(g_in, 16)
                sp.dma_start(g_col[:, 3:5], kv_norm[0].rearrange("(c p) -> p c", p=P)).then_inc(g_in, 16)

        @block.scalar
        def _(act):
            count = 0
            for n, (col, rank) in enumerate(sides):
                for i in range(TT):
                    if count:
                        act.wait_ge(summed, count)
                    act.activation(square[:, 0:rank], h[:, i, col:col + rank], ACT.Square,
                                   accum_out=sums[:, n, i:i + 1]).then_inc(summed, 1)
                    count += 1
            act.wait_ge(summed, count)
            act.wait_ge(eps_set, 1)
            for n, (col, rank) in enumerate(sides):
                act.activation(root[:, n, :], sums[:, n, :], ACT.Sqrt, scale=1.0 / rank, bias=eps[:, 0:1]).then_inc(rooted, 1)
            act.wait_ge(g_in, 32)
            for m, (n, c, half) in enumerate(units):
                act.wait_ge(turned, m + 1)
                if m >= 2:
                    act.wait_ge(lo_done, m - 1)
                act.activation(u[:, m % 2, :], tp[:, m % 4, :], ACT.Copy, scale=g_col[:, 3 * n + c:3 * n + c + 1]).then_inc(placed, 1)

        @block.vector
        def _(dve):
            dve.memset(eps[:, :], EPS).then_inc(eps_set, 1)
            dve.wait_ge(rooted, 2)
            dve.reciprocal(rstd[:, :, :], root[:, :, :]).then_inc(inverted, 1)
            dve.wait_ge(inverted, 1)
            for n, (col, rank) in enumerate(sides):
                for i in range(TT):
                    at = h[:, i, col:col + rank]
                    dve.tensor_scalar(at, at, rstd[:, n, i:i + 1], None, ALU.mult).then_inc(scaled, 1)
            for m, (n, c, half) in enumerate(units):
                cols = slice(half * HALF, (half + 1) * HALF)
                hi, lo = ((q_hi, q_lo), (kv_hi, kv_lo))[n]
                dve.wait_ge(placed, m + 1)
                dve.tensor_copy(hi[:, c, cols], u[:, m % 2, :]).then_inc(hi_done, 1)
                dve.wait_ge(hi_done, m + 1)
                dve.tensor_tensor(lo[:, c, cols], u[:, m % 2, :], hi[:, c, cols].bitcast(F32), ALU.subtract).then_inc(lo_done, 1)

        @block.tensor
        def _(pe):
            pe.wait_ge(scaled, 2 * TT)
            for m, (n, c, half) in enumerate(units):
                if m >= 4:
                    pe.wait_ge(placed, m - 3)
                col = sides[n][0] + c * P
                for i in range(4):
                    t = pe.transpose(tp[:, m % 4, i * P:(i + 1) * P], h[:, 4 * half + i, col:col + P], ident[:, :])
                t.then_inc(turned, 1)


def latent_up(nc, stage, h, w_uq, w_ukv, q_hi, q_lo, kv_hi, kv_lo, ukv_hi, ukv_lo, v):
    with Scope(nc, stage) as s:
        half_q = HEADS * MD // 2
        uq_raw = s.sb("uq_raw", [P, 3, HEADS * MD])
        uq_hi = s.sb("uq_hi", [P, 3, HEADS * MD], F32R)
        uq_lo = s.sb("uq_lo", [P, 3, HEADS * MD], F32R)
        ukv_raw = s.sb("ukv_raw", [P, 2, HEADS * P])
        q_ps = s.ps("q_ps", [P, 4, HALF])
        v_ps = s.ps("v_ps", [P, 4, HALF])
        landed, hi_ready, split = s.sem("landed"), s.sem("hi_ready"), s.sem("split")
        v_done, v_hi_done, v_lo_done, q_done, q_taken = (s.sem(x) for x in ("v_done", "v_hi_done", "v_lo_done", "q_done", "q_taken"))
        block = s.block()
        parts = [(ukv_raw, ukv_hi, ukv_lo, 2), (uq_raw, uq_hi, uq_lo, 3)]

        @block.sync
        def _(sp):
            sp.dma_start(ukv_raw[:, :, :], w_ukv[0].rearrange("(c p) n -> p c n", p=P)).then_inc(landed, 16)
            sp.wait_ge(landed, 16)
            sp.dma_start(uq_raw[:, :, :], w_uq[0].rearrange("(c p) n -> p c n", p=P)).then_inc(landed, 16)

        @block.scalar
        def _(act):
            for m, (raw, hi, lo, chunks) in enumerate(parts):
                act.wait_ge(landed, 16 * (m + 1))
                for c in range(chunks):
                    act.activation(hi[:, c, :], raw[:, c, :], ACT.Copy).then_inc(hi_ready, 1)
            for i in range(TT):
                act.wait_ge(v_done, i + 1)
                act.activation(v[:, :, i, 0:HD], v_ps[:, i % 4, :].rearrange("p (h d) -> p h d", d=HD), ACT.Copy).then_inc(v_hi_done, 1)
            for n in range(2 * TT):
                i, e = divmod(n, 2)
                act.wait_ge(q_done, n + 1)
                at = h[:, i, COL_QM + e * half_q:COL_QM + (e + 1) * half_q]
                act.activation(at, q_ps[:, n % 4, 0:half_q], ACT.Copy, scale=MLA_SCALE).then_inc(q_taken, 1)

        @block.vector
        def _(dve):
            n = 0
            for raw, hi, lo, chunks in parts:
                for c in range(chunks):
                    n += 1
                    dve.wait_ge(hi_ready, n)
                    dve.tensor_tensor(lo[:, c, :], raw[:, c, :], hi[:, c, :].bitcast(F32), ALU.subtract).then_inc(split, 1)
            for i in range(TT):
                dve.wait_ge(v_hi_done, i + 1)
                dve.tensor_tensor(v[:, :, i, HD:2 * HD], v_ps[:, i % 4, :].rearrange("p (h d) -> p h d", d=HD),
                                  v[:, :, i, 0:HD].bitcast(F32), ALU.subtract).then_inc(v_lo_done, 1)

        @block.tensor
        def _(pe):
            pe.wait_ge(split, 2)
            for i in range(TT):
                if i >= 4:
                    pe.wait_ge(v_lo_done, i - 3)
                rows = slice(i * P, (i + 1) * P)
                for c in range(2):
                    for m, (a, w) in enumerate(((kv_hi, ukv_hi), (kv_hi, ukv_lo), (kv_lo, ukv_hi))):
                        values = w[:, c, :].rearrange("p (h d) -> p h d", d=P)[:, :, HD:2 * HD]
                        last = pe.matmul(v_ps[:, i % 4, :], a[:, c, rows], values, start=(c == 0 and m == 0), stop=(c == 1 and m == 2))
                last.then_inc(v_done, 1)
            pe.wait_ge(split, 5)
            for n in range(2 * TT):
                i, e = divmod(n, 2)
                if n >= 4:
                    pe.wait_ge(q_taken, n - 3)
                for c in range(3):
                    for m, (a, w) in enumerate(((q_hi, uq_hi), (q_hi, uq_lo), (q_lo, uq_hi))):
                        last = pe.matmul(q_ps[:, n % 4, 0:half_q], a[:, c, i * P:(i + 1) * P],
                                         w[:, c, e * half_q:(e + 1) * half_q], start=(c == 0 and m == 0), stop=(c == 2 and m == 2))
                last.then_inc(q_done, 1)


def rope_latent(nc, stage, h, table):
    with Scope(nc, stage) as s:
        half = ROPE_M // 2
        tmp = s.sb("tmp", [P, 4, HEADS * half])
        ticks = s.sem("ticks")
        block = s.block()

        @block.vector
        def _(dve):
            count = (ticks, 0)
            for i in range(TT):
                cos, sin = table[:, i, ROPE_N:ROPE_N + half], table[:, i, ROPE_N + half:ROPE_N + 2 * half]
                at = h[:, i, COL_QM:COL_QM + HEADS * MD].rearrange("p (h d) -> p h d", d=MD)[:, :, HD:MD]
                count = rope_rows(dve, at, HEADS, half, cos, sin, tmp, count)


RING = 3
LAG = 2
SUMS = 8


class Unit:

    def __init__(self, blocks, keys, first_row, key_of, widths, mask_of, value_of, out, adds, gate, before):
        self.blocks = blocks
        self.keys = keys
        self.first_row = first_row
        self.key_of = key_of
        self.widths = widths
        self.mask_of = mask_of
        self.value_of = value_of
        self.out = out
        self.adds = adds
        self.gate = gate
        self.before = before
        self.together = 4 if max(widths) <= T // 4 else 2 if max(widths) <= T // 2 else 1

    def columns(self, row, width=None):
        at = row % self.together * (T // self.together)
        return slice(at, at + (self.widths[row] if width is None else width))


def attend(nc, stage, units, staging, ident, ident_r, slots, lead, burst):
    steps = []
    scoring = [x for n, u in enumerate(units) for x in
               [("stage", n, y) for y in u.before] + [("score", n, r) for r in range(0, 4, u.together)]]
    turned = []
    scored_columns = turned_columns = 0

    def score_next():
        kind, n, r = step = scoring.pop(0)
        steps.append(step)
        return sum(units[n].widths[r:r + units[n].together]) if kind == "score" else 0

    def apply_next():
        n, k = turned.pop(0)
        if k == 0 and n:
            steps.append(("finish", n - 1, 0))
        steps.append(("apply", n, k))

    for n, u in enumerate(units):
        for k, block in enumerate(u.blocks):
            free = burst
            while scoring and (scoring[0][1] <= n or free > 0 and scoring[0][1] < n + slots
                               and scored_columns < turned_columns + lead):
                free -= scoring[0][0] == "score"
                scored_columns += score_next()
            steps.append(("turn", n, k))
            turned_columns += (4 - u.first_row(block)) * u.keys
            turned.append((n, k))
            if len(turned) > LAG:
                apply_next()
    while turned:
        apply_next()
    steps.append(("finish", len(units) - 1, 0))

    act_steps, held = [], []
    for step in steps:
        if step[0] == "score":
            if len(held) == 2:
                act_steps.append(held.pop(0))
            held.append(step)
            continue
        if step[0] == "turn":
            while held and held[0][1] <= step[1]:
                act_steps.append(held.pop(0))
        act_steps.append(step)
        if step[0] == "turn":
            act_steps += held
            held = []
    assert not held

    ring_no = {x: m for m, x in enumerate(x for x in steps if x[0] in ("turn", "stage", "finish"))}
    hi_no = {x: m for m, x in enumerate(x for x in steps if x[0] in ("turn", "stage"))}
    turn_no = {x: m for m, x in enumerate(x for x in steps if x[0] == "turn")}
    score_no = {x: m for m, x in enumerate(x for x in steps if x[0] == "score")}
    last_score = {x[1]: m for x, m in score_no.items()}

    with Scope(nc, stage) as s:
        exps = s.sb("exps", [P, slots, 4, T])
        sums = s.sb("sums", [P, SUMS, 4])
        neg_max = s.sb("neg_max", [P, SUMS, 4])
        turned_hi = s.sb("turned_hi", [P, RING, HALF], F32R)
        turned_lo = s.sb("turned_lo", [P, RING, HALF], F32R)
        out_sb = s.sb("out_sb", [P, 4, P])
        floor = s.sb("floor", [P, 2, 4])
        factor = s.sb("factor", [P, 2, 4])
        factor_g = s.sb("factor_g", [P, 2, 4])
        joined = s.sb("joined", [P, 2, 4, HD])
        scores = s.ps("scores", [P, 2, T])
        ring = s.ps("ring", [P, RING, HALF])
        out_ps = s.ps("out_ps", [P, HALF])
        scored, maxed, exped, guarded = s.sem("scored"), s.sem("maxed"), s.sem("exped"), s.sem("guarded")
        ring_full, hi_done, ring_free = s.sem("ring_full"), s.sem("hi_done"), s.sem("ring_free")
        applied, out_moved = s.sem("applied"), s.sem("out_moved")
        tail, fin, factored, weighed = s.sem("tail"), s.sem("fin"), s.sem("factored"), s.sem("weighed")
        block = s.block()
        bank_of = lambda step: ring[:, ring_no[step] % RING, :] if step in ring_no else None

        @block.tensor
        def _(pe):
            for step in steps:
                kind, n, k = step
                u = units[n]
                bank = bank_of(step)
                if step in ring_no and ring_no[step] >= RING:
                    pe.wait_ge(ring_free, ring_no[step] - RING + 1)
                if kind == "stage":
                    staging.pe(pe, k, bank).then_inc(ring_full, 1)
                elif kind == "score":
                    m = score_no[step]
                    pe.wait_ge(ring_free, ring_no[[x for x in steps if x[0] == "stage" and x[1] <= n][-1]] + 1)
                    if m >= 2:
                        pe.wait_ge(exped, m - 1)
                    for r in range(k, k + u.together):
                        w = u.widths[r]
                        own = scores[:, m % 2, u.columns(r)]
                        for c0 in range(0, w, HALF):
                            c1 = min(c0 + HALF, w)
                            products = u.key_of(r, c0, c1 - c0)
                            for p, (q, key) in enumerate(products):
                                last = pe.matmul(own[:, c0:c1], q, key, start=(p == 0), stop=(p == len(products) - 1))
                                if p == 0:
                                    for at, mask in u.mask_of(r):
                                        if c0 <= at < c1:
                                            pe.matmul(own[:, at:at + u.keys], ident_r[:, :], mask, start=False, stop=False)
                    last.then_inc(scored, 1)
                elif kind == "turn":
                    j = turn_no[step]
                    first = u.first_row(u.blocks[k])
                    pe.wait_ge(exped, last_score[n] + 1)
                    for r in range(first, 4):
                        last = pe.transpose(bank[0:u.keys, r * P:(r + 1) * P],
                                            exps[:, n % slots, r, k * u.keys:(k + 1) * u.keys], ident[:, :])
                    last.then_inc(ring_full, 1)
                elif kind == "apply":
                    j = turn_no[("turn", n, k)]
                    cols = slice(u.first_row(u.blocks[k]) * P, HALF)
                    pe.wait_ge(ring_free, ring_no[("turn", n, k)] + 1)
                    if k == 0 and n:
                        pe.wait_ge(out_moved, n)
                    for m, part in enumerate((turned_hi, turned_lo)):
                        last = pe.matmul(out_ps[:, cols], u.value_of(u.blocks[k]), part[0:u.keys, j % RING, cols],
                                         start=(k == 0 and m == 0), stop=(k == len(u.blocks) - 1 and m == 1))
                    last.then_inc(applied, 1)
                else:
                    pe.wait_ge(out_moved, n + 1)
                    for r in range(4):
                        last = pe.transpose(bank[:, r * P:(r + 1) * P], out_sb[:, r, :], ident[:, :])
                    last.then_inc(ring_full, 1)

        @block.scalar
        def _(act):
            for step in act_steps:
                kind, n, k = step
                u = units[n]
                bank = bank_of(step)
                if kind == "stage":
                    act.wait_ge(ring_full, ring_no[step] + 1)
                    staging.act(act, k, bank).then_inc(hi_done, 1)
                elif kind == "score":
                    m = score_no[step]
                    act.wait_ge(maxed, m + 1)
                    for r in range(k, k + u.together):
                        made = act.activation(exps[:, n % slots, r, 0:u.widths[r]], scores[:, m % 2, u.columns(r)], ACT.Exp,
                                              bias=neg_max[:, n % SUMS, r:r + 1], accum_out=sums[:, n % SUMS, r:r + 1])
                    made.then_inc(exped, 1)
                elif kind == "turn":
                    j = turn_no[step]
                    cols = slice(u.first_row(u.blocks[k]) * P, HALF)
                    act.wait_ge(ring_full, ring_no[step] + 1)
                    if j >= RING:
                        act.wait_ge(applied, j - RING + 1)
                    act.activation(turned_hi[0:u.keys, j % RING, cols], bank[0:u.keys, cols], ACT.Copy).then_inc(hi_done, 1)
                elif kind == "apply" and k == len(u.blocks) - 1:
                    act.wait_ge(applied, turn_no[("turn", n, k)] + 1)
                    act.activation(out_sb[:, :, :].rearrange("p r c -> p (r c)"), out_ps[:, :], ACT.Copy).then_inc(out_moved, 1)

        @block.vector
        def _(dve):
            guards = 0
            for step in steps:
                kind, n, k = step
                u = units[n]
                bank = bank_of(step)
                if kind == "stage":
                    dve.wait_ge(hi_done, hi_no[step] + 1)
                    staging.dve(dve, k, bank).then_inc(ring_free, 1)
                elif kind == "score":
                    m = score_no[step]
                    dve.wait_ge(scored, m + 1)
                    at = neg_max[:, n % SUMS, k:k + u.together]
                    if min(u.widths) == max(u.widths):
                        rows = scores[:, m % 2, :].rearrange("p (r c) -> p r c", r=u.together)[:, :, 0:u.widths[0]]
                        top = dve.reduce_max(at, rows, AX, negate=True)
                    else:
                        for r in range(k, k + u.together):
                            top = dve.reduce_max(neg_max[:, n % SUMS, r:r + 1], scores[:, m % 2, u.columns(r)], AX, negate=True)
                    if u.keys == CMP_PAD:
                        top.then_inc(guarded, 1)
                        guards += 1
                        dve.wait_ge(guarded, guards)
                        top = dve.tensor_scalar(at, at, -NO_KEY, None, ALU.min)
                    top.then_inc(maxed, 1)
                elif kind == "turn":
                    j = turn_no[step]
                    cols = slice(u.first_row(u.blocks[k]) * P, HALF)
                    dve.wait_ge(hi_done, hi_no[step] + 1)
                    dve.tensor_tensor(turned_lo[0:u.keys, j % RING, cols], bank[0:u.keys, cols],
                                      turned_hi[0:u.keys, j % RING, cols].bitcast(F32), ALU.subtract).then_inc(ring_free, 1)
                elif kind == "finish":
                    b = n % 2
                    dve.tensor_scalar(floor[:, b, :], sums[:, n % SUMS, :], 1e-30, None, ALU.max).then_inc(tail, 1)
                    dve.wait_ge(tail, n + 1)
                    if n >= 2:
                        dve.wait_ge(fin, n - 1)
                    dve.reciprocal(factor[:, b, :], floor[:, b, :]).then_inc(factored, 1)
                    dve.wait_ge(ring_full, ring_no[step] + 1)
                    parts = bank[:, :].rearrange("p (r a d) -> p r d a", a=2, d=HD)
                    dve.tensor_reduce(joined[:, b, :, :], parts, AX, ALU.add).then_inc(ring_free, 1)

        @block.gpsimd
        def _(pool):
            gated = added = 0
            for step in steps:
                kind, n, k = step
                if kind != "finish":
                    continue
                u, b = units[n], n % 2
                pool.wait_ge(factored, n + 1)
                by = factor
                if u.gate is not None:
                    pool.tensor_tensor(factor_g[:, b, :], factor[:, b, :], u.gate, ALU.mult).then_inc(weighed, 1)
                    gated += 1
                    by = factor_g
                pool.wait_ge(ring_free, ring_no[step] + 1)
                if gated + added:
                    pool.wait_ge(weighed, gated + added)
                wide = by[:, b, :].unsqueeze(2).to_broadcast([P, 4, HD])
                if u.adds:
                    pool.tensor_tensor(joined[:, b, :, :], joined[:, b, :, :], wide, ALU.mult).then_inc(weighed, 1)
                    added += 1
                    pool.wait_ge(weighed, gated + added)
                    pool.tensor_tensor(u.out, u.out, joined[:, b, :, :], ALU.add).then_inc(fin, 1)
                else:
                    pool.tensor_tensor(u.out, joined[:, b, :, :], wide, ALU.mult).then_inc(fin, 1)


def sparse_attention(nc, stage, h, k_hi, k_lo, v, kc_hi, kc_lo, vc, gates, ident, ident_r, causal, window, compressed):
    with Scope(nc, stage) as s:
        q = s.sb("q", [P, 2, HPG, P], F32R)

        class Staging:

            def places(self, t, side):
                for odd in range(2):
                    own, other = slice(odd * HD, (odd + 1) * HD), slice((1 - odd) * HD, (2 - odd) * HD)
                    rows = side[own, 0:2 * P].rearrange("p (a n) -> p a n", a=2)
                    yield rows, q[own, t % 2, odd::2, :], q[other, t % 2, odd::2, :]

            def pe(self, pe, t, side):
                g, i = divmod(t, TT)
                for pair in range(2):
                    col = COL_Q + (g * HPG + 2 * pair) * HD
                    last = pe.transpose(side[:, pair * P:(pair + 1) * P], h[:, i, col:col + P], ident[:, :])
                return last

            def act(self, act, t, side):
                for rows, hi, lo in self.places(t, side):
                    last = act.activation(hi, rows, ACT.Copy, scale=NSA_SCALE)
                return last

            def dve(self, dve, t, side):
                for rows, hi, lo in self.places(t, side):
                    last = dve.scalar_tensor_tensor(out=lo, in0=rows, scalar=NSA_SCALE, in1=hi.bitcast(F32),
                                                    op0=ALU.mult, op1=ALU.subtract)
                return last

        def unit(g, i, branch):
            col = COL_Q + g * HPG * HD
            out = h[:, i, col:col + HPG * HD].rearrange("p (r d) -> p r d", d=HD)
            gate = gates[:, i, g * HPG * 3 + (1, 2, 0)[branch]:(g + 1) * HPG * 3:3]
            at = (g * TT + i) % 2
            if branch == 2:
                blocks, keys, base = [0], CMP_PAD, 0
                kh, kl = kc_hi[:, g, :], kc_lo[:, g, :]
                mask = [(0, compressed[:, i, :])]
                value = lambda j: vc[0:CMP_PAD, g, :]
            else:
                blocks = list(range(max(0, i - WINDOW_BLOCKS) if branch == 1 else 0, i + 1))
                keys, base = P, blocks[0] * P
                kh, kl = k_hi[:, branch, g, :], k_lo[:, branch, g, :]
                mask = [((len(blocks) - 1) * P, causal[:, :])]
                if branch == 1 and i >= WINDOW_BLOCKS:
                    mask.append((0, window[:, :]))
                value = lambda j: v[:, branch, g, j, :]

            def key_of(r, c0, w):
                return [(q[:, at, r, :], k[:, base + c0:base + c0 + w]) for k in (kh, kl)]

            return Unit(blocks, keys, lambda j: 0, key_of, [len(blocks) * keys] * 4, lambda r: mask, value, out,
                        branch > 0, gate, [g * TT + i] if branch == 0 else [])

        units = [unit(g, i, b) for g in range(GROUPS) for i in range(TT) for b in range(3)]
        attend(nc, stage + "a", units, Staging(), ident, ident_r, 3, lead=6 * T, burst=1)


def latent_attention(nc, stage, h, kv_hi, kv_lo, ukv_hi, ukv_lo, v, ident, ident_r, causal):
    with Scope(nc, stage) as s:
        k_hi = s.sb("k_hi", [P, 2, T], F32R)
        k_lo = s.sb("k_lo", [P, 2, T], F32R)
        q_hi = s.sb("q_hi", [P, 2, HALF], F32R)
        q_lo = s.sb("q_lo", [P, 2, HALF], F32R)

        class Staging:

            def pe(self, pe, what, side):
                if what[0] == "k":
                    _, head, half = what
                    for c in range(2):
                        for m, (w, a) in enumerate(((ukv_hi, kv_hi), (ukv_hi, kv_lo), (ukv_lo, kv_hi))):
                            last = pe.matmul(side[:, :], w[:, c, head * P:(head + 1) * P], a[:, c, half * HALF:(half + 1) * HALF],
                                             start=(c == 0 and m == 0), stop=(c == 1 and m == 2))
                    return last
                for r in range(4):
                    if what[0] == "q":
                        _, head, half = what
                        rows = h[:, 4 * half + r, COL_QM + head * MD:COL_QM + (head + 1) * MD]
                    else:
                        rows = h[:, 4 * what[1] + r, COL_KR - HD:COL_KR + ROPE_M]
                    last = pe.transpose(side[0:MD, r * P:(r + 1) * P], rows, ident[:, :])
                return last

            def places(self, what, side):
                if what[0] == "q":
                    _, head, half = what
                    return [(side[0:MD, :], q_hi[0:MD, half, :], q_lo[0:MD, half, :])]
                cols = slice(what[-1] * HALF, (what[-1] + 1) * HALF)
                if what[0] == "k":
                    b = what[1] % 2
                    return [(side[0:HD, :], k_hi[0:HD, b, cols], k_lo[0:HD, b, cols])]
                return [(side[HD:MD, :], k_hi[HD:MD, b, cols], k_lo[HD:MD, b, cols]) for b in range(2)]

            def act(self, act, what, side):
                for rows, hi, lo in self.places(what, side):
                    last = act.activation(hi, rows, ACT.Copy)
                return last

            def dve(self, dve, what, side):
                for rows, hi, lo in self.places(what, side):
                    last = dve.tensor_tensor(lo, rows, hi.bitcast(F32), ALU.subtract)
                return last

        def unit(head, half):
            blocks = list(range(4 * half + 4))
            b = head % 2
            col = COL_QM + head * HD
            out = h[:, 4 * half:4 * half + 4, col:col + HD]

            def key_of(r, c0, w):
                rows = slice(r * P, (r + 1) * P)
                hi, lo = q_hi[0:MD, half, rows], q_lo[0:MD, half, rows]
                return [(hi, k_hi[0:MD, b, c0:c0 + w]), (hi, k_lo[0:MD, b, c0:c0 + w]), (lo, k_hi[0:MD, b, c0:c0 + w])]

            before = [("k", head, half), ("q", head, half)]
            if head == 0:
                before = [("r", half)] + before
            widths = [(4 * half + r + 1) * P for r in range(4)]
            return Unit(blocks, P, lambda j: max(0, j - 4 * half), key_of, widths,
                        lambda r: [((4 * half + r) * P, causal[:, :])], lambda j: v[:, head, j, :], out, False, None, before)

        units = [unit(head, half) for head in range(HEADS) for half in range(2)]
        attend(nc, stage + "a", units, Staging(), ident, ident_r, 2, lead=3 * T, burst=2)


def load_rows(nc, stage, pairs):
    with Scope(nc, stage) as s:
        landed = s.sem("landed")
        block = s.block()

        @block.sync
        def _(sp):
            for place, rows in pairs:
                sp.dma_start(place, rows.rearrange("(i p) d -> p i d", p=P)).then_inc(landed, 16)
            sp.wait_ge(landed, 16 * len(pairs))


def sigmoid_gates(nc, stage, h, gates):
    with Scope(nc, stage) as s:
        block = s.block()

        @block.scalar
        def _(act):
            act.activation(gates[:, :, :], h[:, :, COL_GATE:COL_GATE + N_GATE], ACT.Sigmoid)


def spilled(nc, stage, sem, count):
    with Scope(nc, stage) as s:
        block = s.block()

        @block.sync
        def _(sp):
            sp.wait_ge(sem, count)


def clear_semaphores(nc):
    nc.clear_and_free_semaphores(Scope.finished)
    nc.all_engine_barrier()
    Scope.finished = []


def layer(nc, x, c, w_ada, b_ada, ln_g, ln_b, ffn1_wg, ffn1_wu, ffn1_wd, w_in, cmp_k_pos, cmp_k_w1, cmp_k_w2,
          cmp_v_pos, cmp_v_w1, cmp_v_w2, mla_q_norm, mla_kv_norm, mla_w_uq, mla_w_ukv, w_out, ffn2_wg, ffn2_wu,
          ffn2_wd, rope_table, out):
    Scope.finished = []
    gate_dram = nc.dram_tensor("gate_rows", [3, D], F32, kind="Internal").ap()
    x_dram = nc.dram_tensor("x_rows", [T, D], F32, kind="Internal").ap()
    norm_rows = lambda n: (ln_g[0, n:n + 1, :], ln_b[0, n:n + 1, :])
    with Scope(nc, "all") as a:
        ident = a.sb("ident", [P, P])
        ones = a.sb("ones", [P, P])
        ident_r = a.sb("ident_r", [P, P], F32R)
        causal = a.sb("causal", [P, P], F32R)
        window = a.sb("window", [P, P], F32R)
        compressed = a.sb("compressed", [P, TT, CMP_PAD], F32R)
        table = a.sb("table", [P, TT, ROPE_N + ROPE_M])
        gates = a.sb("gates", [P, TT, N_GATE])
        shift = a.sb("shift", [P, 3, DC])
        scale = a.sb("scale", [P, 3, DC])
        x_out = a.sem("x_out")
        constants(nc, ident, ones)
        masks(nc, "masks", ident, ident_r, causal, window, compressed)
        load_rows(nc, "tables", [(table[:, :, :], rope_table)])

        with ExitStack() as h_alive:
            with Scope(nc, "mix_in", side="right") as r:
                x_sb = r.sb("x", [P, TT, D])
                modulation(nc, c, w_ada, b_ada, x, ones, x_sb, shift, scale, gate_dram)
                u_hi = r.sb("u_hi", [P, DC, T], F32R)
                u_lo = r.sb("u_lo", [P, DC, T], F32R)
                modulated_transpose(nc, "turn1", x_sb, shift[:, 0, :], scale[:, 0, :], ident, u_hi, u_lo)
                swiglu(nc, "ffn1", ffn1_wg, ffn1_wu, ffn1_wd, gate_dram[0:1, :], x_sb, u_hi, u_lo)
                layer_norm(nc, "norm1", x_sb, *norm_rows(0))
                modulated_transpose(nc, "turn2", x_sb, shift[:, 1, :], scale[:, 1, :], ident, u_hi, u_lo, (x_dram, x_out))
                h = h_alive.enter_context(Scope(nc, "h")).sb("h", [P, TT, D_IN])
                project(nc, "in", w_in[0], D_IN // 4, 4, u_hi, u_lo, h)
                spilled(nc, "x_kept", x_out, 16 * TT)

            clear_semaphores(nc)
            rope_sparse(nc, "rope1", h, table)
            sigmoid_gates(nc, "gates", h, gates)
            with Scope(nc, "sparse") as b:
                k_hi = b.sb("k_hi", [P, 2, GROUPS, T], F32R)
                k_lo = b.sb("k_lo", [P, 2, GROUPS, T], F32R)
                v = b.sb("v", [P, 2, GROUPS, TT, P], F32R)
                kc_hi = b.sb("kc_hi", [P, GROUPS, CMP_PAD], F32R)
                kc_lo = b.sb("kc_lo", [P, GROUPS, CMP_PAD], F32R)
                vc = b.sb("vc", [P, GROUPS, P], F32R)
                with Scope(nc, "compress") as t:
                    x2 = t.sb("x2", [P, 2, GROUPS, HALF])
                    sparse_keys(nc, "keys", h, ident, k_hi, k_lo, v, x2)
                    compress(nc, "cmp", x2, (cmp_k_pos, cmp_v_pos), (cmp_k_w1, cmp_v_w1), (cmp_k_w2, cmp_v_w2),
                             kc_hi, kc_lo, vc)
                sparse_attention(nc, "nsa", h, k_hi, k_lo, v, kc_hi, kc_lo, vc, gates, ident, ident_r, causal, window,
                                 compressed)
            with Scope(nc, "latent") as b:
                kv_hi = b.sb("kv_hi", [P, 2, T], F32R)
                kv_lo = b.sb("kv_lo", [P, 2, T], F32R)
                ukv_hi = b.sb("ukv_hi", [P, 2, HEADS * P], F32R)
                ukv_lo = b.sb("ukv_lo", [P, 2, HEADS * P], F32R)
                v = b.sb("v", [P, HEADS, TT, P], F32R)
                with Scope(nc, "queries") as t:
                    q_hi = t.sb("q_hi", [P, 3, T], F32R)
                    q_lo = t.sb("q_lo", [P, 3, T], F32R)
                    latents(nc, "rms", h, ident, mla_q_norm, mla_kv_norm, q_hi, q_lo, kv_hi, kv_lo)
                    latent_up(nc, "up", h, mla_w_uq, mla_w_ukv, q_hi, q_lo, kv_hi, kv_lo, ukv_hi, ukv_lo, v)
                rope_latent(nc, "rope2", h, table)
                latent_attention(nc, "mla", h, kv_hi, kv_lo, ukv_hi, ukv_lo, v, ident, ident_r, causal)

            clear_semaphores(nc)
            r = Scope(nc, "mix_out", side="right")
            r.__enter__()
            x_sb = r.sb("x", [P, TT, D])
            u_hi = r.sb("u_hi", [P, DC, T], F32R)
            u_lo = r.sb("u_lo", [P, DC, T], F32R)
            x_back = r.sem("x_back")
            modulated_transpose(nc, "turn3", h, None, None, ident, u_hi, u_lo, reload=(x_sb, x_dram, x_back))
        project(nc, "out", w_out[0], HALF, 2, u_hi, u_lo, x_sb, gate_dram[1:2, :], (x_back, 16 * TT))
        layer_norm(nc, "norm2", x_sb, *norm_rows(1))
        modulated_transpose(nc, "turn4", x_sb, shift[:, 2, :], scale[:, 2, :], ident, u_hi, u_lo)
        swiglu(nc, "ffn2", ffn2_wg, ffn2_wu, ffn2_wd, gate_dram[2:3, :], x_sb, u_hi, u_lo)
        layer_norm(nc, "norm3", x_sb, *norm_rows(2), out)
        r.__exit__(None, None, None)


INPUTS = ("x", "c", "w_ada", "b_ada", "ln_g", "ln_b", "ffn1_wg", "ffn1_wu", "ffn1_wd", "w_in", "cmp_k_pos", "cmp_k_w1",
          "cmp_k_w2", "cmp_v_pos", "cmp_v_w1", "cmp_v_w2", "mla_q_norm", "mla_kv_norm", "mla_w_uq", "mla_w_ukv",
          "w_out", "ffn2_wg", "ffn2_wu", "ffn2_wd")


def rope_rows_table():
    import numpy as np

    parts = []
    for width in (ROPE_N, ROPE_M):
        half = width // 2
        inverse = np.float32(ROPE_THETA) ** (-np.arange(half, dtype=np.float32) / np.float32(half))
        angle = np.arange(T, dtype=np.float32)[:, None] * inverse[None, :]
        parts += [np.cos(angle), np.sin(angle)]
    return np.concatenate(parts, axis=1).astype(np.float32)


def kernel(**inputs):
    import numpy as np
    import concourse.bacc as bacc
    from concourse.bass_utils import run_bass_kernel_spmd

    nc = bacc.Bacc("TRN2", target_bir_lowering=False, num_devices=1)
    arrays = {f"in_{name}": np.ascontiguousarray(inputs[name]) for name in INPUTS}
    arrays["in_rope_table"] = rope_rows_table()
    args = [nc.dram_tensor(name, a.shape, mybir.dt.from_np(a.dtype), kind="ExternalInput").ap() for name, a in arrays.items()]
    out = nc.dram_tensor("out_x", (1, T, D), F32, kind="ExternalOutput").ap()
    layer(nc, *args, out)
    result = run_bass_kernel_spmd(nc, [arrays], core_ids=[0])
    return result.results[0]["out_x"]
```

```python
from contextlib import ExitStack

import concourse.bass as bass
from concourse import mybir

F32 = mybir.dt.float32
F32R = mybir.dt.float32r
ALU = mybir.AluOpType
ACT = mybir.ActivationFunctionType
AX = mybir.AxisListType.X

P = 128
HALF = 512
T = 1024
D = 1024
TT = T // P
DC = D // P
D_FF = 2816
FC = D_FF // P
N_MOD = 9
EARLY = 2
LATE = N_MOD - EARLY
ALPHA = 2.0 ** 0.25
EPS = 1e-5

HD = 64
HEADS = 8
GROUPS = 2
HPG = HEADS // GROUPS
COL_Q = 0
COL_KC, COL_VC, COL_KS, COL_VS, COL_KW, COL_VW = (HEADS * HD + n * GROUPS * HD for n in range(6))
COL_GATE = COL_VW + GROUPS * HD
N_GATE = 3 * HEADS
Q_RANK = 384
KV_RANK = 256
COL_CQ = COL_GATE + N_GATE
COL_CKV = COL_CQ + Q_RANK
COL_KR = COL_CKV + KV_RANK
ROPE_N = 16
ROPE_M = 32
D_IN = COL_KR + ROPE_M
LATENTS = ((COL_CQ, Q_RANK), (COL_CKV, KV_RANK))
MD = HD + ROPE_M
COL_QM = HEADS * HD
NSA_SCALE = HD ** -0.5
MLA_SCALE = MD ** -0.5
ROPE_THETA = 500000.0

N_CMP = 63
CMP_PAD = 64
CMP_STRIDE = 16
CMP_BLOCK = 32
CMP_PAIRS = CMP_BLOCK // 2
CMP_HIDDEN = 4 * HD
WINDOW_BLOCKS = 4
MASKED = -1e30
NO_KEY = -1e20


class Scope:

    finished = []

    def __init__(self, nc, stage, side="left"):
        self.nc, self.stage, self.side, self.stack, self.sems = nc, stage, side, ExitStack(), []

    def __enter__(self):
        self.stack.__enter__()
        return self

    def __exit__(self, *a):
        Scope.finished += self.sems
        return self.stack.__exit__(*a)

    def sb(self, name, shape, dt=F32):
        return self.stack.enter_context(self.nc.sbuf_tensor(f"{self.stage}_{name}", shape, dt, side=self.side))

    def ps(self, name, shape):
        return self.stack.enter_context(self.nc.psum_tensor(f"{self.stage}_{name}", shape, F32))

    def sem(self, name):
        self.sems.append(self.nc.alloc_semaphore(f"{self.stage}_{name}"))
        return self.sems[-1]

    def block(self):
        return self.stack.enter_context(self.nc.Block())


def constants(nc, ident, ones):
    with Scope(nc, "const") as s:
        filled = s.sem("filled")
        block = s.block()

        @block.gpsimd
        def _(pool):
            pool.memset(ones[:, :], 1.0)
            pool.memset(ident[:, :], 0.0).then_inc(filled, 1)
            pool.wait_ge(filled, 1)
            pool.affine_select(out=ident[:, :], in_=ident[:, :], compare_op=ALU.not_equal, fill=1.0,
                               base=0, pattern=[[-1, P]], channel_multiplier=1)


def column_sums(pe, ones, part, vectors, cols, done):
    for at, n in enumerate(vectors):
        for cc in range(DC):
            last = pe.matmul(cols[:, at, cc:cc + 1], part[:, n, cc * P:(cc + 1) * P], ones[:, 0:1], start=True, stop=True)
    last.then_inc(done, 1)


def row_sums(pe, ones, part, vectors, rows, done):
    for at, n in enumerate(vectors):
        for h in range(2):
            last = pe.matmul(rows[0:1, at, h * HALF:(h + 1) * HALF], ones[:, 0:1],
                             part[:, n, h * HALF:(h + 1) * HALF], start=True, stop=True)
    last.then_inc(done, 1)


def modulation(nc, c, w_ada, b_ada, ln_g, ln_b, x, ident, ones, x_sb, silu_c, part_late, norm_cols, shift, scale,
               rope_table, table, x_in):
    with Scope(nc, "mod") as s:
        c_col = s.sb("c_col", [P, DC])
        w = s.sb("w", [P, EARLY, DC, D])
        part = s.sb("part", [P, EARLY, D])
        norm_rows = s.sb("norm_rows", [2 * 3 * DC, P])
        cols = s.ps("cols", [P, 2, DC])
        norm_ps = s.ps("norm_ps", [P, 2 * 3 * DC])
        c_in, b_in, table_in = s.sem("c_in"), s.sem("b_in"), s.sem("table_in")
        w_in = [[s.sem(f"w_in{v}_{k}") for k in range(DC)] for v in range(EARLY)]
        zeroed, silu_done, w_used = s.sem("zeroed"), s.sem("silu_done"), s.sem("w_used")
        summed = s.sem("summed")
        norm_in, norm_turned = s.sem("norm_in"), s.sem("norm_turned")
        block = s.block()
        w_src = w_ada[0].rearrange("(p k) n -> p k n", k=DC)
        b_src = b_ada.rearrange("l (v n) -> l v n", n=D)

        @block.sync
        def _(sp):
            sp.dma_start(c_col[:, :], c.rearrange("b (p k) -> (b p) k", k=DC)).then_inc(c_in, 16)
            for n, rows_dram in enumerate((ln_g, ln_b)):
                sp.dma_start(norm_rows[n * 3 * DC:(n + 1) * 3 * DC, :], rows_dram[0].rearrange("n (c p) -> (n c) p", p=P)).then_inc(norm_in, 16)

            for v in range(EARLY):
                for k in range(DC):
                    sp.dma_start(w[:, v, k, :], w_src[:, k, v * D:(v + 1) * D]).then_inc(w_in[v][k], 16)
                    if v == 0 and k == 2:
                        sp.wait_ge(zeroed, 1)
                        sp.dma_start(part[0:1, :, :], b_src[:, 0:EARLY, :]).then_inc(b_in, 16)
                        sp.dma_start(part_late[0:1, :, :], b_src[:, EARLY:N_MOD, :]).then_inc(b_in, 16)
            sp.dma_start(table[:, :, :], rope_table.rearrange("(i p) d -> p i d", p=P)).then_inc(table_in, 16)
            for half in range(2):
                tiles = slice(half * TT // 2, (half + 1) * TT // 2)
                sp.dma_start(x_sb[:, tiles, :], x[0].rearrange("(i p) d -> p i d", p=P)[:, tiles, :]).then_inc(x_in[half], 16)
            sp.wait_ge(table_in, 16)

        @block.gpsimd
        def _(pool):
            pool.memset(part[:, :, :], 0.0)
            pool.memset(part_late[:, :, :], 0.0).then_inc(zeroed, 1)

        @block.scalar
        def _(act):
            act.wait_ge(c_in, 16)
            act.activation(silu_c[:, :], c_col[:, :], ACT.Silu).then_inc(silu_done, 1)
            act.wait_ge(norm_turned, 1)
            act.activation(norm_cols[:, :, :, :].rearrange("p a n c -> p (a n c)"), norm_ps[:, :], ACT.Copy)
            act.wait_ge(summed, 1)
            act.activation(shift[:, 0, :], cols[:, 0, :], ACT.Identity)
            act.activation(scale[:, 0, :], cols[:, 1, :], ACT.Identity, bias=ones[:, 0:1])

        @block.vector
        def _(dve):
            dve.wait_ge(silu_done, 1)
            dve.wait_ge(b_in, 32)

            def weigh(v):
                for k in range(DC):
                    dve.wait_ge(w_in[v][k], 16)
                    if v or k:
                        dve.wait_ge(w_used, v * DC + k)
                    acc = part[:, v, :]
                    dve.scalar_tensor_tensor(out=acc, in0=w[:, v, k, :], scalar=silu_c[:, k:k + 1], in1=acc,
                                             op0=ALU.mult, op1=ALU.add).then_inc(w_used, 1)

            for v in range(EARLY):
                weigh(v)

        @block.tensor
        def _(pe):
            pe.wait_ge(norm_in, 32)
            pe.transpose(norm_ps[:, :], norm_rows[:, :], ident[0:2 * 3 * DC, 0:2 * 3 * DC]).then_inc(norm_turned, 1)
            pe.wait_ge(w_used, EARLY * DC)
            column_sums(pe, ones, part, (0, 1), cols, summed)


class Turn:

    SLOTS = 4

    def __init__(self, s, banks, units, ident):
        self.banks, self.units, self.ident = banks, units, ident
        self.u = s.sb("u", [P, self.SLOTS, HALF])
        self.tp = s.ps("tp", [P, banks, HALF])
        self.turned, self.placed, self.lo_done = s.sem("turned"), s.sem("placed"), s.sem("lo_done")
        self.hi_act, self.hi_dve = s.sem("hi_act"), s.sem("hi_dve")
        plain = units[0][3] is None
        self.by_act = [plain or m % 4 == 0 for m in range(len(units))]
        self.made = [self.by_act[:m + 1].count(self.by_act[m]) for m in range(len(units))]
        self.bank_read = self.lo_done if plain else self.placed

    def bank(self, m):
        return self.tp[:, m % self.banks, :]

    def pe(self, pe, m):
        if m >= self.banks:
            pe.wait_ge(self.bank_read, m - self.banks + 1)
        for i, tile in enumerate(self.units[m][0]):
            t = pe.transpose(self.bank(m)[:, i * P:(i + 1) * P], tile, self.ident[:, :])
        t.then_inc(self.turned, 1)

    def act(self, act, m):
        tiles, hi, lo, scale, shift = self.units[m]
        u = self.u[:, m % self.SLOTS, :]
        act.wait_ge(self.turned, m + 1)
        if scale is None:
            act.activation(hi, self.bank(m), ACT.Copy).then_inc(self.hi_act, 1)
            return
        if m >= self.SLOTS:
            act.wait_ge(self.lo_done, m - self.SLOTS + 1)
        if shift is None:
            act.activation(u, self.bank(m), ACT.Copy, scale=scale).then_inc(self.placed, 1)
        else:
            act.activation(u, self.bank(m), ACT.Identity, scale=scale, bias=shift).then_inc(self.placed, 1)
        if self.by_act[m]:
            act.wait_ge(self.placed, m + 1)
            act.activation(hi, u, ACT.Copy).then_inc(self.hi_act, 1)

    def dve(self, dve, m):
        tiles, hi, lo, scale, shift = self.units[m]
        u = self.bank(m) if scale is None else self.u[:, m % self.SLOTS, :]
        if self.by_act[m]:
            dve.wait_ge(self.hi_act, self.made[m])
        else:
            dve.wait_ge(self.placed, m + 1)
            dve.tensor_copy(hi, u).then_inc(self.hi_dve, 1)
            dve.wait_ge(self.hi_dve, self.made[m])
        dve.tensor_tensor(lo, u, hi.bitcast(F32), ALU.subtract).then_inc(self.lo_done, 1)


def row_units(x, scale, shift, u_hi, u_lo):
    units = []
    for h in range(2):
        for c in range(DC):
            cols = slice(h * HALF, (h + 1) * HALF)
            units.append(([x[:, 4 * h + i, c * P:(c + 1) * P] for i in range(4)], u_hi[:, c, cols], u_lo[:, c, cols],
                          None if scale is None else scale[:, c:c + 1], None if scale is None else shift[:, c:c + 1]))
    return units


def modulated_transpose(nc, stage, x_sb, shift, scale, ident, u_hi, u_lo, ahead, reload=None, arrives=None):
    with Scope(nc, stage) as s:
        turn = Turn(s, 6, row_units(x_sb, scale, shift, u_hi, u_lo), ident)
        block = s.block()

        @block.sync
        def _(sp):
            ahead(sp)
            if reload is not None:
                for i in range(TT):
                    sp.dma_start(reload[0][:, i, :], reload[1][i * P:(i + 1) * P, :]).then_inc(reload[2], 16)

        @block.tensor
        def _(pe):
            for m in range(len(turn.units)):
                if arrives is not None and m % DC == 0:
                    pe.wait_ge(arrives[m // DC], 16)
                turn.pe(pe, m)

        @block.scalar
        def _(act):
            for m in range(len(turn.units)):
                turn.act(act, m)

        @block.vector
        def _(dve):
            for m in range(len(turn.units)):
                turn.dve(dve, m)


class Residual:

    def __init__(self, s, norm_rows):
        self.norm_rows = norm_rows
        self.ticks = s.sem("ticks")
        if norm_rows is not None:
            self.gain, self.offset = s.sb("gain", [P, D]), s.sb("offset", [P, D])
            self.rows_in = s.sem("rows_in")

    def load(self, sp):
        if self.norm_rows is not None:
            for place, rows in zip((self.gain, self.offset), self.norm_rows):
                sp.dma_start(place[:, :], rows.to_broadcast([P, D])).then_inc(self.rows_in, 16)

    def grow(self, dve, x_sb, i):
        x = x_sb[:, i, :]
        if self.norm_rows is None:
            dve.tensor_scalar(x, x, ALPHA, None, ALU.mult).then_inc(self.ticks, 1)
            return
        if i == 0:
            dve.wait_ge(self.rows_in, 32)
        dve.scalar_tensor_tensor(out=x, in0=x, scalar=ALPHA, in1=self.gain[:, :], op0=ALU.mult, op1=ALU.mult).then_inc(self.ticks, 1)
        dve.wait_ge(self.ticks, 2 * i + 1)
        dve.scalar_tensor_tensor(out=x, in0=self.offset[:, :], scalar=ALPHA, in1=x, op0=ALU.mult, op1=ALU.add).then_inc(self.ticks, 1)

    def ends(self, i):
        return i + 1 if self.norm_rows is None else 2 * i + 2


LATE_TILES = DC // 2


class HiddenWeights:

    def __init__(self, s, wg, wu, wd):
        self.raw = {k: s.sb(f"w{k}_raw", [P, DC, P]) for k in "gud"}
        self.landed = {k: s.sem(f"w{k}_landed") for k in "gud"}
        self.src = {k: a[0].rearrange("(c p) n -> p c n", p=P) for k, a in (("g", wg), ("u", wu))}
        self.src["d"] = wd[0].rearrange("(f p) n -> f p n", p=P)

    def load(self, sp, k, f):
        if k == "d":
            at = self.src["d"][bass.ts(f, 1)].rearrange("a p n -> p (a n)")
            sp.dma_start(self.raw["d"][:, :, :].rearrange("p c n -> p (c n)"), at).then_inc(self.landed["d"], 16)
        else:
            sp.dma_start(self.raw[k][:, :, :], self.src[k][:, :, bass.ts(f, P)]).then_inc(self.landed[k], 16)

    def ahead(self, sp):
        for k in "gud":
            self.load(sp, k, 0)


def swiglu(nc, stage, weights, gate_dram, x_sb, u_hi, u_lo, norm_rows=None, late=None):
    with Scope(nc, stage) as s:
        raw, landed = weights.raw, weights.landed
        hi = {k: s.sb(f"w{k}_hi", [P, DC, P], F32R) for k in "gud"}
        lo = {k: s.sb(f"w{k}_lo", [P, DC, P], F32R) for k in "gud"}
        wd_gated = s.sb("wd_gated", [P, D])
        gate = s.sb("gate", [P, D])
        gate_in = s.sem("gate_in")
        silu_g = s.sb("silu_g", [P, T])
        h_f32 = s.sb("h_f32", [P, T])
        h_hi = s.sb("h_hi", [P, 2, T], F32R)
        h_lo = s.sb("h_lo", [P, 2, T], F32R)
        g_ps = s.ps("g_ps", [P, T])
        u_ps = s.ps("u_ps", [P, T])
        y_ps = s.ps("y_ps", [P, 4, HALF])
        hi_ready = {k: s.sem(f"w{k}_hi_ready") for k in "gud"}
        split = {k: s.sem(f"w{k}_split") for k in "gud"}
        g_done, u_done, y_done = s.sem("g_done"), s.sem("u_done"), s.sem("y_done")
        silu_done, h_made, h_hi_ready, h_split = s.sem("silu_done"), s.sem("h_made"), s.sem("h_hi_ready"), s.sem("h_split")
        gated, y_added = s.sem("gated"), s.sem("y_added")
        residual = Residual(s, norm_rows)
        if late is not None:
            w_ada, silu_c, ones, part_late = late
            gate_summed = s.sem("gate_summed")
            ada = s.sb("ada", [P, 2, D])
            ada_in, weighed = [s.sem(f"ada_in{n}") for n in range(2)], s.sem("weighed")
            ada_src = w_ada[0].rearrange("(p k) n -> p k n", k=DC)
            parts = part_late[:, :, :].rearrange("p v n -> p (v n)")
        block = s.block()
        flat = lambda a: a.rearrange("p c n -> p (c n)")

        def steps(eng, one, tail=None):
            one(0, 0)
            one(1, 1)
            with eng.Fori(2, FC - 2, 2) as f:
                one(f, 0)
                one(f + 1, 1)
            one(FC - 2, 0)
            one(FC - 1, 1)

        def late_steps(eng, one, rest):
            if late is None:
                return steps(eng, rest)
            one(0, 0)
            one(1, 1)
            with eng.Fori(1, LATE) as v:
                one(v * 2, 0)
                one(v * 2 + 1, 1)
            if rest is not None:
                with eng.Fori(2 * LATE, FC - 2, 2) as f:
                    rest(f, 0)
                    rest(f + 1, 1)
                rest(FC - 2, 0)
                rest(FC - 1, 1)

        def after_first(f):
            return not isinstance(f, int) or f > 0

        def not_last(f):
            return not isinstance(f, int) or f < FC - 1

        @block.sync
        def _(sp):
            def load(f):
                for k in "gud":
                    sp.wait_ge(gated if k == "d" else split[k], f)
                    weights.load(sp, k, f)

            if gate_dram is not None:
                sp.dma_start(gate[:, :], gate_dram.to_broadcast([P, D])).then_inc(gate_in, 16)
            residual.load(sp)
            load(1)
            with sp.Fori(2, FC) as f:
                load(f)

        @block.gpsimd
        def _(pool):
            def bring(f, parity):
                if isinstance(f, int):
                    for k in range(DC if f == 0 else 0):
                        if k >= 2:
                            pool.wait_ge(weighed, k - 1)
                        pool.dma_start(ada[:, k % 2, :], ada_src[:, k, EARLY * D:(EARLY + 1) * D]).then_inc(ada_in[k % 2], 16)
                    return
                for j in range(LATE_TILES):
                    pool.wait_ge(weighed, f * LATE_TILES + (j - 1))
                    at = ada_src[:, parity * LATE_TILES + j, bass.ds(EARLY * D + (f - parity) * (D // 2), D)]
                    pool.dma_start(ada[:, j % 2, :], at).then_inc(ada_in[j % 2], 16)

            if late is not None:
                late_steps(pool, bring, None)

        @block.scalar
        def _(act):
            def hi_of(k, f, source, done):
                if after_first(f):
                    act.wait_ge(done, f * (2 * TT if k == "d" else 1))
                act.activation(flat(hi[k]), source, ACT.Copy).then_inc(hi_ready[k], 1)

            def hidden(f, parity):
                act.wait_ge(gated, f + 1)
                hi_of("d", f, wd_gated[:, :], y_done)
                act.wait_ge(h_made, f + 1)
                act.activation(h_hi[:, parity, :], h_f32[:, :], ACT.Copy).then_inc(h_hi_ready, 1)

            def step(f, parity):
                act.wait_ge(landed["u"], f * 16 + 16)
                hi_of("u", f, flat(raw["u"]), u_done)
                if after_first(f):
                    hidden(f - 1, 1 - parity)
                act.wait_ge(g_done, f + 1)
                if after_first(f):
                    act.wait_ge(h_made, f)
                act.activation(silu_g[:, :], g_ps[:, :], ACT.Silu).then_inc(silu_done, 1)
                if not_last(f):
                    act.wait_ge(landed["g"], f * 16 + 32)
                    hi_of("g", f + 1, flat(raw["g"]), g_done)
                if late is not None and isinstance(f, int) and f == 0:
                    act.wait_ge(gate_summed, 1)
                    act.activation(gate[:, :], y_ps[:, 0:2, :].rearrange("p a n -> p (a n)"), ACT.Copy, scale=0.5,
                                   bias=0.5).then_inc(gate_in, 16)

            act.wait_ge(landed["g"], 16)
            hi_of("g", 0, flat(raw["g"]), g_done)
            steps(act, step)
            act.wait_ge(gated, FC)
            act.wait_ge(g_done, FC)
            act.activation(flat(hi["g"]), wd_gated[:, :], ACT.Copy).then_inc(hi_ready["d"], 1)
            act.wait_ge(h_made, FC)
            act.activation(h_hi[:, (FC - 1) % 2, :], h_f32[:, :], ACT.Copy).then_inc(h_hi_ready, 1)

        @block.vector
        def _(dve):
            def lo_of(k, f, source):
                dve.wait_ge(hi_ready[k], f + 1)
                dve.tensor_tensor(flat(lo[k]), source, flat(hi[k]).bitcast(F32), ALU.subtract).then_inc(split[k], 1)

            def gate_down(f):
                dve.wait_ge(landed["d"], f * 16 + 16)
                if after_first(f):
                    dve.wait_ge(split["d"], f)
                dve.tensor_tensor(wd_gated[:, :], flat(raw["d"]), gate[:, :], ALU.mult).then_inc(gated, 1)

            def make_h(f):
                dve.wait_ge(u_done, f + 1)
                dve.wait_ge(silu_done, f + 1)
                if after_first(f):
                    dve.wait_ge(h_split, f)
                dve.tensor_tensor(h_f32[:, :], silu_g[:, :], u_ps[:, :], ALU.mult).then_inc(h_made, 1)

            def split_h(f, parity):
                dve.wait_ge(h_hi_ready, f + 1)
                dve.tensor_tensor(h_lo[:, parity, :], h_f32[:, :], h_hi[:, parity, :].bitcast(F32),
                                  ALU.subtract).then_inc(h_split, 1)

            def hidden(f, parity):
                gate_down(f)
                make_h(f)
                lo_of("d", f, wd_gated[:, :])
                split_h(f, parity)

            def add_down(f, tiles=range(TT)):
                for n in range(2 * tiles[0], 2 * tiles[-1] + 2):
                    i, e = divmod(n, 2)
                    dve.wait_ge(y_done, f * (2 * TT) + n + 1)
                    x = x_sb[:, i, e * HALF:(e + 1) * HALF]
                    dve.tensor_tensor(x, x, y_ps[:, n % 4, :], ALU.add).then_inc(y_added, 1)

            def weigh_gate():
                for k in range(DC):
                    dve.wait_ge(ada_in[k % 2], 16 * (k // 2 + 1))
                    if k:
                        dve.wait_ge(weighed, k)
                    dve.scalar_tensor_tensor(out=part_late[:, 0, :], in0=ada[:, k % 2, :], scalar=silu_c[:, k:k + 1],
                                             in1=part_late[:, 0, :], op0=ALU.mult, op1=ALU.add).then_inc(weighed, 1)

            def weigh(f, parity, tiles):
                acc = parts[:, bass.ds((f - parity) * (D // 2), D)]
                for j in tiles:
                    dve.wait_ge(ada_in[j % 2], f * (8 * LATE_TILES) + 16 * (j // 2 + 1))
                    dve.wait_ge(weighed, f * LATE_TILES + j)
                    k = parity * LATE_TILES + j
                    dve.scalar_tensor_tensor(out=acc, in0=ada[:, j % 2, :], scalar=silu_c[:, k:k + 1], in1=acc,
                                             op0=ALU.mult, op1=ALU.add).then_inc(weighed, 1)

            def last_steps(f, parity):
                lo_of("u", f, flat(raw["u"]))
                hidden(f - 1, 1 - parity)
                gate_down(f)
                add_down(f - 1, [0])
                make_h(f)
                add_down(f - 1, [1, 2])
                split_h(f, parity)
                add_down(f - 1, [3])
                dve.wait_ge(hi_ready["d"], f + 1)
                dve.tensor_tensor(flat(lo["g"]), wd_gated[:, :], flat(hi["g"]).bitcast(F32), ALU.subtract).then_inc(split["d"], 1)
                add_down(f - 1, range(4, TT))
                add_down(f)

            def step(f, parity, weighing=False):
                if isinstance(f, int) and f == FC - 1:
                    return last_steps(f, parity)
                lo_of("u", f, flat(raw["u"]))
                if weighing and isinstance(f, int) and f == 0:
                    weigh_gate()
                if weighing and not isinstance(f, int):
                    weigh(f, parity, range(LATE_TILES // 2))
                if isinstance(f, int) and f == 1:
                    dve.wait_ge(gate_in, 16)
                if after_first(f):
                    hidden(f - 1, 1 - parity)
                if not_last(f):
                    lo_of("g", f + 1, flat(raw["g"]))
                if weighing and not isinstance(f, int):
                    weigh(f, parity, range(LATE_TILES // 2, LATE_TILES))
                if isinstance(f, int) and f < 2:
                    for i in range(f * TT // 2, (f + 1) * TT // 2):
                        residual.grow(dve, x_sb, i)
                if after_first(f):
                    if isinstance(f, int) and f == 1:
                        dve.wait_ge(residual.ticks, residual.ends(TT - 1))
                    add_down(f - 1)

            lo_of("g", 0, flat(raw["g"]))
            late_steps(dve, lambda f, parity: step(f, parity, True), step)

        @block.tensor
        def _(pe):
            def project(k, out, f, done):
                pe.wait_ge(split[k], f + 1)
                for c in range(DC):
                    for n, (w, u) in enumerate(((hi[k], u_hi), (hi[k], u_lo), (lo[k], u_hi))):
                        for h in range(2):
                            last = pe.matmul(out[:, h * HALF:(h + 1) * HALF], w[:, c, :], u[:, c, h * HALF:(h + 1) * HALF],
                                             start=(c == 0 and n == 0), stop=(c == DC - 1 and n == 2))
                last.then_inc(done, 1)

            def down(f, parity, k="d"):
                pe.wait_ge(split["d"], f + 1)
                pe.wait_ge(h_split, f + 1)
                for n in range(2 * TT):
                    i, e = divmod(n, 2)
                    if not (isinstance(f, int) and f == 0 and n < 4):
                        pe.wait_ge(y_added, f * (2 * TT) + n - 3)
                    for m, (h, w) in enumerate(((h_hi, hi[k]), (h_hi, lo[k]), (h_lo, hi[k]))):
                        last = pe.matmul(y_ps[:, n % 4, :], h[:, parity, i * P:(i + 1) * P],
                                         flat(w)[:, e * HALF:(e + 1) * HALF], start=(m == 0), stop=(m == 2))
                    last.then_inc(y_done, 1)

            def step(f, parity):
                if after_first(f):
                    pe.wait_ge(silu_done, f)
                project("g", g_ps, f, g_done)
                if after_first(f):
                    pe.wait_ge(h_made, f)
                project("u", u_ps, f, u_done)
                if late is not None and isinstance(f, int) and f == 0:
                    pe.wait_ge(weighed, DC)
                    for e in range(2):
                        last = pe.matmul(y_ps[:, e, :], ones[:, :], part_late[:, 0, e * HALF:(e + 1) * HALF], start=True,
                                         stop=True)
                    last.then_inc(gate_summed, 1)
                if late is not None and isinstance(f, int) and f == 1:
                    pe.wait_ge(gate_in, 16)
                if after_first(f):
                    down(f - 1, 1 - parity)

            steps(pe, step)
            down(FC - 1, (FC - 1) % 2, "g")


class Normalise:

    def __init__(self, s, x_sb):
        self.x_sb = x_sb
        self.stats = s.sb("stats", [P, TT, 2, 6])
        self.mv = s.sb("mv", [P, TT, 2])
        self.std = s.sb("std", [P, TT])
        self.rstd = s.sb("rstd", [P, TT])
        self.minus_mean = s.sb("minus_mean", [P, TT])
        self.eps = s.sb("eps", [P, 1])
        self.eps_set, self.halved, self.known = s.sem("eps_set"), s.sem("halved"), s.sem("known")
        self.rooted, self.inverted, self.factored = s.sem("rooted"), s.sem("inverted"), s.sem("factored")
        self.normed = s.sem("normed")

    def begin(self, dve):
        dve.memset(self.eps[:, :], EPS).then_inc(self.eps_set, 1)
        self.statistics(dve, 0)

    def statistics(self, dve, i):
        for h in range(2):
            dve.bn_stats(self.stats[:, i, h, :], self.x_sb[:, i, h * HALF:(h + 1) * HALF]).then_inc(self.halved, 1)
        dve.wait_ge(self.halved, 2 * (i + 1))
        dve.bn_aggr(self.mv[:, i, :], self.stats[:, i, :, :].rearrange("p h s -> p (h s)")).then_inc(self.known, 1)

    def factor(self, dve, i):
        if i + 1 < TT:
            self.statistics(dve, i + 1)
        dve.wait_ge(self.rooted, i + 1)
        dve.reciprocal(self.rstd[:, i:i + 1], self.std[:, i:i + 1]).then_inc(self.inverted, 1)
        dve.wait_ge(self.inverted, i + 1)
        dve.scalar_tensor_tensor(out=self.minus_mean[:, i:i + 1], in0=self.mv[:, i, 0:1], scalar=-1.0,
                                 in1=self.rstd[:, i:i + 1], op0=ALU.mult, op1=ALU.mult).then_inc(self.factored, 1)

    def root(self, act, i):
        if i == 0:
            act.wait_ge(self.eps_set, 1)
        act.wait_ge(self.known, i + 1)
        act.activation(self.std[:, i:i + 1], self.mv[:, i, 1:2], ACT.Sqrt, bias=self.eps[:, 0:1]).then_inc(self.rooted, 1)

    def apply(self, act, i):
        if i + 1 < TT:
            self.root(act, i + 1)
        act.wait_ge(self.factored, i + 1)
        x = self.x_sb[:, i, :]
        act.activation(x, x, ACT.Identity, scale=self.rstd[:, i:i + 1], bias=self.minus_mean[:, i:i + 1]).then_inc(self.normed, 1)


def norm_turn(nc, stage, x_sb, n, norm_cols, shift, scale, ident, u_hi, u_lo, ahead, late=None):
    with Scope(nc, stage) as s:
        norm = Normalise(s, x_sb)
        gain = s.sb("gain", [P, DC])
        offset = s.sb("offset", [P, DC])
        folded, offset_scaled = s.sem("folded"), s.sem("offset_scaled")
        if late is not None:
            ones, part_late, gate_dram, shifts, scales = late
            gate = s.sb("gate", [P, 2, D])
            cols = s.ps("cols", [P, 4, DC])
            rows = s.ps("rows", [P, 2, D])
            cols_summed, rows_summed, cols_out = s.sem("cols_summed"), s.sem("rows_summed"), s.sem("cols_out")
            gate_made, gate_out = s.sem("gate_made"), s.sem("gate_out")
        turn = Turn(s, 3 if late is not None else 6, row_units(x_sb, gain, offset, u_hi, u_lo), ident)
        block = s.block()

        @block.sync
        def _(sp):
            ahead(sp)
            if late is not None:
                sp.wait_ge(gate_made, 2)
                sp.dma_start(gate_dram.unsqueeze(0), gate[0:1, :, :]).then_inc(gate_out, 16)
                sp.wait_ge(gate_out, 16)

        @block.tensor
        def _(pe):
            if late is not None:
                column_sums(pe, ones, part_late, (1, 2, 4, 5), cols, cols_summed)
            for half in range(2):
                pe.wait_ge(norm.normed, (half + 1) * TT // 2)
                for m in range(half * DC, (half + 1) * DC):
                    turn.pe(pe, m)
                if half == 0 and late is not None:
                    row_sums(pe, ones, part_late, (3, 6), rows, rows_summed)

        @block.scalar
        def _(act):
            norm.root(act, 0)
            for i in range(TT):
                norm.apply(act, i)
                if i == 2 and late is not None:
                    act.wait_ge(cols_summed, 1)
                    for m in range(2):
                        act.activation(shifts[:, m + 1, :], cols[:, 2 * m, :], ACT.Identity).then_inc(cols_out, 1)
                        act.activation(scales[:, m + 1, :], cols[:, 2 * m + 1, :], ACT.Identity, bias=ones[:, 0:1]).then_inc(cols_out, 1)
                if i == TT // 2:
                    act.wait_ge(folded, 2)
                if i >= TT // 2:
                    turn.act(act, i - TT // 2)
            for m in range(TT // 2, len(turn.units)):
                turn.act(act, m)
                if m == TT and late is not None:
                    act.wait_ge(rows_summed, 1)
                    for n, part in enumerate((1.0, 0.5)):
                        act.activation(gate[0:1, n, :], rows[0:1, n, :], ACT.Copy, scale=part, bias=part).then_inc(gate_made, 1)

        @block.vector
        def _(dve):
            norm.begin(dve)
            for i in range(TT):
                norm.factor(dve, i)
                if i == 3:
                    if late is not None:
                        dve.wait_ge(cols_out, 4)
                    dve.tensor_tensor(gain[:, :], norm_cols[:, 0, n, :], scale, ALU.mult).then_inc(folded, 1)
                    dve.tensor_tensor(offset[:, :], norm_cols[:, 1, n, :], scale, ALU.mult).then_inc(offset_scaled, 1)
                    dve.wait_ge(offset_scaled, 1)
                    dve.tensor_tensor(offset[:, :], offset[:, :], shift, ALU.add).then_inc(folded, 1)
                if i >= TT // 2 + 1:
                    turn.dve(dve, i - TT // 2 - 1)
            for m in range(TT // 2 - 1, len(turn.units)):
                turn.dve(dve, m)


def norm_out(nc, stage, x_sb, g_dram, b_dram, out_dram):
    with Scope(nc, stage) as s:
        norm = Normalise(s, x_sb)
        g_row = s.sb("g_row", [P, D])
        b_row = s.sb("b_row", [P, D])
        rows_in, scaled, shifted, stored = s.sem("rows_in"), s.sem("scaled"), s.sem("shifted"), s.sem("stored")
        block = s.block()

        @block.sync
        def _(sp):
            sp.dma_start(g_row[:, :], g_dram.to_broadcast([P, D])).then_inc(rows_in, 16)
            sp.dma_start(b_row[:, :], b_dram.to_broadcast([P, D])).then_inc(rows_in, 16)
            for i in range(TT):
                sp.wait_ge(shifted, i + 1)
                sp.dma_start(out_dram[0, i * P:(i + 1) * P, :], x_sb[:, i, :]).then_inc(stored, 16)
            sp.wait_ge(stored, 16 * TT)

        @block.scalar
        def _(act):
            norm.root(act, 0)
            for i in range(TT):
                norm.apply(act, i)

        @block.vector
        def _(dve):
            def scale_tile(i):
                if i == 0:
                    dve.wait_ge(rows_in, 32)
                dve.wait_ge(norm.normed, i + 1)
                dve.tensor_tensor(x_sb[:, i, :], x_sb[:, i, :], g_row[:, :], ALU.mult).then_inc(scaled, 1)

            norm.begin(dve)
            for i in range(TT):
                norm.factor(dve, i)
                if i:
                    scale_tile(i - 1)
            scale_tile(TT - 1)

        @block.gpsimd
        def _(pool):
            pool.wait_ge(rows_in, 32)
            for i in range(TT):
                pool.wait_ge(scaled, i + 1)
                pool.tensor_tensor(x_sb[:, i, :], x_sb[:, i, :], b_row[:, :], ALU.add).then_inc(shifted, 1)


class Chunks:

    SLOTS = 4

    def __init__(self, s, w_dram, width, gate_dram=None):
        self.width, self.gate_dram = width, gate_dram
        self.raw = s.sb("w_raw", [P, self.SLOTS, width])
        self.landed = [s.sem(f"w_landed{k}") for k in range(self.SLOTS)]
        self.src = w_dram.rearrange("(c p) n -> p c n", p=P)
        if gate_dram is not None:
            self.gate = s.sb("gate", [P, w_dram.shape[1]])
            self.gate_in = s.sem("gate_in")

    def load(self, sp, n, c):
        k = c % self.SLOTS
        sp.dma_start(self.raw[:, k, :], self.src[:, c, bass.ds(n * self.width, self.width)]).then_inc(self.landed[k], 16)

    def ahead(self, sp):
        if self.gate_dram is not None:
            sp.dma_start(self.gate[:, :], self.gate_dram.to_broadcast(list(self.gate.shape))).then_inc(self.gate_in, 16)
        for c in range(self.SLOTS):
            self.load(sp, 0, c)


def project(nc, stage, chunks, blocks, u_hi, u_lo, out, out_in=None, beside=None):
    slots, width, gated_too = chunks.SLOTS, chunks.width, chunks.gate_dram is not None
    raw, landed = chunks.raw, chunks.landed
    with Scope(nc, stage) as s:
        hi = s.sb("w_hi", [P, slots, width], F32R)
        lo = s.sb("w_lo", [P, slots, width], F32R)
        if beside is not None:
            x_sb, norm_rows, x_dram, x_out, table = beside
            residual = Residual(s, norm_rows)
            rope = RopeSparse(s)
        acc = s.ps("acc", [P, TT, HALF])
        gated, hi_ready, split = s.sem("gated"), s.sem("hi_ready"), s.sem("split")
        used, row_done, taken = s.sem("used"), s.sem("row_done"), s.sem("taken")
        block = s.block()

        def wait_slot_used(eng, n, c):
            if c >= slots:
                eng.wait_ge(used, n * (DC - 1) + c - slots + 1)
            elif c == slots - 1:
                eng.wait_ge(row_done, n * TT)
            else:
                eng.wait_ge(used, (n - 1) * (DC - 1) + c + slots + 1)

        def steps(eng, one, begun=False):
            if not begun:
                one(0)
            if blocks > 2:
                with eng.Fori(1, blocks - 1) as n:
                    one(n)
            one(blocks - 1)

        later = lambda n, c: not isinstance(n, int) or n > 0 or c >= slots

        def per_block(split_chunk, take):
            def one(n):
                for c in range(slots, DC):
                    split_chunk(n, c)
                more = not isinstance(n, int) or n < blocks - 1
                if more:
                    for c in range(slots - 1):
                        split_chunk(n + 1, c)
                take(n)
                if more:
                    split_chunk(n + 1, slots - 1)
            return one

        @block.sync
        def _(sp):
            def load(n, first=0):
                for c in range(first, DC):
                    sp.wait_ge(split, n * DC + c - slots + 1)
                    chunks.load(sp, n, c)

            load(0, slots)
            if beside is not None:
                residual.load(sp)
                for i in range(TT):
                    sp.wait_ge(residual.ticks, residual.ends(i))
                    sp.dma_start(x_dram[i * P:(i + 1) * P, :], x_sb[:, i, :]).then_inc(x_out, 16)
            steps(sp, load, True)
            if beside is not None:
                sp.wait_ge(x_out, 16 * TT)

        @block.scalar
        def _(act):
            def make_hi(n, c):
                k = c % slots
                if not gated_too:
                    act.wait_ge(landed[k], (n * 2 + c // slots) * 16 + 16)
                else:
                    act.wait_ge(gated, n * DC + c + 1)
                if later(n, c):
                    wait_slot_used(act, n, c)
                act.activation(hi[:, k, :], raw[:, k, :], ACT.Copy).then_inc(hi_ready, 1)

            def take(n):
                if not gated_too:
                    for i in range(TT):
                        act.wait_ge(row_done, n * TT + i + 1)
                        act.activation(out[:, i, bass.ds(n * width, width)], acc[:, i, 0:width],
                                       ACT.Copy).then_inc(taken, 1)

            for c in range(slots):
                make_hi(0, c)
            steps(act, per_block(make_hi, take))

        @block.vector
        def _(dve):
            def make_lo(n, c):
                k = c % slots
                if gated_too:
                    dve.wait_ge(landed[k], (n * 2 + c // slots) * 16 + 16)
                    dve.tensor_tensor(raw[:, k, :], raw[:, k, :], chunks.gate[:, bass.ds(n * width, width)],
                                      ALU.mult).then_inc(gated, 1)
                dve.wait_ge(hi_ready, n * DC + c + 1)
                dve.tensor_tensor(lo[:, k, :], raw[:, k, :], hi[:, k, :].bitcast(F32), ALU.subtract).then_inc(split, 1)
                if beside is not None and isinstance(n, int) and c >= slots:
                    for i in range(2 * (c - slots), 2 * (c - slots) + 2):
                        if n == 0:
                            residual.grow(dve, x_sb, i)
                        else:
                            if i == 0:
                                dve.wait_ge(taken, n * TT)
                            rope.tile(dve, out, table, i)

            def take(n):
                if gated_too:
                    if n == 0:
                        dve.wait_ge(*out_in)
                    for i in range(TT):
                        dve.wait_ge(row_done, n * TT + i + 1)
                        at = out[:, i, bass.ds(n * width, width)]
                        dve.tensor_tensor(at, at, acc[:, i, 0:width], ALU.add).then_inc(taken, 1)

            if gated_too:
                dve.wait_ge(chunks.gate_in, 16)
            for c in range(slots):
                make_lo(0, c)
            steps(dve, per_block(make_lo, take))

        @block.tensor
        def _(pe):
            def one(n):
                for c in range(DC):
                    pe.wait_ge(split, n * DC + c + 1)
                    for i in range(TT):
                        if c == 0 and later(n, 0):
                            pe.wait_ge(taken, (n - 1) * TT + i + 1)
                        for m, (u, w) in enumerate(((u_hi, hi), (u_hi, lo), (u_lo, hi))):
                            last = pe.matmul(acc[:, i, 0:width], u[:, c, i * P:(i + 1) * P], w[:, c % slots, :],
                                             start=(c == 0 and m == 0), stop=(c == DC - 1 and m == 2))
                        if c == DC - 1:
                            last.then_inc(row_done, 1)
                    if c < DC - 1:
                        last.then_inc(used, 1)

            steps(pe, one)


def rope_rows(eng, at, heads, half, cos, sin, tmp, ticks):
    sem, n = ticks
    x1, x2 = at[:, :, 0:half], at[:, :, half:2 * half]
    wide = lambda table: table.unsqueeze(1).to_broadcast([P, heads, half])
    a, b, c, d = (tmp[:, k, 0:heads * half].rearrange("p (h j) -> p h j", j=half) for k in range(4))
    if n:
        eng.wait_ge(sem, n)
    eng.tensor_tensor(a, x1, wide(cos), ALU.mult).then_inc(sem, 1)
    eng.tensor_tensor(b, x2, wide(sin), ALU.mult).then_inc(sem, 1)
    eng.tensor_tensor(c, x2, wide(cos), ALU.mult).then_inc(sem, 1)
    eng.tensor_tensor(d, x1, wide(sin), ALU.mult).then_inc(sem, 1)
    eng.wait_ge(sem, n + 4)
    eng.tensor_tensor(x1, a, b, ALU.subtract).then_inc(sem, 1)
    eng.tensor_tensor(x2, c, d, ALU.add).then_inc(sem, 1)
    return sem, n + 6


class RopeSparse:

    def __init__(self, s):
        self.tmp = s.sb("rope_tmp", [P, 4, (HEADS + GROUPS) * ROPE_N // 2])
        self.ticks = (s.sem("roped"), 0)

    def tile(self, eng, h, table, i):
        half = ROPE_N // 2
        cos, sin = table[:, i, 0:half], table[:, i, half:2 * half]
        for col, heads in ((COL_Q, HEADS + GROUPS), (COL_KS, GROUPS), (COL_KW, GROUPS)):
            at = h[:, i, col:col + heads * HD].rearrange("p (h d) -> p h d", d=HD)
            self.ticks = rope_rows(eng, at, heads, half, cos, sin, self.tmp, self.ticks)


class RopeLatent:

    def __init__(self, s, name, heads, col, width):
        self.heads, self.col, self.width = heads, col, width
        self.tmp = s.sb(name + "_tmp", [P, 4, heads * ROPE_M // 2])
        self.ticks = (s.sem(name), 0)

    def tile(self, eng, h, table, i):
        half = ROPE_M // 2
        cos, sin = table[:, i, ROPE_N:ROPE_N + half], table[:, i, ROPE_N + half:ROPE_N + ROPE_M]
        at = h[:, i, self.col:self.col + self.heads * self.width].rearrange("p (h d) -> p h d", d=self.width)
        at = at[:, :, self.width - ROPE_M:self.width]
        self.ticks = rope_rows(eng, at, self.heads, half, cos, sin, self.tmp, self.ticks)


def sparse_inputs(nc, stage, h, table, gates, ident, pos, w1, w2, k_hi, k_lo, v, kc_hi, kc_lo, vc, rstd):
    with Scope(nc, stage) as s:
        x2 = s.sb("x2", [P, 2, GROUPS, HALF])
        blocks = s.sb("blocks", [P, 2, CMP_PAIRS, GROUPS, CMP_PAD])
        w1_sb = s.sb("w1", [P, 2, CMP_PAIRS, CMP_HIDDEN])
        w2_sb = s.sb("w2", [P, 2, 2, P])
        pos_sb = s.sb("pos", [P, 2, CMP_PAIRS])
        hidden = s.sb("hidden", [P, 2, 2, GROUPS * CMP_PAD])
        square = s.sb("square", [P, Q_RANK])
        sums = s.sb("sums", [P, 2, TT])
        eps = s.sb("eps", [P, 1])
        root = s.sb("root", [P, 2, TT])
        tp = s.ps("tp", [P, 4, HALF])
        hid_banks = s.ps("hid_ps", [P, 2, HALF])
        out_banks = s.ps("out_ps", [P, 2, HALF])
        hid_ps = hid_banks[:, :, 0:2 * P].rearrange("p k (m n) -> p k m n", m=2)
        kc_ps = out_banks[:, 0, 0:GROUPS * CMP_PAD].rearrange("p (g n) -> p g n", g=GROUPS)
        vc_ps = out_banks[:, 1, 0:GROUPS * CMP_PAD].rearrange("p (g n) -> p g n", g=GROUPS)
        turned, moved = s.sem("turned"), s.sem("moved")
        hi_done, v_hi_done = s.sem("hi_done"), s.sem("v_hi_done")
        w_in, w2_in, pos_in, padded = [s.sem(f"w_in{n}") for n in range(2)], s.sem("w2_in"), s.sem("pos_in"), s.sem("padded")
        placed, hid_done, gelu_done, out_done = s.sem("placed"), s.sem("hid_done"), s.sem("gelu_done"), s.sem("out_done")
        c_hi_done = s.sem("c_hi_done")
        eps_set, squared, rooted = s.sem("eps_set"), s.sem("squared"), s.sem("rooted")
        rope = RopeLatent(s, "rope_k", 1, COL_KR, ROPE_M)
        block = s.block()
        tokens = [(kv, half) for kv in range(2) for half in range(2)]
        keys = [(br, half) for br in range(2) for half in range(2)]
        col_k, col_v, col_c = (COL_KS, COL_KW), (COL_VS, COL_VW), (COL_KC, COL_VC)

        @block.sync
        def _(sp):
            for kv in range(2):
                sp.dma_start(w1_sb[:, kv, :, :], w1[kv][0].rearrange("(a p) n -> p a n", p=P)).then_inc(w_in[kv], 16)
                if kv == 0:
                    with nc.allow_non_contiguous_dma(reason="two small tables of positions, their dimension on partitions"):
                        for n in range(2):
                            sp.dma_start(pos_sb[:, n, :], pos[n][0].rearrange("(a j) d -> (j d) a", j=2)).then_inc(pos_in, 16)
                for twice in range(2):
                    sp.dma_start(w2_sb[:, kv, :, twice * HD:(twice + 1) * HD],
                                 w2[kv][0].rearrange("(m p) d -> p m d", p=P)).then_inc(w2_in, 16)

        @block.tensor
        def _(pe):
            for n, (kind, half) in enumerate(tokens + keys):
                col = col_c[kind] if n < len(tokens) else col_k[kind]
                if n >= 4:
                    pe.wait_ge(moved, 4 * (n - 3))
                for i in range(4):
                    t = pe.transpose(tp[:, n % 4, i * P:(i + 1) * P], h[:, 4 * half + i, col:col + P], ident[:, :])
                t.then_inc(turned, 1)
            pe.wait_ge(padded, 1)
            for kv in range(2):
                pe.wait_ge(w_in[kv], 16)
                for m in range(2):
                    for a in range(CMP_PAIRS):
                        if m == 0:
                            pe.wait_ge(placed, kv * CMP_PAIRS + a + 1)
                        last = pe.matmul(hid_ps[:, kv, m, :], w1_sb[:, kv, a, m * P:(m + 1) * P],
                                         blocks[:, kv, a, :, :].rearrange("p g n -> p (g n)"),
                                         start=(a == 0), stop=(a == CMP_PAIRS - 1))
                last.then_inc(hid_done, 1)
            pe.wait_ge(w2_in, 64)
            pe.wait_ge(gelu_done, 1)
            for m in range(2):
                last = pe.matmul(out_banks[:, 0, 0:GROUPS * CMP_PAD], w2_sb[:, 0, m, :], hidden[:, 0, m, :],
                                 start=(m == 0), stop=(m == 1))
            last.then_inc(out_done, 1)
            pe.wait_ge(gelu_done, 2)
            for g in range(GROUPS):
                for m in range(2):
                    last = pe.matmul(vc_ps[0:CMP_PAD, g, :], hidden[:, 1, m, g * CMP_PAD:(g + 1) * CMP_PAD],
                                     w2_sb[:, 1, m, 0:HD], start=(m == 0), stop=(m == 1))
            last.then_inc(out_done, 1)

        @block.gpsimd
        def _(pool):
            pool.memset(blocks[:, :, :, :, N_CMP:CMP_PAD], 0.0).then_inc(padded, 1)
            for i in range(TT):
                rope.tile(pool, h, table, i)

        @block.scalar
        def _(act):
            for n, (kv, half) in enumerate(tokens):
                act.wait_ge(turned, n + 1)
                for g in range(GROUPS):
                    for odd in range(2):
                        act.activation(x2[odd * HD:(odd + 1) * HD, kv, g, half * 256:(half + 1) * 256],
                                       tp[g * HD:(g + 1) * HD, n % 4, odd::2], ACT.Copy).then_inc(moved, 1)
            for n, (br, half) in enumerate(keys):
                act.wait_ge(turned, len(tokens) + n + 1)
                for g in range(GROUPS):
                    for place in range(2):
                        act.activation(k_hi[place * HD:(place + 1) * HD, br, g, half * HALF:(half + 1) * HALF],
                                       tp[g * HD:(g + 1) * HD, n % 4, :], ACT.Copy).then_inc(hi_done, 1)
            for br in range(2):
                for g in range(GROUPS):
                    rows = h[:, :, col_v[br] + g * HD:col_v[br] + (g + 1) * HD]
                    act.activation(v[:, br, g, :, 0:HD], rows, ACT.Copy).then_inc(v_hi_done, 1)
            count = 0
            for n, (col, rank) in enumerate(LATENTS):
                for i in range(TT):
                    if count:
                        act.wait_ge(squared, count)
                    act.activation(square[:, 0:rank], h[:, i, col:col + rank], ACT.Square,
                                   accum_out=sums[:, n, i:i + 1]).then_inc(squared, 1)
                    count += 1
            act.wait_ge(squared, count)
            act.wait_ge(eps_set, 1)
            for n, (col, rank) in enumerate(LATENTS):
                act.activation(root[:, n, :], sums[:, n, :], ACT.Sqrt, scale=1.0 / rank, bias=eps[:, 0:1]).then_inc(rooted, 1)
            for kv in range(2):
                act.wait_ge(hid_done, kv + 1)
                act.activation(hidden[:, kv, :, :], hid_ps[:, kv, :, :], ACT.Gelu).then_inc(gelu_done, 1)
            act.wait_ge(out_done, 1)
            act.activation(kc_hi[:, :, :], kc_ps[:, :, :], ACT.Copy).then_inc(c_hi_done, 1)
            act.wait_ge(out_done, 2)
            act.activation(vc[0:CMP_PAD, :, 0:HD], vc_ps[0:CMP_PAD, :, :], ACT.Copy).then_inc(c_hi_done, 1)
            act.activation(gates[:, :, :], h[:, :, COL_GATE:COL_GATE + N_GATE], ACT.Sigmoid)

        @block.vector
        def _(dve):
            dve.memset(eps[:, :], EPS).then_inc(eps_set, 1)
            dve.wait_ge(pos_in, 32)
            for kv in range(2):
                dve.wait_ge(moved, 8 * (kv + 1))
                for a in range(CMP_PAIRS):
                    seen = x2[:, kv, :, a:a + 8 * (N_CMP - 1) + 1:8]
                    dve.tensor_scalar(blocks[:, kv, a, :, 0:N_CMP], seen, pos_sb[:, kv, a:a + 1], None,
                                      ALU.add).then_inc(placed, 1)
            for n, (br, half) in enumerate(keys):
                cols = slice(half * HALF, (half + 1) * HALF)
                for g in range(GROUPS):
                    dve.wait_ge(hi_done, 4 * n + 2 * g + 2)
                    same = k_hi[g * HD:(g + 1) * HD, br, g, cols]
                    for place in range(2):
                        dve.tensor_tensor(k_lo[place * HD:(place + 1) * HD, br, g, cols], tp[g * HD:(g + 1) * HD, n % 4, :],
                                          same.bitcast(F32), ALU.subtract)
            for n, (br, g) in enumerate((br, g) for br in range(2) for g in range(GROUPS)):
                dve.wait_ge(v_hi_done, n + 1)
                rows = h[:, :, col_v[br] + g * HD:col_v[br] + (g + 1) * HD]
                dve.tensor_tensor(v[:, br, g, :, HD:2 * HD], rows, v[:, br, g, :, 0:HD].bitcast(F32), ALU.subtract)
            dve.wait_ge(rooted, 2)
            dve.reciprocal(rstd[:, :, :], root[:, :, :])
            dve.wait_ge(c_hi_done, 1)
            dve.tensor_tensor(kc_lo[:, :, :], kc_ps[:, :, :], kc_hi[:, :, :].bitcast(F32), ALU.subtract)
            dve.wait_ge(c_hi_done, 2)
            dve.tensor_tensor(vc[0:CMP_PAD, :, HD:2 * HD], vc_ps[0:CMP_PAD, :, :], vc[0:CMP_PAD, :, 0:HD].bitcast(F32),
                              ALU.subtract)


def masks(nc, stage, ident, ident_r, causal, window, compressed):
    with Scope(nc, stage) as s:
        width = 2 * P + TT * CMP_PAD
        m = s.sb("m", [P, width])
        zeroed, cut, copied = s.sem("zeroed"), s.sem("cut"), s.sem("copied")
        block = s.block()

        @block.gpsimd
        def _(pool):
            pool.memset(m[:, :], 0.0).then_inc(zeroed, 1)
            pool.wait_ge(zeroed, 1)
            pool.affine_select(out=m[:, 0:P], in_=m[:, 0:P], compare_op=ALU.is_ge, fill=MASKED, base=0,
                               pattern=[[-1, P]], channel_multiplier=1).then_inc(cut, 1)
            pool.affine_select(out=m[:, P:2 * P], in_=m[:, P:2 * P], compare_op=ALU.is_gt, fill=MASKED, base=0,
                               pattern=[[1, P]], channel_multiplier=-1).then_inc(cut, 1)
            last = m[:, 2 * P:width].rearrange("p (i n) -> p i n", n=CMP_PAD)
            pool.affine_select(out=last, in_=last, compare_op=ALU.is_ge, fill=MASKED, base=1 - CMP_BLOCK,
                               pattern=[[P, TT], [-CMP_STRIDE, CMP_PAD]], channel_multiplier=1).then_inc(cut, 1)

        @block.vector
        def _(dve):
            dve.tensor_copy(ident_r[:, :], ident[:, :])
            dve.wait_ge(cut, 3)
            dve.tensor_copy(causal[:, :], m[:, 0:P])
            dve.tensor_copy(window[:, :], m[:, P:2 * P])
            dve.tensor_copy(compressed[:, :, :], m[:, 2 * P:width].rearrange("p (i n) -> p i n", n=CMP_PAD))


class LatentWeights:

    def __init__(self, nc, s, w_uq, w_ukv, q_norm, kv_norm):
        self.nc = nc
        self.w_uq, self.w_ukv, self.q_norm, self.kv_norm = w_uq, w_ukv, q_norm, kv_norm
        self.uq = s.sb("uq", [P, Q_RANK // P, HEADS * MD])
        self.ukv = s.sb("ukv", [P, KV_RANK // P, HEADS * P])
        self.gain = s.sb("gain", [P, (Q_RANK + KV_RANK) // P])
        self.uq_in, self.ukv_in, self.gain_in = s.sem("uq_in"), s.sem("ukv_in"), s.sem("gain_in")

    def ahead(self, sp):
        sp.dma_start(self.ukv[:, :, :], self.w_ukv[0].rearrange("(c p) n -> p c n", p=P)).then_inc(self.ukv_in, 16)
        sp.dma_start(self.uq[:, :, :], self.w_uq[0].rearrange("(c p) n -> p c n", p=P)).then_inc(self.uq_in, 16)
        q_chunks = Q_RANK // P
        with self.nc.allow_non_contiguous_dma(reason="two norms' gains, one column each chunk"):
            for place, row in ((self.gain[:, 0:q_chunks], self.q_norm), (self.gain[:, q_chunks:], self.kv_norm)):
                sp.dma_start(place, row[0].rearrange("(c p) -> p c", p=P)).then_inc(self.gain_in, 16)


def latent_inputs(nc, stage, h, table, ident, weights, q_hi, q_lo, kv_hi, kv_lo, ukv_hi, ukv_lo, v):
    with Scope(nc, stage) as s:
        half_q = HEADS * MD // 2
        q_chunks, kv_chunks = Q_RANK // P, KV_RANK // P
        uq_hi = s.sb("uq_hi", [P, q_chunks, HEADS * MD], F32R)
        uq_lo = s.sb("uq_lo", [P, q_chunks, HEADS * MD], F32R)
        q_ps = s.ps("q_ps", [P, 3, HALF])
        v_ps = s.ps("v_ps", [P, 3, HALF])
        hi_ready, split = s.sem("hi_ready"), s.sem("split")
        v_done, v_hi_done, v_lo_done, q_done, q_taken = (s.sem(x) for x in ("v_done", "v_hi_done", "v_lo_done", "q_done", "q_taken"))

        def units_of(col, chunks, gain_at, hi, lo):
            for c in range(chunks):
                for half in range(2):
                    cols = slice(half * HALF, (half + 1) * HALF)
                    yield ([h[:, 4 * half + i, col + c * P:col + (c + 1) * P] for i in range(4)], hi[:, c, cols], lo[:, c, cols],
                           weights.gain[:, gain_at + c:gain_at + c + 1], None)

        kv_units = list(units_of(COL_CKV, kv_chunks, q_chunks, kv_hi, kv_lo))
        q_units = list(units_of(COL_CQ, q_chunks, 0, q_hi, q_lo))
        turn = Turn(s, 2, kv_units + q_units, ident)
        rope = RopeLatent(s, "rope_q", HEADS, COL_QM, MD)
        chunks = [(weights.ukv, ukv_hi, ukv_lo, c, weights.ukv_in) for c in range(kv_chunks)]
        chunks += [(weights.uq, uq_hi, uq_lo, c, weights.uq_in) for c in range(q_chunks)]
        block = s.block()

        order = [("w", n) for n in range(kv_chunks)] + [("u", m) for m in range(len(kv_units))]
        others = [("u", len(kv_units) + m) for m in range(len(q_units))] + [("w", kv_chunks + n) for n in range(q_chunks)]
        for i in range(TT):
            order += [others.pop(0), ("v", i)]
        order += others

        @block.scalar
        def _(act):
            for kind, n in order:
                if kind == "w":
                    raw, hi, lo, c, landed = chunks[n]
                    act.wait_ge(landed, 16)
                    act.activation(hi[:, c, :], raw[:, c, :], ACT.Copy).then_inc(hi_ready, 1)
                elif kind == "u":
                    if n == 0:
                        act.wait_ge(weights.gain_in, 32)
                    turn.act(act, n)
                else:
                    act.wait_ge(v_done, n + 1)
                    act.activation(v[:, :, n, 0:HD], v_ps[:, n % 3, :].rearrange("p (h d) -> p h d", d=HD), ACT.Copy).then_inc(v_hi_done, 1)
            for n in range(2 * TT):
                i, e = divmod(n, 2)
                act.wait_ge(q_done, n + 1)
                at = h[:, i, COL_QM + e * half_q:COL_QM + (e + 1) * half_q]
                act.activation(at, q_ps[:, n % 3, 0:half_q], ACT.Copy, scale=MLA_SCALE).then_inc(q_taken, 1)

        @block.vector
        def _(dve):
            for kind, n in order:
                if kind == "w":
                    raw, hi, lo, c, landed = chunks[n]
                    dve.wait_ge(hi_ready, n + 1)
                    dve.tensor_tensor(lo[:, c, :], raw[:, c, :], hi[:, c, :].bitcast(F32), ALU.subtract).then_inc(split, 1)
                elif kind == "u":
                    turn.dve(dve, n)
                else:
                    dve.wait_ge(v_hi_done, n + 1)
                    dve.tensor_tensor(v[:, :, n, HD:2 * HD], v_ps[:, n % 3, :].rearrange("p (h d) -> p h d", d=HD),
                                      v[:, :, n, 0:HD].bitcast(F32), ALU.subtract).then_inc(v_lo_done, 1)
            for i in range(TT):
                dve.wait_ge(q_taken, 2 * (i + 1))
                rope.tile(dve, h, table, i)

        @block.tensor
        def _(pe):
            for m in range(len(kv_units)):
                turn.pe(pe, m)
            pe.wait_ge(split, kv_chunks)
            for i in range(TT):
                if i < len(q_units):
                    turn.pe(pe, len(kv_units) + i)
                if i == 0:
                    pe.wait_ge(turn.lo_done, len(kv_units))
                if i >= 3:
                    pe.wait_ge(v_lo_done, i - 2)
                rows = slice(i * P, (i + 1) * P)
                for c in range(kv_chunks):
                    for m, (a, w) in enumerate(((kv_hi, ukv_hi), (kv_hi, ukv_lo), (kv_lo, ukv_hi))):
                        values = w[:, c, :].rearrange("p (h d) -> p h d", d=P)[:, :, HD:2 * HD]
                        last = pe.matmul(v_ps[:, i % 3, :], a[:, c, rows], values, start=(c == 0 and m == 0),
                                         stop=(c == kv_chunks - 1 and m == 2))
                last.then_inc(v_done, 1)
            pe.wait_ge(turn.lo_done, len(turn.units))
            pe.wait_ge(split, len(chunks))
            for n in range(2 * TT):
                i, e = divmod(n, 2)
                if n >= 3:
                    pe.wait_ge(q_taken, n - 2)
                for c in range(q_chunks):
                    for m, (a, w) in enumerate(((q_hi, uq_hi), (q_hi, uq_lo), (q_lo, uq_hi))):
                        last = pe.matmul(q_ps[:, n % 3, 0:half_q], a[:, c, i * P:(i + 1) * P],
                                         w[:, c, e * half_q:(e + 1) * half_q], start=(c == 0 and m == 0),
                                         stop=(c == q_chunks - 1 and m == 2))
                last.then_inc(q_done, 1)


RING = 3
LAG = 2
SUMS = 8


class Unit:

    def __init__(self, blocks, keys, first_row, key_of, widths, mask_of, value_of, out, adds, gate, before):
        self.blocks = blocks
        self.keys = keys
        self.first_row = first_row
        self.key_of = key_of
        self.widths = widths
        self.mask_of = mask_of
        self.value_of = value_of
        self.out = out
        self.adds = adds
        self.gate = gate
        self.before = before
        self.one_block = max(widths) < P
        self.together = 4 if max(widths) <= T // 4 else 2 if max(widths) <= T // 2 else 1

    def columns(self, row, width=None):
        at = row % self.together * (self.keys if self.one_block else T // self.together)
        return slice(at, at + (self.widths[row] if width is None else width))


def attend(nc, stage, units, staging, ident, ident_r, slots, lead, burst, early, ahead=None, beside=None):
    steps = []
    scoring = []
    staged = 0
    for n, u in enumerate(units):
        at = len(scoring)
        while len(scoring) - at < early and at and scoring[at - 1] != ("score", staged, 0):
            at -= 1
        if u.before:
            scoring[at:at] = [("stage", n, y) for y in u.before]
            staged = n
        scoring += [("score", n, r) for r in range(0, 4, u.together)]
    turned = []
    scored_columns = turned_columns = 0

    def score_next():
        kind, n, r = step = scoring.pop(0)
        steps.append(step)
        return sum(units[n].widths[r:r + units[n].together]) if kind == "score" else 0

    def apply_next():
        n, k = turned.pop(0)
        if k == 0 and n:
            steps.append(("finish", n - 1, 0))
        steps.append(("apply", n, k))

    for n, u in enumerate(units):
        for k, block in enumerate(u.blocks):
            free = burst
            while scoring and (("score", n, 4 - u.together) in scoring or free > 0 and scoring[0][1] < n + slots
                               and scored_columns < turned_columns + lead):
                free -= scoring[0][0] == "score"
                scored_columns += score_next()
            steps.append(("turn", n, k))
            turned_columns += (4 - u.first_row(block)) * u.keys
            turned.append((n, k))
            if len(turned) > LAG:
                apply_next()
    while turned:
        apply_next()
    steps.append(("finish", len(units) - 1, 0))

    act_steps, held = [], []
    for step in steps:
        if step[0] == "score":
            if len(held) == 2:
                act_steps.append(held.pop(0))
            held.append(step)
            continue
        if step[0] == "turn":
            while held and held[0][1] <= step[1]:
                act_steps.append(held.pop(0))
        act_steps.append(step)
        if step[0] == "turn":
            act_steps += held
            held = []
    assert not held

    ring_no = {x: m for m, x in enumerate(x for x in steps if x[0] in ("turn", "stage", "finish"))}
    hi_no = {x: m for m, x in enumerate(x for x in steps if x[0] in ("turn", "stage"))}
    turn_no = {x: m for m, x in enumerate(x for x in steps if x[0] == "turn")}
    score_no = {x: m for m, x in enumerate(x for x in steps if x[0] == "score")}
    last_score = {x[1]: m for x, m in score_no.items()}

    with Scope(nc, stage) as s:
        exps = s.sb("exps", [P, slots, 4, T])
        sums = s.sb("sums", [P, SUMS, 4])
        neg_max = s.sb("neg_max", [P, SUMS, 4])
        turned_hi = s.sb("turned_hi", [P, RING, HALF], F32R)
        turned_lo = s.sb("turned_lo", [P, RING, HALF], F32R)
        out_sb = s.sb("out_sb", [P, 4, P])
        floor = s.sb("floor", [P, 2, 4])
        factor = s.sb("factor", [P, 2, 4])
        factor_g = s.sb("factor_g", [P, 2, 4])
        joined = s.sb("joined", [P, 2, 4, HD])
        scores = s.ps("scores", [P, 2, T])
        ring = s.ps("ring", [P, RING, HALF])
        out_ps = s.ps("out_ps", [P, HALF])
        scored, maxed, exped, guarded = s.sem("scored"), s.sem("maxed"), s.sem("exped"), s.sem("guarded")
        ring_full, hi_done, ring_free = s.sem("ring_full"), s.sem("hi_done"), s.sem("ring_free")
        applied, out_moved = s.sem("applied"), s.sem("out_moved")
        tail, fin, factored, weighed = s.sem("tail"), s.sem("fin"), s.sem("factored"), s.sem("weighed")
        block = s.block()
        bank_of = lambda step: ring[:, ring_no[step] % RING, :] if step in ring_no else None

        @block.sync
        def _(sp):
            if ahead is not None:
                ahead(sp)

        @block.tensor
        def _(pe):
            for step in steps:
                kind, n, k = step
                u = units[n]
                bank = bank_of(step)
                if step in ring_no and ring_no[step] >= RING:
                    pe.wait_ge(ring_free, ring_no[step] - RING + 1)
                if kind == "stage":
                    staging.pe(pe, k, bank).then_inc(ring_full, 1)
                elif kind == "score":
                    m = score_no[step]
                    pe.wait_ge(ring_free, ring_no[[x for x in steps if x[0] == "stage" and x[1] <= n][-1]] + 1)
                    if m >= 2:
                        pe.wait_ge(exped, m - 1)
                    if u.one_block:
                        mask = u.mask_of(k)[0][1].unsqueeze(1).to_broadcast([P, 4, u.keys])
                        pe.matmul(scores[:, m % 2, 0:4 * u.keys].rearrange("p (r c) -> p r c", r=4), ident_r[:, :], mask,
                                  start=True, stop=False)
                    for r in range(k, k + u.together):
                        w = u.widths[r]
                        own = scores[:, m % 2, u.columns(r)]
                        for c0 in range(0, w, HALF):
                            c1 = min(c0 + HALF, w)
                            products = u.key_of(r, c0, c1 - c0)
                            for p, (q, key) in enumerate(products):
                                last = pe.matmul(own[:, c0:c1], q, key, start=(p == 0 and not u.one_block),
                                                 stop=(p == len(products) - 1 and (not u.one_block or r == 3)))
                                if p == 0 and not u.one_block:
                                    for at, mask in u.mask_of(r):
                                        if c0 <= at < c1:
                                            pe.matmul(own[:, at:at + u.keys], ident_r[:, :], mask, start=False, stop=False)
                    last.then_inc(scored, 1)
                elif kind == "turn":
                    j = turn_no[step]
                    first = u.first_row(u.blocks[k])
                    pe.wait_ge(exped, last_score[n] + 1)
                    for r in range(first, 4):
                        last = pe.transpose(bank[0:u.keys, r * P:(r + 1) * P],
                                            exps[:, n % slots, r, k * u.keys:(k + 1) * u.keys], ident[:, :])
                    last.then_inc(ring_full, 1)
                elif kind == "apply":
                    j = turn_no[("turn", n, k)]
                    cols = slice(u.first_row(u.blocks[k]) * P, HALF)
                    pe.wait_ge(ring_free, ring_no[("turn", n, k)] + 1)
                    if k == 0 and n:
                        pe.wait_ge(out_moved, n)
                    for m, part in enumerate((turned_hi, turned_lo)):
                        last = pe.matmul(out_ps[:, cols], u.value_of(u.blocks[k]), part[0:u.keys, j % RING, cols],
                                         start=(k == 0 and m == 0), stop=(k == len(u.blocks) - 1 and m == 1))
                    last.then_inc(applied, 1)
                else:
                    pe.wait_ge(out_moved, n + 1)
                    for r in range(4):
                        last = pe.transpose(bank[:, r * P:(r + 1) * P], out_sb[:, r, :], ident[:, :])
                    last.then_inc(ring_full, 1)

        @block.scalar
        def _(act):
            for step in act_steps:
                kind, n, k = step
                u = units[n]
                bank = bank_of(step)
                if kind == "stage":
                    act.wait_ge(ring_full, ring_no[step] + 1)
                    staging.act(act, k, bank).then_inc(hi_done, 1)
                elif kind == "score":
                    m = score_no[step]
                    act.wait_ge(maxed, m + 1)
                    for r in range(k, k + u.together):
                        made = act.activation(exps[:, n % slots, r, 0:u.widths[r]], scores[:, m % 2, u.columns(r)], ACT.Exp,
                                              bias=neg_max[:, n % SUMS, r:r + 1], accum_out=sums[:, n % SUMS, r:r + 1])
                    made.then_inc(exped, 1)
                elif kind == "turn":
                    j = turn_no[step]
                    cols = slice(u.first_row(u.blocks[k]) * P, HALF)
                    act.wait_ge(ring_full, ring_no[step] + 1)
                    if j >= RING:
                        act.wait_ge(applied, j - RING + 1)
                    act.activation(turned_hi[0:u.keys, j % RING, cols], bank[0:u.keys, cols], ACT.Copy).then_inc(hi_done, 1)
                elif kind == "apply" and k == len(u.blocks) - 1:
                    act.wait_ge(applied, turn_no[("turn", n, k)] + 1)
                    act.activation(out_sb[:, :, :].rearrange("p r c -> p (r c)"), out_ps[:, :], ACT.Copy).then_inc(out_moved, 1)

        @block.vector
        def _(dve):
            guards = 0
            for step in steps:
                kind, n, k = step
                u = units[n]
                bank = bank_of(step)
                if kind == "stage":
                    dve.wait_ge(hi_done, hi_no[step] + 1)
                    staging.dve(dve, k, bank).then_inc(ring_free, 1)
                elif kind == "score":
                    m = score_no[step]
                    dve.wait_ge(scored, m + 1)
                    at = neg_max[:, n % SUMS, k:k + u.together]
                    if min(u.widths) == max(u.widths):
                        rows = scores[:, m % 2, 0:u.together * (u.columns(1).start or T)]
                        rows = rows.rearrange("p (r c) -> p r c", r=u.together)[:, :, 0:u.widths[0]]
                        top = dve.reduce_max(at, rows, AX, negate=True)
                    else:
                        for r in range(k, k + u.together):
                            top = dve.reduce_max(neg_max[:, n % SUMS, r:r + 1], scores[:, m % 2, u.columns(r)], AX, negate=True)
                    if u.keys == CMP_PAD:
                        top.then_inc(guarded, 1)
                        guards += 1
                        dve.wait_ge(guarded, guards)
                        top = dve.tensor_scalar(at, at, -NO_KEY, None, ALU.min)
                    top.then_inc(maxed, 1)
                elif kind == "turn":
                    j = turn_no[step]
                    cols = slice(u.first_row(u.blocks[k]) * P, HALF)
                    dve.wait_ge(hi_done, hi_no[step] + 1)
                    dve.tensor_tensor(turned_lo[0:u.keys, j % RING, cols], bank[0:u.keys, cols],
                                      turned_hi[0:u.keys, j % RING, cols].bitcast(F32), ALU.subtract).then_inc(ring_free, 1)
                elif kind == "finish":
                    b = n % 2
                    dve.tensor_scalar(floor[:, b, :], sums[:, n % SUMS, :], 1e-30, None, ALU.max).then_inc(tail, 1)
                    dve.wait_ge(tail, n + 1)
                    if n >= 2:
                        dve.wait_ge(fin, n - 1)
                    dve.reciprocal(factor[:, b, :], floor[:, b, :]).then_inc(factored, 1)
                    dve.wait_ge(ring_full, ring_no[step] + 1)
                    parts = bank[:, :].rearrange("p (r a d) -> p r d a", a=2, d=HD)
                    dve.tensor_reduce(joined[:, b, :, :], parts, AX, ALU.add).then_inc(ring_free, 1)

        @block.gpsimd
        def _(pool):
            gated = added = 0
            for step in steps:
                kind, n, k = step
                if kind != "finish":
                    continue
                u, b = units[n], n % 2
                pool.wait_ge(factored, n + 1)
                by = factor
                if u.gate is not None:
                    pool.tensor_tensor(factor_g[:, b, :], factor[:, b, :], u.gate, ALU.mult).then_inc(weighed, 1)
                    gated += 1
                    by = factor_g
                pool.wait_ge(ring_free, ring_no[step] + 1)
                if gated + added:
                    pool.wait_ge(weighed, gated + added)
                wide = by[:, b, :].unsqueeze(2).to_broadcast([P, 4, HD])
                if u.adds:
                    pool.tensor_tensor(joined[:, b, :, :], joined[:, b, :, :], wide, ALU.mult).then_inc(weighed, 1)
                    added += 1
                    pool.wait_ge(weighed, gated + added)
                    pool.tensor_tensor(u.out, u.out, joined[:, b, :, :], ALU.add).then_inc(fin, 1)
                else:
                    pool.tensor_tensor(u.out, joined[:, b, :, :], wide, ALU.mult).then_inc(fin, 1)
                if beside is not None:
                    beside(pool, n)


def sparse_attention(nc, stage, h, k_hi, k_lo, v, kc_hi, kc_lo, vc, gates, ident, ident_r, causal, window, compressed,
                     rstd, ahead):
    with Scope(nc, stage) as s:
        q = s.sb("q", [P, 2, HPG, P], F32R)

        class Staging:

            def places(self, t, side):
                for odd in range(2):
                    own, other = slice(odd * HD, (odd + 1) * HD), slice((1 - odd) * HD, (2 - odd) * HD)
                    rows = side[own, 0:2 * P].rearrange("p (a n) -> p a n", a=2)
                    yield rows, q[own, t % 2, odd::2, :], q[other, t % 2, odd::2, :]

            def pe(self, pe, t, side):
                g, i = divmod(t, TT)
                for pair in range(2):
                    col = COL_Q + (g * HPG + 2 * pair) * HD
                    last = pe.transpose(side[:, pair * P:(pair + 1) * P], h[:, i, col:col + P], ident[:, :])
                return last

            def act(self, act, t, side):
                for rows, hi, lo in self.places(t, side):
                    last = act.activation(hi, rows, ACT.Copy, scale=NSA_SCALE)
                return last

            def dve(self, dve, t, side):
                for rows, hi, lo in self.places(t, side):
                    last = dve.scalar_tensor_tensor(out=lo, in0=rows, scalar=NSA_SCALE, in1=hi.bitcast(F32),
                                                    op0=ALU.mult, op1=ALU.subtract)
                return last

        def unit(g, i, branch):
            col = COL_Q + g * HPG * HD
            out = h[:, i, col:col + HPG * HD].rearrange("p (r d) -> p r d", d=HD)
            gate = gates[:, i, g * HPG * 3 + (1, 2, 0)[branch]:(g + 1) * HPG * 3:3]
            at = (g * TT + i) % 2
            if branch == 2:
                blocks, keys, base = [0], CMP_PAD, 0
                kh, kl = kc_hi[:, g, :], kc_lo[:, g, :]
                mask = [(0, compressed[:, i, :])]
                value = lambda j: vc[0:CMP_PAD, g, :]
            else:
                blocks = list(range(max(0, i - WINDOW_BLOCKS) if branch == 1 else 0, i + 1))
                keys, base = P, blocks[0] * P
                kh, kl = k_hi[:, branch, g, :], k_lo[:, branch, g, :]
                mask = [((len(blocks) - 1) * P, causal[:, :])]
                if branch == 1 and i >= WINDOW_BLOCKS:
                    mask.append((0, window[:, :]))
                value = lambda j: v[:, branch, g, j, :]

            def key_of(r, c0, w):
                return [(q[:, at, r, :], k[:, base + c0:base + c0 + w]) for k in (kh, kl)]

            return Unit(blocks, keys, lambda j: 0, key_of, [len(blocks) * keys] * 4, lambda r: mask, value, out,
                        branch > 0, gate, [g * TT + i] if branch == 0 else [])

        def scale_latents(pool, n):
            if n < 2 * TT:
                which, i = divmod(n, TT)
                col, rank = LATENTS[which]
                at = h[:, i, col:col + rank]
                pool.tensor_scalar(at, at, rstd[:, which, i:i + 1], None, ALU.mult)

        tiles = list(range(2, TT)) + [0, 1]
        units = [unit(g, i, b) for g in range(GROUPS) for i in tiles for b in range(3)]
        attend(nc, stage + "a", units, Staging(), ident, ident_r, 3, lead=4 * T, burst=1, early=1, ahead=ahead,
               beside=scale_latents)


def latent_attention(nc, stage, h, kv_hi, kv_lo, ukv_hi, ukv_lo, v, ident, ident_r, causal):
    with Scope(nc, stage) as s:
        k_hi = s.sb("k_hi", [P, 2, T], F32R)
        k_lo = s.sb("k_lo", [P, 2, T], F32R)
        q_hi = s.sb("q_hi", [P, 2, HALF], F32R)
        q_lo = s.sb("q_lo", [P, 2, HALF], F32R)

        class Staging:

            def pe(self, pe, what, side):
                if what[0] == "k":
                    _, head, half = what
                    for c in range(2):
                        for m, (w, a) in enumerate(((ukv_hi, kv_hi), (ukv_hi, kv_lo), (ukv_lo, kv_hi))):
                            last = pe.matmul(side[:, :], w[:, c, head * P:(head + 1) * P], a[:, c, half * HALF:(half + 1) * HALF],
                                             start=(c == 0 and m == 0), stop=(c == 1 and m == 2))
                    return last
                for r in range(4):
                    if what[0] == "q":
                        _, head, half = what
                        rows = h[:, 4 * half + r, COL_QM + head * MD:COL_QM + (head + 1) * MD]
                    else:
                        rows = h[:, 4 * what[1] + r, COL_KR - HD:COL_KR + ROPE_M]
                    last = pe.transpose(side[0:MD, r * P:(r + 1) * P], rows, ident[:, :])
                return last

            def places(self, what, side):
                if what[0] == "q":
                    _, head, half = what
                    return [(side[0:MD, :], q_hi[0:MD, half, :], q_lo[0:MD, half, :])]
                cols = slice(what[-1] * HALF, (what[-1] + 1) * HALF)
                if what[0] == "k":
                    b = what[1] % 2
                    return [(side[0:HD, :], k_hi[0:HD, b, cols], k_lo[0:HD, b, cols])]
                return [(side[HD:MD, :], k_hi[HD:MD, b, cols], k_lo[HD:MD, b, cols]) for b in range(2)]

            def act(self, act, what, side):
                for rows, hi, lo in self.places(what, side):
                    last = act.activation(hi, rows, ACT.Copy)
                return last

            def dve(self, dve, what, side):
                for rows, hi, lo in self.places(what, side):
                    last = dve.tensor_tensor(lo, rows, hi.bitcast(F32), ALU.subtract)
                return last

        def unit(head, half):
            blocks = list(range(4 * half + 4))
            b = head % 2
            col = COL_QM + head * HD
            out = h[:, 4 * half:4 * half + 4, col:col + HD]

            def key_of(r, c0, w):
                rows = slice(r * P, (r + 1) * P)
                hi, lo = q_hi[0:MD, half, rows], q_lo[0:MD, half, rows]
                return [(hi, k_hi[0:MD, b, c0:c0 + w]), (hi, k_lo[0:MD, b, c0:c0 + w]), (lo, k_hi[0:MD, b, c0:c0 + w])]

            before = [("k", head, half), ("q", head, half)]
            if head == 0:
                before = [("r", half)] + before
            widths = [(4 * half + r + 1) * P for r in range(4)]
            return Unit(blocks, P, lambda j: max(0, j - 4 * half), key_of, widths,
                        lambda r: [((4 * half + r) * P, causal[:, :])], lambda j: v[:, head, j, :], out, False, None, before)

        units = [unit(head, half) for head in range(HEADS) for half in range(2)]
        attend(nc, stage + "a", units, Staging(), ident, ident_r, 2, lead=4 * T, burst=9, early=1)


def clear_semaphores(nc):
    nc.clear_and_free_semaphores(Scope.finished)
    nc.all_engine_barrier()
    Scope.finished = []


def layer(nc, x, c, w_ada, b_ada, ln_g, ln_b, ffn1_wg, ffn1_wu, ffn1_wd, w_in, cmp_k_pos, cmp_k_w1, cmp_k_w2,
          cmp_v_pos, cmp_v_w1, cmp_v_w2, mla_q_norm, mla_kv_norm, mla_w_uq, mla_w_ukv, w_out, ffn2_wg, ffn2_wu,
          ffn2_wd, rope_table, out):
    Scope.finished = []
    gate_dram = nc.dram_tensor("gate_rows", [2, D], F32, kind="Internal").ap()
    x_dram = nc.dram_tensor("x_rows", [T, D], F32, kind="Internal").ap()
    norm_rows = lambda n: (ln_g[0, n:n + 1, :], ln_b[0, n:n + 1, :])
    with Scope(nc, "all") as a:
        ident = a.sb("ident", [P, P])
        ones = a.sb("ones", [P, P])
        ident_r = a.sb("ident_r", [P, P], F32R)
        causal = a.sb("causal", [P, P], F32R)
        window = a.sb("window", [P, P], F32R)
        compressed = a.sb("compressed", [P, TT, CMP_PAD], F32R)
        table = a.sb("table", [P, TT, ROPE_N + ROPE_M])
        gates = a.sb("gates", [P, TT, N_GATE])
        shift = a.sb("shift", [P, 3, DC])
        scale = a.sb("scale", [P, 3, DC])
        silu_c = a.sb("silu_c", [P, DC])
        norm_cols = a.sb("norm_cols", [P, 2, 3, DC])
        x_in, x_out = [a.sem(f"x_in{half}") for half in range(2)], a.sem("x_out")
        constants(nc, ident, ones)
        masks(nc, "masks", ident, ident_r, causal, window, compressed)

        with ExitStack() as h_alive:
            with Scope(nc, "mix_in", side="right") as r:
                x_sb = r.sb("x", [P, TT, D])
                with Scope(nc, "late") as t:
                    part_late = t.sb("part_late", [P, LATE, D])
                    modulation(nc, c, w_ada, b_ada, ln_g, ln_b, x, ident, ones, x_sb, silu_c, part_late, norm_cols, shift,
                               scale, rope_table, table, x_in)
                    u_hi = r.sb("u_hi", [P, DC, T], F32R)
                    u_lo = r.sb("u_lo", [P, DC, T], F32R)
                    with Scope(nc, "ffn1") as w:
                        weights = HiddenWeights(w, ffn1_wg, ffn1_wu, ffn1_wd)
                        modulated_transpose(nc, "turn1", x_sb, shift[:, 0, :], scale[:, 0, :], ident, u_hi, u_lo,
                                            weights.ahead, arrives=x_in)
                        swiglu(nc, "glu1", weights, None, x_sb, u_hi, u_lo, late=(w_ada, silu_c, ones, part_late))
                    chunks = Chunks(r, w_in[0], D_IN // 4)
                    norm_turn(nc, "norm1", x_sb, 0, norm_cols, shift[:, 1, :], scale[:, 1, :], ident, u_hi, u_lo,
                              chunks.ahead, late=(ones, part_late, gate_dram, shift, scale))
                h = h_alive.enter_context(Scope(nc, "h")).sb("h", [P, TT, D_IN])
                project(nc, "in", chunks, 4, u_hi, u_lo, h, beside=(x_sb, norm_rows(0), x_dram, x_out, table))

            clear_semaphores(nc)
            latent_in = Scope(nc, "latent_w", side="right")
            latent_in.__enter__()
            latent_weights = LatentWeights(nc, latent_in, mla_w_uq, mla_w_ukv, mla_q_norm, mla_kv_norm)
            with Scope(nc, "sparse") as b:
                k_hi = b.sb("k_hi", [P, 2, GROUPS, T], F32R)
                k_lo = b.sb("k_lo", [P, 2, GROUPS, T], F32R)
                v = b.sb("v", [P, 2, GROUPS, TT, P], F32R)
                kc_hi = b.sb("kc_hi", [P, GROUPS, CMP_PAD], F32R)
                kc_lo = b.sb("kc_lo", [P, GROUPS, CMP_PAD], F32R)
                vc = b.sb("vc", [P, GROUPS, P], F32R)
                rstd = b.sb("rstd", [P, 2, TT])
                sparse_inputs(nc, "sparse_in", h, table, gates, ident, (cmp_k_pos, cmp_v_pos), (cmp_k_w1, cmp_v_w1),
                              (cmp_k_w2, cmp_v_w2), k_hi, k_lo, v, kc_hi, kc_lo, vc, rstd)
                sparse_attention(nc, "nsa", h, k_hi, k_lo, v, kc_hi, kc_lo, vc, gates, ident, ident_r, causal, window,
                                 compressed, rstd, latent_weights.ahead)
            with Scope(nc, "latent") as b:
                kv_hi = b.sb("kv_hi", [P, 2, T], F32R)
                kv_lo = b.sb("kv_lo", [P, 2, T], F32R)
                ukv_hi = b.sb("ukv_hi", [P, 2, HEADS * P], F32R)
                ukv_lo = b.sb("ukv_lo", [P, 2, HEADS * P], F32R)
                v = b.sb("v", [P, HEADS, TT, P], F32R)
                with Scope(nc, "queries") as t:
                    q_hi = t.sb("q_hi", [P, 3, T], F32R)
                    q_lo = t.sb("q_lo", [P, 3, T], F32R)
                    latent_inputs(nc, "latent_in", h, table, ident, latent_weights, q_hi, q_lo, kv_hi, kv_lo, ukv_hi,
                                  ukv_lo, v)
                latent_in.__exit__(None, None, None)
                latent_attention(nc, "mla", h, kv_hi, kv_lo, ukv_hi, ukv_lo, v, ident, ident_r, causal)

            clear_semaphores(nc)
            r = Scope(nc, "mix_out", side="right")
            r.__enter__()
            x_sb = r.sb("x", [P, TT, D])
            u_hi = r.sb("u_hi", [P, DC, T], F32R)
            u_lo = r.sb("u_lo", [P, DC, T], F32R)
            x_back = r.sem("x_back")
            chunks_in = Scope(nc, "w_out", side="right")
            chunks_in.__enter__()
            chunks = Chunks(chunks_in, w_out[0], HALF, gate_dram[0:1, :])
            modulated_transpose(nc, "turn3", h, None, None, ident, u_hi, u_lo, chunks.ahead, (x_sb, x_dram, x_back))
        project(nc, "out", chunks, 2, u_hi, u_lo, x_sb, (x_back, 16 * TT))
        chunks_in.__exit__(None, None, None)
        with Scope(nc, "ffn2") as w:
            weights = HiddenWeights(w, ffn2_wg, ffn2_wu, ffn2_wd)
            norm_turn(nc, "norm2", x_sb, 1, norm_cols, shift[:, 2, :], scale[:, 2, :], ident, u_hi, u_lo, weights.ahead)
            swiglu(nc, "glu2", weights, gate_dram[1:2, :], x_sb, u_hi, u_lo, norm_rows(1))
        norm_out(nc, "norm3", x_sb, *norm_rows(2), out)
        r.__exit__(None, None, None)


INPUTS = ("x", "c", "w_ada", "b_ada", "ln_g", "ln_b", "ffn1_wg", "ffn1_wu", "ffn1_wd", "w_in", "cmp_k_pos", "cmp_k_w1",
          "cmp_k_w2", "cmp_v_pos", "cmp_v_w1", "cmp_v_w2", "mla_q_norm", "mla_kv_norm", "mla_w_uq", "mla_w_ukv",
          "w_out", "ffn2_wg", "ffn2_wu", "ffn2_wd")


def rope_rows_table():
    import numpy as np

    parts = []
    for width in (ROPE_N, ROPE_M):
        half = width // 2
        inverse = np.float32(ROPE_THETA) ** (-np.arange(half, dtype=np.float32) / np.float32(half))
        angle = np.arange(T, dtype=np.float32)[:, None] * inverse[None, :]
        parts += [np.cos(angle), np.sin(angle)]
    return np.concatenate(parts, axis=1).astype(np.float32)


def kernel(**inputs):
    import numpy as np
    import concourse.bacc as bacc
    from concourse.bass_utils import run_bass_kernel_spmd

    nc = bacc.Bacc("TRN2", target_bir_lowering=False, num_devices=1)
    arrays = {f"in_{name}": np.ascontiguousarray(inputs[name]) for name in INPUTS}
    arrays["in_rope_table"] = rope_rows_table()
    args = [nc.dram_tensor(name, a.shape, mybir.dt.from_np(a.dtype), kind="ExternalInput").ap() for name, a in arrays.items()]
    out = nc.dram_tensor("out_x", (1, T, D), F32, kind="ExternalOutput").ap()
    layer(nc, *args, out)
    result = run_bass_kernel_spmd(nc, [arrays], core_ids=[0])
    return result.results[0]["out_x"]
```
